# Optimizing a Trainium2 kernel written in Bass

```python
import math
import jax, jax.numpy as jnp
from jax import lax
import numpy as np

D_MODEL = 1024
BATCH = 1
SEQ = 512
DEPTH = 2

N_A = DEPTH // 2
N_B = DEPTH - N_A
POOL_WINDOWS = (2, 4, 8, 16)
N_POOL_GROUPS = len(POOL_WINDOWS)
GROUP_CH = D_MODEL // N_POOL_GROUPS
HEAD_DIM = 64
N_Q_HEADS = D_MODEL // HEAD_DIM
N_KV_HEADS = 4
Q_PER_KV = N_Q_HEADS // N_KV_HEADS
WINDOW = 128
BLOCK = 128
ROPE_THETA = 10000.0
ATTN_SCALE = 1.0 / math.sqrt(HEAD_DIM)
NEG_INF = -1e30
D_FF = 2816
CONV_WIDTH = 3
RMS_EPS = 1e-6


def rms_norm(x, g):
    xf = x.astype(jnp.float32)
    y = xf * lax.rsqrt(jnp.mean(xf * xf, axis=-1, keepdims=True) + RMS_EPS)
    return (y * g.astype(jnp.float32)).astype(x.dtype)

def pool_mixer(h, w_pool, scale):
    B, S, D = h.shape
    hf = h.astype(jnp.float32)
    csum = jnp.concatenate([jnp.zeros((B, 1, D), jnp.float32), jnp.cumsum(hf, axis=1)], axis=1)
    t = jnp.arange(1, S + 1)
    diffs = []
    for gi, w in enumerate(POOL_WINDOWS):
        sl = slice(gi * GROUP_CH, (gi + 1) * GROUP_CH)
        lo = jnp.maximum(t - w, 0)
        cnt = jnp.minimum(t, w).astype(jnp.float32)
        mean = (csum[:, 1:, sl] - csum[:, lo, sl]) / cnt[None, :, None]
        diffs.append(mean - hf[..., sl])
    d = jnp.stack(diffs, axis=2).astype(h.dtype)
    y = jnp.einsum('bsgc,gcd->bsgd', d, w_pool).reshape(B, S, D)
    return y * scale

def conv_glu_ffn(h, w_in, conv_w, conv_b, w_out):
    S = h.shape[1]
    u = h @ w_in
    up = jnp.pad(u, ((0, 0), (CONV_WIDTH - 1, 0), (0, 0)))
    u = sum(conv_w[k] * up[:, k:k + S] for k in range(CONV_WIDTH)) + conv_b
    gate, val = jnp.split(u, 2, axis=-1)
    return (jax.nn.gelu(gate, approximate=True) * val) @ w_out

def rope(x, cos, sin):
    xf = x.astype(jnp.float32)
    x1, x2 = jnp.split(xf, 2, axis=-1)
    return jnp.concatenate([x1 * cos - x2 * sin, x2 * cos + x1 * sin], axis=-1).astype(x.dtype)

def rope_tables(positions):
    inv_freq = 1.0 / (ROPE_THETA ** (jnp.arange(0, HEAD_DIM, 2, dtype=jnp.float32) / HEAD_DIM))
    ang = positions.astype(jnp.float32)[..., None] * inv_freq
    return jnp.cos(ang)[:, :, None, :], jnp.sin(ang)[:, :, None, :]

def band_blocks(t):
    B, S = t.shape[:2]
    nb = S // BLOCK
    tb = t.reshape(B, nb, BLOCK, N_KV_HEADS, HEAD_DIM)
    prev = jnp.pad(tb, ((0, 0), (1, 0), (0, 0), (0, 0), (0, 0)))[:, :-1]
    return jnp.concatenate([prev, tb], axis=2).astype(jnp.float32)

def swa_sink_attention(q, kk, vv, sinks):
    B, S = q.shape[:2]
    nb = S // BLOCK
    qb = q.reshape(B, nb, BLOCK, N_KV_HEADS, Q_PER_KV, HEAD_DIM).astype(jnp.float32) * ATTN_SCALE
    s = jnp.einsum('bnqhgd,bnkhd->bnhgqk', qb, kk)
    qi = jnp.arange(BLOCK)[:, None]
    kj = jnp.arange(2 * BLOCK)[None, :]
    rel = BLOCK + qi - kj
    blk = jnp.arange(nb)[:, None, None]
    valid = (rel >= 0) & (rel < WINDOW) & (blk * BLOCK + kj - BLOCK >= 0)
    s = jnp.where(valid[None, :, None, None], s, NEG_INF)
    sink = sinks.astype(jnp.float32).reshape(N_KV_HEADS, Q_PER_KV)[None, None, :, :, None, None]
    m = jnp.maximum(jnp.max(s, axis=-1, keepdims=True), sink)
    p = jnp.exp(s - m)
    denom = jnp.sum(p, axis=-1) + jnp.exp(sink - m)[..., 0]
    o = jnp.einsum('bnhgqk,bnkhd->bnhgqd', p, vv) / denom[..., None]
    o = o.transpose(0, 1, 4, 2, 3, 5).reshape(B, S, N_Q_HEADS * HEAD_DIM)
    return o.astype(q.dtype)

def first_inputs(seed: int = 0) -> dict:
    key = jax.random.key(seed)
    ks = jax.random.split(key, 20)
    f32 = jnp.float32
    D, F = D_MODEL, D_FF
    HQD, HKVD = N_Q_HEADS * HEAD_DIM, N_KV_HEADS * HEAD_DIM

    def gain(k, shape):
        return 1.0 + 0.05 * jax.random.normal(k, shape, f32)

    x = jax.random.normal(ks[0], (BATCH, SEQ, D), f32)
    positions = jnp.broadcast_to(jnp.arange(SEQ, dtype=jnp.int32)[None, :], (BATCH, SEQ))
    return {
        "x": x,
        "positions": positions,
        "mix_pre_g": gain(ks[1], (DEPTH, D)),
        "mix_post_g": gain(ks[2], (DEPTH, D)),
        "pool_w": jax.random.normal(ks[3], (N_A, N_POOL_GROUPS, GROUP_CH, GROUP_CH), f32) * GROUP_CH ** -0.5,
        "pool_scale": 1.0 + 0.1 * jax.random.normal(ks[4], (N_A, D), f32),
        "kv_norm_g": gain(ks[5], (D,)),
        "w_kv": jax.random.normal(ks[6], (D, 2 * HKVD), f32) * D ** -0.5,
        "w_q": jax.random.normal(ks[7], (N_B, D, HQD), f32) * D ** -0.5,
        "w_o": jax.random.normal(ks[8], (N_B, HQD, D), f32) * HQD ** -0.5,
        "sinks": jax.random.normal(ks[9], (N_B, N_Q_HEADS), f32),
        "ffn_pre_g": gain(ks[10], (DEPTH, D)),
        "ffn_post_g": gain(ks[11], (DEPTH, D)),
        "ffn_w_in": jax.random.normal(ks[12], (DEPTH, D, 2 * F), f32) * D ** -0.5,
        "ffn_conv_w": jax.random.normal(ks[13], (DEPTH, CONV_WIDTH, 2 * F), f32) * CONV_WIDTH ** -0.5,
        "ffn_conv_b": 0.01 * jax.random.normal(ks[14], (DEPTH, 2 * F), f32),
        "ffn_w_out": jax.random.normal(ks[15], (DEPTH, F, D), f32) * F ** -0.5,
    }

def first_block(x, positions, mix_pre_g, mix_post_g, pool_w, pool_scale, kv_norm_g, w_kv,
              w_q, w_o, sinks, ffn_pre_g, ffn_post_g, ffn_w_in, ffn_conv_w, ffn_conv_b, ffn_w_out):
    B, S, D = x.shape
    cos, sin = rope_tables(positions)
    kk = vv = None
    for layer in range(DEPTH):
        h = rms_norm(x, mix_pre_g[layer])
        if layer < N_A:
            m = pool_mixer(h, pool_w[layer], pool_scale[layer])
        else:
            if layer == N_A:
                hkv = rms_norm(x, kv_norm_g)
                kv = (hkv @ w_kv).reshape(B, S, 2, N_KV_HEADS, HEAD_DIM)
                k_shared = rope(kv[:, :, 0], cos, sin)
                kk, vv = band_blocks(k_shared), band_blocks(kv[:, :, 1])
            j = layer - N_A
            q = rope((h @ w_q[j]).reshape(B, S, N_Q_HEADS, HEAD_DIM), cos, sin)
            m = swa_sink_attention(q, kk, vv, sinks[j]) @ w_o[j]
        x = x + rms_norm(m, mix_post_g[layer])
        f = conv_glu_ffn(rms_norm(x, ffn_pre_g[layer]), ffn_w_in[layer], ffn_conv_w[layer],
                         ffn_conv_b[layer], ffn_w_out[layer])
        x = x + rms_norm(f, ffn_post_g[layer])
    return x


DEPTH_2 = 1

PLE_DIM = 256
M_HEADS = 4
M_HEAD_DIM = 128
M_WIDTH = M_HEADS * M_HEAD_DIM
M_CHUNK = 64
A_HEADS = 8
A_KV_GROUPS = 2
A_HEAD_DIM = 64
A_WIDTH = A_HEADS * A_HEAD_DIM
KV_WIDTH = A_KV_GROUPS * A_HEAD_DIM
CMP_BLOCK = 32
CMP_STRIDE = 16
CMP_HIDDEN = 128
SEL_BLOCK = 64
N_SELECT = 16
WINDOW_2 = 512
A_Q_BLOCK = 32
ALIBI_MAX = 8.0
MIX_WIDTH = M_WIDTH + A_WIDTH
IN_WIDTH = 4 * M_WIDTH + 2 * M_HEADS + A_WIDTH + 6 * KV_WIDTH + 3 * A_HEADS
D_FF_2 = 2048
EPS = 1e-6
NEG = -1e30
BIG = 1e30


def rms_norm_2(x, g):
    xf = x.astype(jnp.float32)
    y = xf * lax.rsqrt(jnp.mean(xf * xf, axis=-1, keepdims=True) + EPS)
    return (y * g.astype(jnp.float32)).astype(x.dtype)

def alibi_slopes(n):
    return jnp.exp2(-ALIBI_MAX * jnp.arange(1, n + 1, dtype=jnp.float32) / n)

def mlstm(q, k, v, i_pre, f_pre):
    B, S, H, dh = q.shape
    L = M_CHUNK
    NC = S // L
    f32 = jnp.float32

    def chunks(t):
        t = t.astype(f32).reshape((B, NC, L, H) + t.shape[3:])
        return jnp.moveaxis(t, 3, 1)

    qc = chunks(q) * (dh ** -0.5)
    kc = chunks(k)
    vc = chunks(v)
    ig = chunks(i_pre)
    b = jnp.cumsum(jax.nn.log_sigmoid(chunks(f_pre)), axis=-1)
    bL = b[..., -1]
    a = bL[..., None] - b + ig

    def step(carry, inp):
        C, n, m = carry
        k_, v_, a_, bL_ = inp
        m_new = jnp.maximum(bL_ + m, jnp.max(a_, axis=-1))
        decay = jnp.exp(bL_ + m - m_new)
        w = jnp.exp(a_ - m_new[..., None])
        C_new = decay[..., None, None] * C + jnp.einsum('bhl,bhlk,bhlv->bhkv', w, k_, v_)
        n_new = decay[..., None] * n + jnp.einsum('bhl,bhlk->bhk', w, k_)
        return (C_new, n_new, m_new), (C, n, m)

    init = (jnp.zeros((B, H, dh, dh), f32), jnp.zeros((B, H, dh), f32), jnp.zeros((B, H), f32))
    xs = (jnp.moveaxis(kc, 2, 0), jnp.moveaxis(vc, 2, 0), jnp.moveaxis(a, 2, 0), jnp.moveaxis(bL, 2, 0))
    _, (Cs, ns, ms) = lax.scan(step, init, xs)
    Cs = jnp.moveaxis(Cs, 0, 2)
    ns = jnp.moveaxis(ns, 0, 2)
    ms = jnp.moveaxis(ms, 0, 2)

    bq = b + ms[..., None]
    causal = jnp.tril(jnp.ones((L, L), dtype=bool))
    Dm = jnp.where(causal, b[..., :, None] - b[..., None, :] + ig[..., None, :], -jnp.inf)
    m = jnp.maximum(bq, jnp.max(Dm, axis=-1))
    inter = jnp.exp(bq - m)
    Wt = jnp.exp(Dm - m[..., None]) * jnp.einsum('bhcld,bhcsd->bhcls', qc, kc)
    num = inter[..., None] * jnp.einsum('bhcld,bhcdv->bhclv', qc, Cs) + jnp.einsum('bhcls,bhcsv->bhclv', Wt, vc)
    den = inter * jnp.einsum('bhcld,bhcd->bhcl', qc, ns) + jnp.sum(Wt, axis=-1)
    h = num / jnp.maximum(jnp.abs(den), jnp.exp(-m))[..., None]
    return jnp.moveaxis(h, 1, 3).reshape(B, S, H, dh)

def nsa(q, kc_raw, vc_raw, ks_raw, vs_raw, kw_raw, vw_raw, g_pre, pe_k, pe_v, ck_w1, ck_w2, cv_w1, cv_w2):
    f32 = jnp.float32
    B, S, H, dh = q.shape
    G = A_KV_GROUPS
    R = H // G
    qg = q.astype(f32).reshape(B, S, G, R, dh).transpose(0, 2, 3, 1, 4) * (dh ** -0.5)
    gates = jax.nn.sigmoid(g_pre.astype(f32).reshape(B, S, G, R, 3)).transpose(0, 2, 3, 1, 4)
    to_g = lambda t: t.astype(f32).transpose(0, 2, 1, 3)

    Nc = (S - CMP_BLOCK) // CMP_STRIDE + 1
    cidx = jnp.arange(Nc)[:, None] * CMP_STRIDE + jnp.arange(CMP_BLOCK)[None, :]

    def compress(t, pe, w1, w2):
        blk = to_g(t)[:, :, cidx] + pe.astype(f32)
        flat = blk.reshape(B, G, Nc, CMP_BLOCK * dh)
        return jax.nn.gelu(flat @ w1.astype(f32)) @ w2.astype(f32)

    Kc = compress(kc_raw, pe_k, ck_w1, ck_w2)
    Vc = compress(vc_raw, pe_v, cv_w1, cv_w2)
    cmp_start = jnp.arange(Nc) * CMP_STRIDE
    cmp_end = cmp_start + CMP_BLOCK - 1

    Ns = S // SEL_BLOCK
    n_sel = min(N_SELECT, Ns)
    Ks = to_g(ks_raw).reshape(B, G, Ns, SEL_BLOCK, dh)
    Vs = to_g(vs_raw).reshape(B, G, Ns, SEL_BLOCK, dh)
    sel_start = jnp.arange(Ns) * SEL_BLOCK
    overlap = ((cmp_start[:, None] <= sel_start[None, :] + SEL_BLOCK - 1)
               & (cmp_end[:, None] >= sel_start[None, :])).astype(f32)

    pad = ((0, 0), (0, 0), (WINDOW_2, 0), (0, 0))
    Kw = jnp.pad(to_g(kw_raw), pad)
    Vw = jnp.pad(to_g(vw_raw), pad)

    slope = alibi_slopes(H).reshape(1, G, R, 1, 1)
    bi = jnp.arange(B)[:, None, None, None]
    gi = jnp.arange(G)[None, :, None, None]
    T = A_Q_BLOCK

    def block(qb):
        t0 = qb * T
        t = t0 + jnp.arange(T)
        qblk = lax.dynamic_slice_in_dim(qg, t0, T, axis=3)
        gblk = lax.dynamic_slice_in_dim(gates, t0, T, axis=3)

        valid_c = cmp_end[None, :] <= t[:, None]
        dist_c = (t[:, None] - cmp_end[None, :]).astype(f32)
        s_c = jnp.einsum('bgrtd,bgnd->bgrtn', qblk, Kc) - slope * dist_c
        p_c = jnp.where(valid_c, jax.nn.softmax(jnp.where(valid_c, s_c, NEG), axis=-1), 0.0)
        o_c = jnp.einsum('bgrtn,bgnd->bgrtd', p_c, Vc)

        imp = jnp.einsum('bgrtn,nj->bgtj', p_c, overlap)
        j = jnp.arange(Ns)[None, :]
        cur = (t // SEL_BLOCK)[:, None]
        forced = (j == 0) | (j == cur) | (j == cur - 1)
        causal_b = sel_start[None, :] <= t[:, None]
        score = jnp.where(causal_b, jnp.where(forced, BIG, imp), NEG)
        sel_idx = lax.top_k(score, n_sel)[1]
        Ksel = Ks[bi, gi, sel_idx]
        Vsel = Vs[bi, gi, sel_idx]
        pos_s = sel_idx[..., None] * SEL_BLOCK + jnp.arange(SEL_BLOCK)
        dist_s = (t[None, None, :, None, None] - pos_s)
        valid_s = (dist_s >= 0)[:, :, None]
        s_s = jnp.einsum('bgrtd,bgtnld->bgrtnl', qblk, Ksel) - slope[..., None] * dist_s[:, :, None].astype(f32)
        s_s = jnp.where(valid_s, s_s, NEG).reshape(B, G, R, T, n_sel * SEL_BLOCK)
        p_s = jax.nn.softmax(s_s, axis=-1).reshape(B, G, R, T, n_sel, SEL_BLOCK)
        o_s = jnp.einsum('bgrtnl,bgtnld->bgrtd', p_s, Vsel)

        kwin = lax.dynamic_slice_in_dim(Kw, t0, WINDOW_2 + T, axis=2)
        vwin = lax.dynamic_slice_in_dim(Vw, t0, WINDOW_2 + T, axis=2)
        pos_w = t0 - WINDOW_2 + jnp.arange(WINDOW_2 + T)
        dist_w = t[:, None] - pos_w[None, :]
        valid_w = (pos_w[None, :] >= 0) & (dist_w >= 0) & (dist_w < WINDOW_2)
        s_w = jnp.einsum('bgrtd,bgsd->bgrts', qblk, kwin) - slope * dist_w.astype(f32)
        p_w = jax.nn.softmax(jnp.where(valid_w, s_w, NEG), axis=-1)
        o_w = jnp.einsum('bgrts,bgsd->bgrtd', p_w, vwin)

        return gblk[..., 0:1] * o_c + gblk[..., 1:2] * o_s + gblk[..., 2:3] * o_w

    outs = lax.map(block, jnp.arange(S // T))
    return outs.transpose(1, 0, 4, 2, 3, 5).reshape(B, S, H * dh)

def conv_ffn(h, w_up, conv_w, conv_b, w_down):
    u = h @ w_up
    gate, val = jnp.split(u, 2, axis=-1)
    gate = lax.conv_general_dilated(gate, conv_w[:, None, :].astype(gate.dtype), window_strides=(1,),
                                    padding=[(CONV_WIDTH - 1, 0)],
                                    dimension_numbers=('NWC', 'WIO', 'NWC'),
                                    feature_group_count=D_FF_2) + conv_b
    return (jax.nn.silu(gate) * val) @ w_down

def second_inputs(seed: int = 0) -> dict:
    key = jax.random.key(seed)
    ks = jax.random.split(key, 24)
    f32 = jnp.float32
    nrm = lambda k, shape, scale: jax.random.normal(k, shape, f32) * scale
    gain = lambda k, shape: 1.0 + 0.05 * jax.random.normal(k, shape, f32)
    i_bias = nrm(ks[4], (DEPTH_2, M_HEADS), 0.1)
    f_bias = jnp.linspace(3.0, 6.0, M_HEADS, dtype=f32)[None, :] + nrm(ks[5], (DEPTH_2, M_HEADS), 0.1)
    return {
        "x": nrm(ks[0], (BATCH, SEQ, D_MODEL), 1.0),
        "p": nrm(ks[1], (DEPTH_2, BATCH, SEQ, PLE_DIM), 1.0),
        "ln1_g": gain(ks[2], (DEPTH_2, D_MODEL)),
        "w_in": nrm(ks[3], (DEPTH_2, D_MODEL, IN_WIDTH), D_MODEL ** -0.5),
        "mlstm_gate_bias": jnp.concatenate([i_bias, f_bias], axis=-1),
        "mlstm_norm_g": gain(ks[6], (DEPTH_2, M_WIDTH)),
        "cmp_pos_k": nrm(ks[7], (DEPTH_2, CMP_BLOCK, A_HEAD_DIM), 0.02),
        "cmp_pos_v": nrm(ks[8], (DEPTH_2, CMP_BLOCK, A_HEAD_DIM), 0.02),
        "cmp_k_w1": nrm(ks[9], (DEPTH_2, CMP_BLOCK * A_HEAD_DIM, CMP_HIDDEN), (CMP_BLOCK * A_HEAD_DIM) ** -0.5),
        "cmp_k_w2": nrm(ks[10], (DEPTH_2, CMP_HIDDEN, A_HEAD_DIM), CMP_HIDDEN ** -0.5),
        "cmp_v_w1": nrm(ks[11], (DEPTH_2, CMP_BLOCK * A_HEAD_DIM, CMP_HIDDEN), (CMP_BLOCK * A_HEAD_DIM) ** -0.5),
        "cmp_v_w2": nrm(ks[12], (DEPTH_2, CMP_HIDDEN, A_HEAD_DIM), CMP_HIDDEN ** -0.5),
        "w_out": nrm(ks[13], (DEPTH_2, MIX_WIDTH, D_MODEL), MIX_WIDTH ** -0.5),
        "ln2_g": gain(ks[14], (DEPTH_2, D_MODEL)),
        "w_up": nrm(ks[15], (DEPTH_2, D_MODEL, 2 * D_FF_2), D_MODEL ** -0.5),
        "conv_w": nrm(ks[16], (DEPTH_2, CONV_WIDTH, D_FF_2), CONV_WIDTH ** -0.5),
        "conv_b": nrm(ks[17], (DEPTH_2, D_FF_2), 0.02),
        "w_down": nrm(ks[18], (DEPTH_2, D_FF_2, D_MODEL), D_FF_2 ** -0.5),
        "ple_norm_g": gain(ks[19], (DEPTH_2, D_MODEL)),
        "w_ple_gate": nrm(ks[20], (DEPTH_2, D_MODEL, D_MODEL), D_MODEL ** -0.5),
        "w_ple_proj": nrm(ks[21], (DEPTH_2, PLE_DIM, D_MODEL), PLE_DIM ** -0.5),
        "final_g": gain(ks[22], (D_MODEL,)),
    }

def second_block(x, p, ln1_g, w_in, mlstm_gate_bias, mlstm_norm_g, cmp_pos_k, cmp_pos_v, cmp_k_w1, cmp_k_w2,
              cmp_v_w1, cmp_v_w2, w_out, ln2_g, w_up, conv_w, conv_b, w_down, ple_norm_g, w_ple_gate,
              w_ple_proj, final_g):
    B, S, _ = x.shape
    sizes = [M_WIDTH] * 4 + [M_HEADS, M_HEADS, A_WIDTH] + [KV_WIDTH] * 6 + [3 * A_HEADS]
    offs = np.cumsum(sizes)[:-1].tolist()
    for i in range(DEPTH_2):
        h = rms_norm_2(x, ln1_g[i])
        z = h @ w_in[i]
        mq, mk, mv, mo, mi, mf, aq, akc, avc, aks, avs, akw, avw, ag = jnp.split(z, offs, axis=-1)
        mshape = (B, S, M_HEADS, M_HEAD_DIM)
        hm = mlstm(mq.reshape(mshape), mk.reshape(mshape), mv.reshape(mshape),
                   mi + mlstm_gate_bias[i, :M_HEADS], mf + mlstm_gate_bias[i, M_HEADS:])
        hm = rms_norm_2(hm, mlstm_norm_g[i].reshape(M_HEADS, M_HEAD_DIM)).reshape(B, S, M_WIDTH)
        m_out = (hm * jax.nn.sigmoid(mo.astype(jnp.float32))).astype(x.dtype)
        kvshape = (B, S, A_KV_GROUPS, A_HEAD_DIM)
        a_out = nsa(aq.reshape(B, S, A_HEADS, A_HEAD_DIM), akc.reshape(kvshape), avc.reshape(kvshape),
                    aks.reshape(kvshape), avs.reshape(kvshape), akw.reshape(kvshape), avw.reshape(kvshape),
                    ag, cmp_pos_k[i], cmp_pos_v[i], cmp_k_w1[i], cmp_k_w2[i], cmp_v_w1[i], cmp_v_w2[i]).astype(x.dtype)
        x = x + jnp.concatenate([m_out, a_out], axis=-1) @ w_out[i]
        x = x + conv_ffn(rms_norm_2(x, ln2_g[i]), w_up[i], conv_w[i], conv_b[i], w_down[i])
        gate = jax.nn.sigmoid(rms_norm_2(x, ple_norm_g[i]) @ w_ple_gate[i])
        x = x + gate * (p[i].astype(x.dtype) @ w_ple_proj[i])
    return rms_norm_2(x, final_g)


def setup_inputs(seed=0):
    out = dict(first_inputs(seed))
    for name, value in second_inputs(seed + 1).items():
        if name != "x":
            out[name + "_2"] = value
    return out


def reference(
    x, positions, mix_pre_g, mix_post_g, pool_w, pool_scale, kv_norm_g, w_kv, w_q, w_o, sinks,
    ffn_pre_g, ffn_post_g, ffn_w_in, ffn_conv_w, ffn_conv_b, ffn_w_out, p_2, ln1_g_2, w_in_2,
    mlstm_gate_bias_2, mlstm_norm_g_2, cmp_pos_k_2, cmp_pos_v_2, cmp_k_w1_2, cmp_k_w2_2,
    cmp_v_w1_2, cmp_v_w2_2, w_out_2, ln2_g_2, w_up_2, conv_w_2, conv_b_2, w_down_2,
    ple_norm_g_2, w_ple_gate_2, w_ple_proj_2, final_g_2,
):
    x = first_block(
        x, positions, mix_pre_g, mix_post_g, pool_w, pool_scale, kv_norm_g, w_kv, w_q, w_o,
        sinks, ffn_pre_g, ffn_post_g, ffn_w_in, ffn_conv_w, ffn_conv_b, ffn_w_out,
    )
    return second_block(
        x, p_2, ln1_g_2, w_in_2, mlstm_gate_bias_2, mlstm_norm_g_2, cmp_pos_k_2, cmp_pos_v_2,
        cmp_k_w1_2, cmp_k_w2_2, cmp_v_w1_2, cmp_v_w2_2, w_out_2, ln2_g_2, w_up_2, conv_w_2,
        conv_b_2, w_down_2, ple_norm_g_2, w_ple_gate_2, w_ple_proj_2, final_g_2,
    )


_drawn_inputs = setup_inputs


def setup_inputs(seed=0):
    import zlib

    import numpy as np

    out = dict(_drawn_inputs(seed))
    spreads = {}
    factors = {'ffn_conv_b': 3.301,
     'ln1_g_2': 3.012,
     'mlstm_norm_g_2': 6.759,
     'cmp_pos_k_2': 8.0,
     'cmp_pos_v_2': 27.941,
     'cmp_k_w1_2': 3.596,
     'cmp_k_w2_2': 3.654,
     'ln2_g_2': 3.13,
     'conv_b_2': 8.0,
     'ple_norm_g_2': 64.0}
    for name, (base, spread) in spreads.items():
        noise = np.random.default_rng([zlib.crc32(name.encode()), seed]).standard_normal(out[name].shape)
        drawn = base * np.exp(spread * noise) if base else spread * noise
        out[name] = __import__('jax').numpy.asarray(drawn.astype(out[name].dtype))
    for name, factor in factors.items():
        out[name] = (out[name] * factor).astype(out[name].dtype)
    return out
```

```python
import math
from contextlib import ExitStack

import numpy as np

import concourse.bass as bass
from concourse import mybir

ALU = mybir.AluOpType
ACT = mybir.ActivationFunctionType
F32 = mybir.dt.float32
F32R = mybir.dt.float32r
I32 = mybir.dt.int32
AX = mybir.AxisListType.X

P = 128
S = 512
D = 1024
KD = 8
FT = 22
FT2 = 16
NEG = -1e30
EPS = 1e-6
SLOPES = [2.0 ** (-(h + 1)) for h in range(8)]
NPIECE = 512
TW = S + 2
MAGIC = 12582912.0
PI_HI, PI_MID, PI_LO = 6.28125, 0.0019350051879882812, 3.0197183517896e-07

COLS = {}
_at = 0
for _n, _w in (("mix_pre0", 8), ("mix_pre1", 8), ("mix_post0", 8), ("mix_post1", 8), ("pool_scale", 8),
               ("kv_g", 8), ("ffn_pre0", 8), ("ffn_pre1", 8), ("ffn_post0", 8), ("ffn_post1", 8),
               ("ln1", 8), ("ln2", 8), ("ple_g", 8), ("final_g", 8), ("m_g", 4),
               ("cw0", 132), ("cb0", 44), ("cw1", 132), ("cb1", 44), ("cw2", 48), ("cb2", 16),
               ("sinks", 16), ("gbias", 2), ("invf", 1), ("rv", 1)):
    COLS[_n] = (_at, _w)
    _at += _w
NCOLS = _at

CONST = {}
_at = 0
for _n, _w in (("ident", 128), ("dist", 512), ("swa", 256), ("cmp", 124), ("sel", 512), ("invc", 64)):
    CONST[_n] = (_at, _w)
    _at += _w
NCONST = _at


class Engine:

    def __init__(self, e, sem):
        self.e, self.sem, self.count, self.queue, self.seen = e, sem, 0, [], {}

    def wait(self, *tokens):
        for t in flat(tokens):
            who, value = t
            if self.seen.get(who, 0) < value:
                self.seen[who] = value
                self.queue.append((self.e.wait_ge, (who.sem, value), {}, None, 0))

    def do(self, tokens, op, *args, **named):
        self.wait(tokens)
        self.count += 1
        self.queue.append((op, args, named, self.sem, 1))
        return (self, self.count)

    def quiet(self, tokens, op, *args, **named):
        self.wait(tokens)
        self.queue.append((op, args, named, None, 0))

    def dma(self, tokens, lot, op, *args, **named):
        self.wait(tokens)
        lot.count += 16
        self.queue.append((op, args, named, lot.sem, 16))
        return (lot, lot.count)

    def run(self):
        for op, args, named, sem, by in self.queue:
            done = op(*args, **named)
            if sem is not None:
                done.then_inc(sem, by)


class Lot:

    def __init__(self, sem):
        self.sem, self.count = sem, 0


def flat(tokens):
    for t in tokens:
        if isinstance(t, list):
            yield from flat(t)
        elif t is not None:
            yield t


class Slots:

    def __init__(self, places):
        self.free = [(p, []) for p in places]

    def take(self):
        return self.free.pop(0)

    def give(self, place, *tokens):
        self.free.append((place, list(flat(tokens))))


def build(nc, A, out, stop=None):
    ctx = ExitStack()
    with ctx:
        base = [(nc.sbuf_base + 63) // 64 * 64]
        limit = nc.sbuf_base + 212000

        def place(nbytes):
            at = base[0]
            base[0] += (nbytes + 63) // 64 * 64
            assert base[0] <= limit, (base[0], limit)
            return at

        def at(name, shape, off, dt=F32):
            return nc.alloc_sbuf_tensor_at(name, shape, dt, offset=off)

        def sb(name, shape, dt=F32):
            n = 4
            for x in shape[1:]:
                n *= x
            return at(name, shape, place(n), dt)

        pe, act, dve, pool, sp = (
            Engine(e, ctx.enter_context(nc.semaphore(n)))
            for e, n in ((nc.tensor, "s_pe"), (nc.scalar, "s_act"), (nc.vector, "s_dve"), (nc.gpsimd, "s_pool"),
                         (nc.sync, "s_sp")))

        def lot(name):
            return Lot(ctx.enter_context(nc.semaphore(name)))

        X = sb("X", [P, KD, S])
        m_at = place(KD * S * 4)
        M = at("M", [P, KD, S], m_at)
        Hh = sb("Hh", [P, KD, S], F32R)
        Hl = sb("Hl", [P, KD, S], F32R)
        arena = place(2 * FT * S * 4)
        NRAW, NSPL, NT = 5, 4, 8
        raws = [sb(f"raw{i}", [P, NPIECE]) for i in range(NRAW)]
        raw_lots = [lot(f"s_raw{i}") for i in range(NRAW)]
        spls = [(sb(f"wh{i}", [P, NPIECE], F32R), sb(f"wl{i}", [P, NPIECE], F32R)) for i in range(NSPL)]
        ts = [sb(f"t{i}", [P, TW]) for i in range(NT)]
        RB = sb("RB", [P, S])
        DG = sb("DG", [P, 4, P])
        cols = sb("cols", [P, NCOLS])
        ident = sb("ident", [P, P])
        ones = sb("ones", [P, P])
        st = sb("st", [P, 128])
        banks = [ctx.enter_context(nc.psum_tensor(f"ps{i}", [P, S], F32)) for i in range(8)]

        raw_slots = Slots(list(range(NRAW)))
        spl_slots = Slots(list(range(NSPL)))
        T = Slots(ts)
        B = Slots(banks)

        def col(name, i):
            o = COLS[name][0] + i
            return cols[:, o:o + 1]

        l_x, l_c, l_k = lot("s_x"), lot("s_cols"), lot("s_ident")
        d_x = act.dma([], l_x, act.e.dma_start, X[:, :, :], A["xT"].rearrange("(c p) t -> p c t", p=P))
        d_c = act.dma([], l_c, act.e.dma_start, cols[:, :], A["cols"])
        d_k = act.dma([], l_k, act.e.dma_start, ident[:, :], A["const"][:, 0:P])
        ones_t = pool.do([], pool.e.memset, ones[:, :], 1.0)
        pads = [pool.do([], pool.e.memset, t[:, 0:2], 0.0) for t in ts]
        pads_t = pads[-1]
        for e in (act, dve, pool, pe):
            e.wait(d_c)
        for e in (dve, pe):
            e.wait(d_k, ones_t, pads_t)
        act.wait(pads_t)
        for e in (act, dve, pool):
            e.wait(d_x)

        plan = []

        def pieces_of(w, k, groups):
            at_ = 0
            for g in groups:
                for r in range(k):
                    plan.append((w[r * P:(r + 1) * P, at_:at_ + g], g))
                at_ += g

        for gi in range(4):
            plan.append((A["pool_w"][gi].rearrange("(k p) c -> p k c", p=P), 512))
        for layer in range(2):
            if layer == 1:
                pieces_of(A["w_kv"], 8, [512])
                pieces_of(A["w_q"], 8, [512, 512])
                pieces_of(A["w_o"], 8, [512, 512])
            pieces_of(A[f"w_in{layer}"], 8, [512] * 11)
            pieces_of(A[f"w_out{layer}"], FT, [512, 512])
        pieces_of(A["w_in_2"], 8, [512, 512, 344] + [512] * 4)
        pieces_of(A["w_out_2"], 8, [512, 512])
        pieces_of(A["w_up_2"], 8, [512] * 8)
        pieces_of(A["w_down_2"], FT2, [512, 512])
        for g in range(2):
            for k in range(8):
                plan.append((A["w_pg"][k * P:(k + 1) * P, g * 512:g * 512 + 512], 512))
            for k in range(2):
                plan.append((A["w_pp"][k * P:(k + 1) * P, g * 512:g * 512 + 512], 512))

        class W:
            loaded = 0
            split = 0
            used = 0
            raw = {}
            ready = {}

        def load_piece():
            n = W.loaded
            if n >= len(plan):
                return
            r, free = raw_slots.take()
            src, width = plan[n]
            dst = raws[r][:, 0:width]
            if len(src.shape) == 3:
                dst = dst.rearrange("p (k c) -> p k c", k=src.shape[1])
            t = sp.dma([free], raw_lots[r], sp.e.dma_start, dst, src)
            W.raw[n] = (r, t)
            W.loaded += 1

        def split_piece():
            n = W.split
            if n >= len(plan) or n - W.used >= NSPL:
                return
            while W.loaded <= n:
                load_piece()
            r, landed = W.raw.pop(n)
            width = plan[n][1]
            s, free = spl_slots.take()
            wh, wl = spls[s]
            raw = raws[r][:, 0:width]
            th = act.do([landed, free], act.e.activation, wh[:, 0:width], raw, ACT.Copy)
            tl = dve.do([landed, free, th], dve.e.tensor_tensor, wl[:, 0:width], raw, wh[:, 0:width].bitcast(F32),
                        ALU.subtract)
            raw_slots.give(r, th, tl)
            W.ready[n] = (s, th, tl)
            W.split += 1
            load_piece()

        def next_piece():
            while W.split <= W.used + (NSPL - 1) and W.split < len(plan) and W.split - W.used < NSPL:
                split_piece()
            n = W.used
            s, th, tl = W.ready.pop(n)
            return s, [th, tl]

        def done_piece(s, t):
            spl_slots.give(s, t)
            W.used += 1

        for _ in range(NRAW):
            load_piece()

        def mm3(bank_ap, wh, wl, xh, xl, first, last):
            pe.quiet([], pe.e.matmul, bank_ap, wh, xh, start=first, stop=False)
            pe.quiet([], pe.e.matmul, bank_ap, wh, xl, start=False, stop=False)
            return pe.do([], pe.e.matmul, bank_ap, wl, xh, start=False, stop=last)

        def gemm(widths, rhs, mid=None, midk=3):
            res = []
            for w in widths:
                b, free = B.take()
                res.append([b, free, None])
            nk = len(rhs)
            for k in range(nk):
                s, ready = next_piece()
                wh, wl = spls[s]
                xh, xl, t = rhs[k]
                pe.wait(ready, t)
                o = 0
                for i, w in enumerate(widths):
                    b, free, _ = res[i]
                    if k == 0:
                        pe.wait(free)
                    last = mm3(b[0:w, :], wh[:, o:o + w], wl[:, o:o + w], xh, xl, k == 0, k == nk - 1)
                    res[i][2] = last
                    o += w
                done_piece(s, last)
                if mid is not None and k == midk:
                    mid()
            return [(b, t) for b, _, t in res]

        class Stat:

            def __init__(self):
                self.bank, self.free = B.take()
                self.n = 0
                self.last = None

            def add(self, sq, tok):
                for b in range(4):
                    first = self.n == 0 and b == 0
                    self.last = pe.do([tok, self.free if first else None], pe.e.matmul, self.bank[:, b:b + 1],
                                      sq[:, b * P:(b + 1) * P], ones[:, 0:1], start=first, stop=True,
                                      skip_group_check=True)
                self.n += 1
                return self.last

            def finish(self, free, inv_n=1.0 / D):
                v, r = st[:, 0:4], st[:, 4:8]
                a = dve.do([self.last], dve.e.tensor_scalar, v, self.bank[:, 0:4], inv_n, EPS, ALU.mult, ALU.add)
                B.give(self.bank, a)
                a = act.do([a], act.e.activation, r, v, ACT.Sqrt)
                a = dve.do([a], dve.e.reciprocal, v, r)
                return spread(v, 4, [a], RB[:, :], free)

        def spread(v, n, toks, dst, free):
            a = dve.do([toks, spread.dg], dve.e.tensor_tensor, DG[:, :, :],
                       ident[:, :].unsqueeze(1).to_broadcast([P, 4, P]), v.unsqueeze(2).to_broadcast([P, 4, P]),
                       ALU.mult)
            b, bf = B.take()
            a = pe.do([a, bf], pe.e.matmul, b[:, :], ones[:, :], DG[:, :, :].rearrange("p a b -> p (a b)"),
                      start=True, stop=True)
            spread.dg = a
            a = act.do([a, free], act.e.activation, dst, b[:, :], ACT.Copy)
            B.give(b, a)
            return a
        spread.dg = None

        state = {"rb_readers": [], "h_readers": None, "m_readers": []}

        def square_into(dst, src, *toks):
            return act.do([*toks], act.e.activation, dst, src, ACT.Square)

        def parts(c, gname, xt, kv=False):
            g = col(gname, c)
            th = act.do([xt, state["h_readers"]], act.e.activation, Hh[:, c, :], X[:, c, :], ACT.Copy, scale=g)
            tl = dve.do([xt, th, state["h_readers"]], dve.e.scalar_tensor_tensor, Hl[:, c, :], X[:, c, :], g,
                        Hh[:, c, :].bitcast(F32), ALU.mult, ALU.subtract)
            return [th, tl]

        def hrhs(toks):
            return [(Hh[:, c, :], Hl[:, c, :], toks[c]) for c in range(KD)]

        def residual(mt, stat, gname, sq=True):
            r = stat.finish(state["rb_readers"])
            xt, qt = [], []
            for c in range(KD):
                g = col(gname, c)
                a = dve.do([r, mt[c]], dve.e.scalar_tensor_tensor, M[:, c, :], M[:, c, :], g, RB[:, :], ALU.mult,
                           ALU.mult)
                x = pool.do([a, state.get("x_readers")], pool.e.tensor_tensor, X[:, c, :], X[:, c, :], M[:, c, :],
                            ALU.add)
                xt.append(x)
                last = a
            state["rb_readers"] = [last]
            return xt

        def squares(xt):
            return [square_into(M[:, c, :], X[:, c, :], xt[c], state["m_readers"]) for c in range(KD)]

        def evac_m(group, c0, stat_in, scale=None):
            toks, held = [], []
            for i, (b, t) in enumerate(group):
                c = c0 + i
                if scale is None:
                    a = dve.do([t, state["m_readers"]], dve.e.tensor_copy, M[:, c, :], b[:, :])
                else:
                    g = col(scale, c)
                    a = dve.do([t, state["m_readers"]], dve.e.tensor_scalar, M[:, c, :], b[:, :], g, None, ALU.mult)
                B.give(b, a)
                q, qf = T.take()
                s = square_into(q[:, 2:TW], M[:, c, :], a, qf)
                toks.append(a)
                held.append((q, s))
            return toks, held

        def count_squares(stat, held):
            for q, s in held:
                T.give(q, stat.add(q[:, 2:TW], s))

        def ffn(n, groups, gname, conv, both, func, ntile, post):
            AHn = at(f"AH{n}", [P, ntile, S], arena, F32R)
            ALn = at(f"AL{n}", [P, ntile, S], arena + ntile * S * 4, F32R)
            toks = [parts(c, gname, state["xt"][c]) for c in range(KD)]
            sq = squares(state["xt"])
            box = {}

            def stats():
                s = Stat()
                for c in range(KD):
                    last = s.add(M[:, c, :], sq[c])
                state["m_readers"] = [last]
                box["rb"] = s.finish(state["rb_readers"])

            cw, cb = (COLS[x][0] for x in (f"cw{n}", f"cb{n}"))
            nct = {0: 44, 1: 44, 2: 16}[n]
            at_toks = []
            arena_free = state["arena_readers"]

            def conv_tile(u, ut, i):
                w = [cols[:, cw + k * nct + i:cw + k * nct + i + 1] for k in range(3)]
                bb = cols[:, cb + i:cb + i + 1]
                c, cf = T.take()
                co = c[:, 2:TW]
                a = act.do([ut, cf], act.e.activation, co, u[:, 2:TW], ACT.Identity, bias=bb, scale=w[2])
                a = dve.do([a], dve.e.scalar_tensor_tensor, co, u[:, 1:TW - 1], w[1], co, ALU.mult, ALU.add)
                a = dve.do([a], dve.e.scalar_tensor_tensor, co, u[:, 0:TW - 2], w[0], co, ALU.mult, ALU.add)
                T.give(u, a)
                return c, a

            for g in range(groups):
                res = gemm([P] * 4, hrhs(toks))
                if g == 0:
                    stats()
                rb = box["rb"]
                for i in range(2):
                    f = 2 * g + i
                    (gb, gt), (vb, vt) = res[i], res[2 + i]
                    u, uf = T.take()
                    a = dve.do([gt, rb, uf], dve.e.tensor_tensor, u[:, 2:TW], gb[:, :], RB[:, :], ALU.mult)
                    B.give(gb, a)
                    v, vf = T.take()
                    b = dve.do([vt, rb, vf], dve.e.tensor_tensor, v[:, 2:TW], vb[:, :], RB[:, :], ALU.mult)
                    B.give(vb, b)
                    state["rb_readers"] = [b]
                    u, a = conv_tile(u, a, f)
                    if both:
                        v, b = conv_tile(v, b, ntile + f)
                    a = act.do([a], act.e.activation, u[:, 2:TW], u[:, 2:TW], func)
                    p = pool.do([a, b], pool.e.tensor_tensor, u[:, 2:TW], u[:, 2:TW], v[:, 2:TW], ALU.mult)
                    T.give(v, p)
                    h = act.do([p, arena_free], act.e.activation, AHn[:, f, :], u[:, 2:TW], ACT.Copy)
                    l = dve.do([p, h, arena_free], dve.e.tensor_tensor, ALn[:, f, :], u[:, 2:TW],
                               AHn[:, f, :].bitcast(F32), ALU.subtract)
                    T.give(u, l, h)
                    at_toks.append([h, l])
            state["h_readers"] = (pe, pe.count)
            arhs = [(AHn[:, f, :], ALn[:, f, :], at_toks[f]) for f in range(ntile)]
            if post is None:
                res = []
                xt = []
                for g in range(2):
                    for i, (b, t) in enumerate(gemm([P] * 4, arhs)):
                        c = 4 * g + i
                        x = dve.do([t, state["xt"][c], sq[c], toks[c]], dve.e.tensor_tensor, X[:, c, :], b[:, :],
                                   X[:, c, :], ALU.add)
                        B.give(b, x)
                        xt.append(x)
                state["xt"] = xt
            else:
                mt, held = [], []
                box["s"] = None
                stat = None
                for g in range(2):
                    def mid():
                        box["s"] = Stat()
                        count_squares(box["s"], held)
                    res = gemm([P] * 4, arhs, mid if g == 1 else None)
                    m, held = evac_m(res, 4 * g, None)
                    mt += m
                count_squares(box["s"], held)
                state["xt"] = residual(mt, box["s"], post)
            state["arena_readers"] = [(pe, pe.count)]

        state["arena_readers"] = []

        def sub(name, shape, off, dt=F32):
            return at(name, shape, arena + off, dt)

        def pool_mixer():
            invc = sub("invc", [P, 64], 0)
            l = lot("s_invc")
            dk = act.dma([], l, act.e.dma_start, invc[:, :], A["const"][:, CONST["invc"][0]:CONST["invc"][0] + 64])
            s = Stat()
            for c in range(KD):
                t = square_into(M[:, c, :], X[:, c, :])
                last = s.add(M[:, c, :], t)
            rb = s.finish([])
            state["m_readers"] = [last]
            toks = []
            for c in range(KD):
                gi = c // 2
                h, hf = T.take()
                g = col("mix_pre0", c)
                hv = h[:, 2:TW]
                ht = dve.do([rb, hf], dve.e.scalar_tensor_tensor, hv, X[:, c, :], g, RB[:, :], ALU.mult, ALU.mult)
                cur, ct = h, ht
                for step in range(gi + 1):
                    w = 1 << step
                    n, nf = T.take()
                    eng = dve if (c + step) % 3 else pool
                    a = eng.do([ct, nf], eng.e.tensor_tensor, n[:, 2 + w:TW], cur[:, 2 + w:TW], cur[:, 2:TW - w],
                               ALU.add)
                    b = act.do([ct, nf], act.e.activation, n[:, 2:2 + w], cur[:, 2:2 + w], ACT.Copy)
                    if cur is not h:
                        T.give(cur, a, b)
                    cur, ct = n, [a, b]
                w = 2 << gi
                d, df = T.take()
                a = dve.do([ct, ht, df], dve.e.scalar_tensor_tensor, d[:, 2 + w:TW], cur[:, 2 + w:TW], 1.0 / w,
                           h[:, 2 + w:TW], ALU.mult, ALU.subtract)
                b = dve.do([ct, dk], dve.e.tensor_tensor, cur[:, 2:2 + w], cur[:, 2:2 + w],
                           invc[:, 16 * gi:16 * gi + w], ALU.mult)
                b = dve.do([b, df], dve.e.tensor_tensor, d[:, 2:2 + w], cur[:, 2:2 + w], h[:, 2:2 + w], ALU.subtract)
                T.give(cur, a, b)
                T.give(h, a, b)
                th = act.do([a, b], act.e.activation, Hh[:, c, :], d[:, 2:TW], ACT.Copy)
                tl = dve.do([a, b, th], dve.e.tensor_tensor, Hl[:, c, :], d[:, 2:TW], Hh[:, c, :].bitcast(F32),
                            ALU.subtract)
                T.give(d, th, tl)
                toks.append([th, tl])
            state["rb_readers"] = [ht]
            mt, stat = [], Stat()
            for gi in range(4):
                sl, ready = next_piece()
                wh, wl = spls[sl]
                res = []
                for m in range(2):
                    b, bf = B.take()
                    pe.wait(bf, ready)
                    for k in range(2):
                        c = 2 * gi + k
                        pe.wait(toks[c])
                        o = k * 256 + m * P
                        t = mm3(b[:, :], wh[:, o:o + P], wl[:, o:o + P], Hh[:, c, :], Hl[:, c, :], k == 0, k == 1)
                    res.append((b, t))
                done_piece(sl, t)
                m_, held = evac_m(res, 2 * gi, None, "pool_scale")
                mt += m_
                count_squares(stat, held)
            state["h_readers"] = (pe, pe.count)
            state["xt"] = residual(mt, stat, "mix_post0")

        def window_mixer():
            q = sub("wq", [P, 8, S], 0)
            k_ = sub("wk", [P, 2, S], 16384)
            v_ = sub("wv", [P, 2, S], 20480)
            vt_ = sub("wvt", [P, 4, 256], 24576)
            cs = sub("wcs", [P, S], 28672)
            sn = sub("wsn", [P, S], 30720)
            ang = sub("wang", [P, S], 32768)
            y0 = sub("wy0", [P, S], 34816)
            y1 = sub("wy1", [P, S], 36864)
            posi = sub("wpos", [P, S], 38912, I32)
            mask = sub("wmask", [P, 256], 40960)
            Sb = [sub(f"wSb{i}", [P, 4, 256], 43008 + 4096 * i) for i in range(2)]
            PT = [sub(f"wPT{i}", [P, 8, P], 51200 + 4096 * i) for i in range(2)]
            sm = [sub(f"wsm{i}", [P, 32], 59392 + 128 * i) for i in range(2)]
            af = state["arena_readers"]
            lp, lm = lot("s_pos"), lot("s_mask")
            dp = act.dma([af], lp, act.e.dma_start, posi[:, :], A["pos"])
            o = CONST["swa"][0]
            dm = act.dma([af], lm, act.e.dma_start, mask[:, :], A["const"][:, o:o + 256])
            xt = state["xt"]
            toks = [parts(c, "kv_g", xt[c]) for c in range(KD)]
            sq = squares(xt)
            a = dve.do([dp, af], dve.e.tensor_copy, y0[:, :], posi[:, :])
            a = dve.do([a, af], dve.e.tensor_scalar, ang[:, :], y0[:, :], col("invf", 0), None, ALU.mult)
            r = None
            for turn, dst in ((0.0, sn), (0.25, cs)):
                b = dve.do([a, r], dve.e.tensor_scalar, y0[:, :], ang[:, :], 1.0 / (2 * math.pi), turn, ALU.mult,
                           ALU.add)
                b = dve.do([b], dve.e.tensor_scalar, y0[:, :], y0[:, :], MAGIC, None, ALU.add)
                b = dve.do([b], dve.e.tensor_scalar, y0[:, :], y0[:, :], MAGIC, None, ALU.subtract)
                src = ang
                for part in (PI_HI, PI_MID, PI_LO):
                    b = dve.do([b, r], dve.e.scalar_tensor_tensor, y1[:, :], y0[:, :], -part, src[:, :], ALU.mult,
                               ALU.add)
                    src = y1
                b = dve.do([b], dve.e.tensor_scalar, y1[:, :], y1[:, :], turn * 2 * math.pi, 3.1415925, ALU.add,
                           ALU.min)
                b = dve.do([b], dve.e.tensor_scalar, y1[:, :], y1[:, :], -3.1415925, None, ALU.max)
                r = act.do([b, af], act.e.activation, dst[:, :], y1[:, :], ACT.Sin)
            trig = r
            res = gemm([P] * 4, hrhs(toks))
            s = Stat()
            for c in range(KD):
                last = s.add(M[:, c, :], sq[c])
            state["m_readers"] = [last]
            rb = s.finish(state["rb_readers"])
            t1 = dve.do([trig, rb], dve.e.tensor_tensor, cs[:, :], cs[:, :], RB[:, :], ALU.mult)
            t2 = dve.do([trig, rb], dve.e.tensor_tensor, sn[:, :], sn[:, :], RB[:, :], ALU.mult)

            def rotate(ra, rbk, da, db, scale):
                (a, at_), (b, bt) = ra, rbk
                out_ = []
                tmp = []
                for src, st_, tab, tt in ((a, at_, cs, t1), (b, bt, sn, t2), (b, bt, cs, t1), (a, at_, sn, t2)):
                    x, xf = T.take()
                    if scale == 1.0:
                        y = dve.do([st_, tt, xf], dve.e.tensor_tensor, x[:, 2:TW], src[:, :], tab[:, :], ALU.mult)
                    else:
                        y = dve.do([st_, tt, xf], dve.e.scalar_tensor_tensor, x[:, 2:TW], src[:, :], scale,
                                   tab[:, :], ALU.mult, ALU.mult)
                    tmp.append((x, y))
                B.give(a, tmp[3][1])
                B.give(b, tmp[2][1])
                for i, dst, op in ((0, da, ALU.subtract), (2, db, ALU.add)):
                    (x, xt_), (y, yt_) = tmp[i], tmp[i + 1]
                    z = pool.do([xt_, yt_, af], pool.e.tensor_tensor, dst, x[:, 2:TW], y[:, 2:TW], op)
                    T.give(x, z)
                    T.give(y, z)
                    out_.append(z)
                return out_

            kt = rotate(res[0], res[1], k_[:, 0, :], k_[:, 1, :], 0.125)
            vts = []
            for i in range(2):
                b, t = res[2 + i]
                a = dve.do([t, rb, af], dve.e.tensor_tensor, v_[:, i, :], b[:, :], RB[:, :], ALU.mult)
                B.give(b, a)
                vts.append(a)
            state["rb_readers"] = [a]
            state["h_readers"] = (pe, pe.count)
            toks = [parts(c, "mix_pre1", xt[c]) for c in range(KD)]
            qt = []
            for g in range(2):
                res = gemm([P] * 4, hrhs(toks))
                for i in range(2):
                    p = 2 * g + i
                    qt.append(rotate(res[2 * i], res[2 * i + 1], q[:, 2 * p, :], q[:, 2 * p + 1, :], 1.0))
                if g == 0:
                    for i in range(2):
                        b, bf = B.take()
                        for n in range(4):
                            t = pe.do([bf, vts[i]], pe.e.transpose, b[:, n * P:(n + 1) * P],
                                      v_[:, i, n * P:(n + 1) * P], ident[:, :])
                        vtok = act.do([t], act.e.activation, vt_[:, :, i * P:(i + 1) * P],
                                      b[:, :].rearrange("p (n c) -> p n c", n=4), ACT.Copy)
                        B.give(b, vtok)
            state["h_readers"] = (pe, pe.count)
            hr = state["h_readers"]
            ht = []
            sbr = [[], []]
            ptr = [[], []]
            smr = [[], []]
            it = 0
            so = COLS["sinks"][0]
            for n in range(4):
                k0 = 128 * max(n - 1, 0)
                nk = 128 * (n + 1) - k0
                mo = 256 - nk
                for p in range(4):
                    z = it % 2
                    it += 1
                    if p % 2 == 0:
                        ob, obf = B.take()
                    sx, sc = Sb[z], sm[z]
                    sbk = [B.take() for j in range(4)]
                    for half in range(2):
                        for j in range(4):
                            b, bf = sbk[j]
                            t = pe.do([bf, qt[p], kt], pe.e.matmul, b[:, 0:nk],
                                      q[32 * j:32 * j + 32, 2 * p + half, n * P:(n + 1) * P],
                                      k_[32 * j:32 * j + 32, half, k0:k0 + nk], start=half == 0, stop=half == 1)
                            if half == 1:
                                sbk[j] = (b, t)
                    for j in range(4):
                        b, t = sbk[j]
                        a = dve.do([t, dm, sbr[z], smr[z]], dve.e.tensor_tensor_reduce, sx[:, j, 0:nk], b[:, 0:nk],
                                   mask[:, mo:256], 1.0, -3e38, ALU.add, ALU.max, sc[:, j:j + 1])
                        B.give(b, a)
                    sk = cols[:, so + 4 * p:so + 4 * p + 4]
                    a = dve.do([a], dve.e.tensor_tensor, sc[:, 4:8], sc[:, 0:4], sk, ALU.max)
                    a = dve.do([a], dve.e.tensor_scalar, sc[:, 8:12], sc[:, 4:8], -1.0, None, ALU.mult)
                    b2 = dve.do([a], dve.e.tensor_tensor, sc[:, 12:16], sc[:, 8:12], sk, ALU.add)
                    for j in range(4):
                        x = act.do([a], act.e.activation, sx[:, j, 0:nk], sx[:, j, 0:nk], ACT.Exp,
                                   bias=sc[:, 8 + j:9 + j], accum_out=sc[:, 16 + j:17 + j])
                    x = act.do([b2], act.e.activation, sc[:, 20:24], sc[:, 12:16], ACT.Exp)
                    a = dve.do([x], dve.e.tensor_tensor, sc[:, 24:28], sc[:, 16:20], sc[:, 20:24], ALU.add)
                    a = dve.do([a], dve.e.reciprocal, sc[:, 28:32], sc[:, 24:28])
                    for j in range(4):
                        a = dve.do([a], dve.e.tensor_scalar, sx[:, j, 0:nk], sx[:, j, 0:nk], sc[:, 28 + j:29 + j],
                                   None, ALU.mult)
                    smr[z] = [a]
                    pt = PT[z]
                    nb = nk // P
                    pts = []
                    for kb in range(nb):
                        b, bf = B.take()
                        for j in range(4):
                            t = pe.do([bf, a], pe.e.transpose, b[:, j * P:(j + 1) * P],
                                      sx[:, j, kb * P:(kb + 1) * P], ident[:, :])
                        eng = act if kb == 0 else dve
                        if kb == 0:
                            c = act.do([t, ptr[z]], act.e.activation, pt[:, 4 * kb:4 * kb + 4, :],
                                       b[:, :].rearrange("p (j c) -> p j c", j=4), ACT.Copy)
                        else:
                            c = dve.do([t, ptr[z]], dve.e.tensor_copy, pt[:, 4 * kb:4 * kb + 4, :],
                                       b[:, :].rearrange("p (j c) -> p j c", j=4))
                        B.give(b, c)
                        pts.append(c)
                    sbr[z] = [t]
                    for j in range(4):
                        o = (p % 2) * 256 + (j // 2) * P
                        r0 = 64 * (j % 2)
                        for kb in range(nb):
                            blk = k0 // P + kb
                            t = pe.do([pts, vtok, obf], pe.e.matmul, ob[r0:r0 + 64, o:o + P],
                                      vt_[:, blk, j * 64:(j + 1) * 64], pt[:, 4 * kb + j, :], start=kb == 0,
                                      stop=kb == nb - 1, skip_group_check=True)
                    ptr[z] = [t]
                    if p % 2 == 1:
                        c0 = 4 * (p // 2)
                        src = ob[:, :].rearrange("p (c t) -> p c t", c=4)
                        h = act.do([t, hr], act.e.activation, Hh[:, c0:c0 + 4, n * P:(n + 1) * P], src, ACT.Copy)
                        l = dve.do([t, h, hr], dve.e.tensor_tensor, Hl[:, c0:c0 + 4, n * P:(n + 1) * P], src,
                                   Hh[:, c0:c0 + 4, n * P:(n + 1) * P].bitcast(F32), ALU.subtract)
                        B.give(ob, l, h)
                        ht += [h, l]
            rhs = [(Hh[:, c, :], Hl[:, c, :], ht) for c in range(KD)]
            mt, held = [], []
            box = {}
            for g in range(2):
                def mid():
                    box["s"] = Stat()
                    count_squares(box["s"], held)
                res = gemm([P] * 4, rhs, mid if g == 1 else None)
                m, held = evac_m(res, 4 * g, None)
                mt += m
            state["h_readers"] = (pe, pe.count)
            count_squares(box["s"], held)
            state["arena_readers"] = [(pe, pe.count), (dve, dve.count), (act, act.count), (pool, pool.count)]
            state["xt"] = residual(mt, box["s"], "mix_post1")

        def second_mixer():
            af = state["arena_readers"]
            big = sub("b_big", [P, 26, S], 0)
            KCR, VCR, KS, VS, KW, VW, Q2, MQ, MK, MV, MO = 0, 1, 2, 3, 4, 5, 6, 10, 14, 18, 22
            o = 26 * 2048
            bias = sub("b_bias", [P, 8, S], o)
            o += 16384
            vtok = sub("b_vtok", [P, 2, 4, P], o)
            o += 4096
            mvt = sub("b_mvt", [P, 4, 4, P], o)
            blk = [at(f"b_blk{i}", [P, 16, 62], arena + o + 4096 * i) for i in range(2)]
            o += 8192
            pe2 = sub("b_pe", [P, 2, 2, 16], o)
            w2 = sub("b_w2", [P, 2, 64], o + 256)
            hid = sub("b_hid", [P, 2, 64], o + 768)
            kct = sub("b_kct", [P, 32], o + 1280)
            vct = sub("b_vct", [32, 2, 64], o + 1408)
            cb = sub("b_cb", [P, 4, 8, 31], o + 1920)
            gsig = sub("b_gsig", [P, 4, 24], o + 5888)
            assert o + 6272 <= 2 * FT * 2048, o
            w1 = [at(f"b_w1{i}", [P, 16, P], m_at + 8192 * i) for i in range(2)]
            Sb = at("b_Sb", [P, 8, S], m_at)
            xt = state["xt"]
            toks = [parts(c, "ln1", xt[c]) for c in range(KD)]
            sq = squares(xt)
            lots = [lot(f"s_b{i}") for i in range(6)]
            dist = at("b_dist", [P, S], arena + MO * 2048)
            cmpc = at("b_cmp", [P, 124], arena + (MO + 1) * 2048)
            sel = at("b_sel", [4, 4, P], arena + (MO + 2) * 2048)
            def const(name):
                c, w = CONST[name]
                return A["const"][:, c:c + w]
            d_dist = act.dma([af], lots[0], act.e.dma_start, dist[:, :], const("dist"))
            d_cmp = act.dma([af], lots[1], act.e.dma_start, cmpc[:, :], const("cmp"))
            d_pe = act.dma([af], lots[2], act.e.dma_start, pe2[:, :, :, :], A["cmp_pe"])
            d_w2 = act.dma([af], lots[3], act.e.dma_start, w2[:, :, :], A["cmp_w2"])
            bt = []
            for h in range(8):
                bt.append(pool.do([d_dist, af], pool.e.tensor_scalar, bias[:, h, :], dist[:, :], SLOPES[h], None,
                                  ALU.mult))
                bt.append(pool.do([d_cmp, af], pool.e.tensor_scalar, cb[:, :, h, :],
                                  cmpc[:, :].rearrange("p (b n) -> p b n", b=4), SLOPES[h], None, ALU.mult))
            biast = bt[-1]
            box = {}
            tk = {}

            def stats():
                s = Stat()
                for c in range(KD):
                    last = s.add(M[:, c, :], sq[c])
                state["m_readers"] = [last]
                box["rb"] = s.finish(state["rb_readers"])
                box["sq"] = last

            def scaled(i, b, t, scale, eng=None, extra=None):
                if scale == 1.0:
                    a = dve.do([t, box["rb"], af, extra], dve.e.tensor_tensor, big[:, i, :], b[:, :], RB[:, :],
                               ALU.mult)
                else:
                    a = dve.do([t, box["rb"], af, extra], dve.e.scalar_tensor_tensor, big[:, i, :], b[:, :], scale,
                               RB[:, :], ALU.mult, ALU.mult)
                B.give(b, a)
                tk[i] = a
                return a

            def to_tokens(src, dst, t, eng):
                b, bf = B.take()
                for n in range(4):
                    a = pe.do([bf, t], pe.e.transpose, b[:, n * P:(n + 1) * P], big[:, src, n * P:(n + 1) * P],
                              ident[:, :])
                a = act.do([a, af], act.e.activation, dst, b[:, :].rearrange("p (n c) -> p n c", n=4), ACT.Copy)
                B.give(b, a)
                return a

            res = gemm([P] * 4, hrhs(toks))
            stats()
            dw1 = [act.dma([box["sq"]], lots[4 + i], act.e.dma_start, w1[i][:, :, :],
                           A["cmp_w1"][i].rearrange("(c p) m -> p c m", p=P)) for i in range(2)]
            for i, (b, t) in enumerate(res):
                scaled((KCR, VCR, KS, VS)[i], b, t, 1.0)
            bl = []
            for i in range(2):
                for g in range(2):
                    for par in range(2):
                        src = big[64 * g:64 * g + 64, i, :]
                        a0 = src.rearrange("p (n c r) -> p n c r", c=8, r=2)[:, :, :, par]
                        for hf in range(2):
                            a = dve.do([tk[i], d_pe, af], dve.e.tensor_tensor,
                                       blk[i][64 * par:64 * par + 64, 8 * hf:8 * hf + 8, 31 * g:31 * g + 31],
                                       a0[:, hf:hf + 31, :].rearrange("p n c -> p c n"),
                                       pe2[64 * g:64 * g + 64, i, par, 8 * hf:8 * hf + 8].unsqueeze(2).to_broadcast( [64, 8, 31]),
                                       ALU.add)
                            bl.append(a)
            res = gemm([P] * 4, hrhs(toks))
            for i, (b, t) in enumerate(res):
                scaled((KW, VW, Q2, Q2 + 1)[i], b, t, 1.0 if i < 2 else 0.125)
            hb, hbf = B.take()
            for i in range(2):
                for c in range(16):
                    t = pe.do([hbf, dw1[i], bl], pe.e.matmul, hb[:, 64 * i:64 * i + 62], w1[i][:, c, :],
                              blk[i][:, c, :], start=c == 0, stop=c == 15, skip_group_check=True)
            hidt = t
            a = act.do([t, af], act.e.activation, hid[:, :, 0:62],
                       hb[:, 0:128].rearrange("p (i n) -> p i n", i=2)[:, :, 0:62], ACT.Gelu_apprx_tanh)
            B.give(hb, a)
            cbk, cbf = B.take()
            t = pe.do([cbf, a, d_w2], pe.e.matmul, cbk[0:64, 0:62], w2[:, 0, :], hid[:, 0, 0:62], start=True,
                      stop=True)
            k0 = dve.do([t, af], dve.e.tensor_copy, kct[0:64, 0:31], cbk[0:64, 0:31])
            k1 = dve.do([t, af], dve.e.tensor_copy, kct[64:128, 0:31], cbk[0:64, 31:62])
            B.give(cbk, k0, k1)
            cbk, cbf = B.take()
            for g in range(2):
                t = pe.do([cbf, a, d_w2], pe.e.matmul, cbk[0:31, 64 * g:64 * g + 64], hid[:, 1, 31 * g:31 * g + 31],
                          w2[:, 1, :], start=True, stop=True, skip_group_check=True)
            vc = dve.do([t, af], dve.e.tensor_copy, vct[0:31, :, :],
                        cbk[0:31, 0:128].rearrange("p (g d) -> p g d", g=2))
            B.give(cbk, vc)
            cmpt = [k0, k1, vc]
            vst = to_tokens(VS, vtok[:, 0, :, :], tk[VS], act)
            vwt = to_tokens(VW, vtok[:, 1, :, :], tk[VW], act)
            res = gemm([P, P, 88], hrhs(toks))
            scaled(Q2 + 2, res[0][0], res[0][1], 0.125)
            scaled(Q2 + 3, res[1][0], res[1][1], 0.125)
            gb, gt = res[2]
            zi, zif = T.take()
            zf, zff = T.take()
            za, zaf = T.take()
            a0 = dve.do([gt, box["rb"], zif], dve.e.tensor_tensor, zi[0:4, 2:TW], gb[0:4, :], RB[0:4, :], ALU.mult)
            a1 = dve.do([gt, zff], dve.e.tensor_tensor, zf[0:4, 2:TW], gb[32:36, :], RB[32:36, :], ALU.mult)
            a2 = dve.do([gt, zaf], dve.e.tensor_tensor, za[0:24, 2:TW], gb[64:88, :], RB[64:88, :], ALU.mult)
            B.give(gb, a2)
            b, bf = B.take()
            for n in range(4):
                t = pe.do([bf, a2], pe.e.transpose, b[:, 24 * n:24 * n + 24], za[0:24, 2 + n * P:2 + (n + 1) * P],
                          ident[0:24, 0:24])
            a = act.do([t, af], act.e.activation, gsig[:, :, :], b[:, 0:96].rearrange("p (n c) -> p n c", n=4),
                       ACT.Sigmoid)
            gc = dve.do([a], dve.e.tensor_scalar, gsig[:, 0, 0:24:3], gsig[:, 0, 0:24:3], col("rv", 0), None,
                        ALU.mult)
            gt_ = [a, gc]
            B.give(b, a)
            T.give(za, t)
            gbo = COLS["gbias"][0]
            lf, lff = T.take()
            l1, l1f = T.take()
            on, onf = T.take()
            R = lambda x: x[0:4, 2:TW]
            i1 = dve.do([a0], dve.e.tensor_scalar, R(zi), R(zi), cols[0:4, gbo:gbo + 1], None, ALU.add)
            f1 = dve.do([a1], dve.e.tensor_scalar, R(zf), R(zf), cols[0:4, gbo + 1:gbo + 2], None, ALU.add)
            a = act.do([f1, l1f], act.e.activation, R(l1), R(zf), ACT.Abs)
            a = act.do([a], act.e.activation, R(l1), R(l1), ACT.Exp, scale=-1.0)
            a = act.do([a], act.e.activation, R(l1), R(l1), ACT.Ln, bias=1.0)
            a = dve.do([a, lff], dve.e.scalar_tensor_tensor, R(lf), R(zf), 0.0, R(l1), ALU.min, ALU.subtract)
            c = dve.do([onf], dve.e.memset, R(on), 1.0)
            a = dve.do([a, c], dve.e.tensor_tensor_scan, R(zf), R(on), R(lf), 0.0, ALU.mult, ALU.add)
            T.give(on, a)
            g_ = dve.do([a, i1], dve.e.tensor_tensor, R(zi), R(zi), R(zf), ALU.subtract)
            m_ = dve.do([g_], dve.e.tensor_tensor_scan, R(lf), R(zi), R(zi), 0.0, ALU.max, ALU.max)
            nm = dve.do([m_], dve.e.scalar_tensor_tensor, R(l1), R(zf), -1.0, R(lf), ALU.mult, ALU.subtract)
            nM = dve.do([m_, nm], dve.e.tensor_scalar, R(lf), R(lf), -1.0, None, ALU.mult)
            T.give(zf, nm)
            b, bf = B.take()
            for n in range(4):
                t = pe.do([bf, g_], pe.e.transpose, b[:, 4 * n:4 * n + 4], zi[0:4, 2 + n * P:2 + (n + 1) * P],
                          ident[0:4, 0:4])
            for n in range(4):
                t = pe.do([nm], pe.e.transpose, b[:, 16 + 4 * n:20 + 4 * n], l1[0:4, 2 + n * P:2 + (n + 1) * P],
                          ident[0:4, 0:4])
            gcol = st[:, 32:48]
            emc = st[:, 48:64]
            gct = act.do([t], act.e.activation, gcol, b[:, 0:16], ACT.Copy)
            emt = act.do([t], act.e.activation, emc, b[:, 16:32], ACT.Exp)
            B.give(b, emt)
            T.give(zi, t)
            T.give(l1, t)
            for i, (b, t) in enumerate(gemm([P] * 4, hrhs(toks))):
                scaled(MQ + i, b, t, 128 ** -0.5)
            for i, (b, t) in enumerate(gemm([P] * 4, hrhs(toks))):
                scaled(MK + i, b, t, 1.0)
            for i, (b, t) in enumerate(gemm([P] * 4, hrhs(toks))):
                scaled(MV + i, b, t, 1.0)
            mvtt = [to_tokens(MV + h, mvt[:, h, :, :], [tk[MV + h], hidt], act) for h in range(4)]
            for i, (b, t) in enumerate(gemm([P] * 4, hrhs(toks))):
                a = scaled(MO + i, b, t, 1.0, extra=[biast])
                tk[MO + i] = act.do([a], act.e.activation, big[:, MO + i, :], big[:, MO + i, :], ACT.Sigmoid)
            state["rb_readers"] = [a]
            hr = (pe, pe.count)
            ht = {c: [] for c in range(8)}

            selb, selbf = T.take()
            seld = lot("s_sel")
            d_sel = act.dma([selbf], seld, act.e.dma_start, selb[0:4, 0:512],
                            A["const"][0:4, CONST["sel"][0]:CONST["sel"][0] + 512])
            z0 = None
            for h in range(4):
                b, bf = B.take()
                t = pe.do([bf, nM, d_sel], pe.e.matmul, b[:, :], selb[0:4, h * P:(h + 1) * P], R(lf), start=True,
                          stop=True)
                nb_, nbf = T.take()
                nbt = act.do([t, nbf], act.e.activation, nb_[:, 2:TW], b[:, :], ACT.Copy)
                B.give(b, nbt)
                num, numf = B.take()
                den, denf = B.take()
                for sbk in range(4):
                    n0 = sbk * P
                    w = S - n0
                    s_, sf = B.take()
                    t = pe.do([sf, tk[MK + h], tk[MQ + h]], pe.e.matmul, s_[:, 0:w], big[:, MK + h, n0:n0 + P],
                              big[:, MQ + h, n0:S], start=True, stop=True)
                    e_, ef = T.take()
                    a = dve.do([nbt, gct, ef], dve.e.tensor_scalar, e_[:, 2 + n0:TW], nb_[:, 2 + n0:TW],
                               gcol[:, 4 * sbk + h:4 * sbk + h + 1], 0.0, ALU.add, ALU.min)
                    a = act.do([a], act.e.activation, e_[:, 2 + n0:TW], e_[:, 2 + n0:TW], ACT.Exp)
                    a = dve.do([a, t], dve.e.tensor_tensor, e_[:, 2 + n0:TW], s_[:, 0:w], e_[:, 2 + n0:TW], ALU.mult)
                    B.give(s_, a)
                    a = pool.do([a], pool.e.affine_select, out=e_[:, 2 + n0:2 + n0 + P],
                                in_=e_[:, 2 + n0:2 + n0 + P], compare_op=ALU.is_ge, fill=0.0, base=0,
                                pattern=[[1, P]], channel_multiplier=-1)
                    t = pe.do([numf, a, mvtt[h]], pe.e.matmul, num[:, n0:S], mvt[:, h, sbk, :], e_[:, 2 + n0:TW],
                              start=sbk == 0, stop=sbk == 3, skip_group_check=True)
                    for tb in range(sbk, 4):
                        t = pe.do([denf, a], pe.e.matmul, den[:, tb:tb + 1], e_[:, 2 + tb * P:2 + (tb + 1) * P],
                                  ones[:, 0:1], start=sbk == 0 and tb == 0, stop=True, skip_group_check=True)
                    T.give(e_, t)
                T.give(nb_, a)
                nsb, nsf = T.take()
                a = dve.do([t, nsf], dve.e.tensor_copy, nsb[:, 2:TW], num[:, :])
                B.give(num, a)
                q_, qf = T.take()
                s2 = act.do([a, qf], act.e.activation, q_[:, 2:TW], nsb[:, 2:TW], ACT.Square)
                for tb in range(4):
                    t = pe.do([s2], pe.e.matmul, den[:, 8 + tb:9 + tb], q_[:, 2 + tb * P:2 + (tb + 1) * P],
                              ones[:, 0:1], start=False, stop=True, skip_group_check=True)
                T.give(q_, t)
                c0 = st[:, 64:68]
                c1 = st[:, 68:72]
                c2 = st[:, 72:76]
                em = emc.rearrange("p (n h) -> p n h", h=4)[:, :, h]
                z = act.do([t, z0], act.e.activation, c0, den[:, 0:4], ACT.Abs)
                z = dve.do([z, emt], dve.e.tensor_tensor, c0, c0, em, ALU.max)
                z = dve.do([z], dve.e.reciprocal, c1, c0)
                z = dve.do([z], dve.e.tensor_tensor, c0, c1, c1, ALU.mult)
                z = dve.do([z], dve.e.tensor_tensor, c0, den[:, 8:12], c0, ALU.mult)
                B.give(den, z)
                z = dve.do([z], dve.e.tensor_scalar, c0, c0, 1.0 / 128, EPS, ALU.mult, ALU.add)
                z = act.do([z], act.e.activation, c2, c0, ACT.Sqrt)
                z = dve.do([z], dve.e.reciprocal, c0, c2)
                z = dve.do([z], dve.e.tensor_tensor, c1, c1, c0, ALU.mult)
                z0 = z
                rb_, rbf = T.take()
                r = spread(c1, 4, [z], rb_[:, 2:TW], rbf)
                g = col("m_g", h)
                a = dve.do([a, r, s2], dve.e.scalar_tensor_tensor, nsb[:, 2:TW], nsb[:, 2:TW], g, rb_[:, 2:TW],
                           ALU.mult, ALU.mult)
                T.give(rb_, a)
                a = pool.do([a, tk[MO + h]], pool.e.tensor_tensor, nsb[:, 2:TW], nsb[:, 2:TW], big[:, MO + h, :],
                            ALU.mult)
                x = act.do([a, hr], act.e.activation, Hh[:, h, :], nsb[:, 2:TW], ACT.Copy)
                l = dve.do([a, x, hr], dve.e.tensor_tensor, Hl[:, h, :], nsb[:, 2:TW], Hh[:, h, :].bitcast(F32),
                           ALU.subtract)
                T.give(nsb, x, l)
                ht[h] = [x, l]
            T.give(selb, (pe, pe.count))
            T.give(lf, (pe, pe.count))

            msk = [hidt]
            mx, nmx, sums, fac = st[:, 80:88], st[:, 88:96], st[:, 96:104], st[:, 104:112]
            cmx, csum, cfac = st[:, 112:116], st[:, 116:120], st[:, 120:124]
            sb_free = [hidt]
            for tb in range(4):
                L = (tb + 1) * P
                ob, obf = B.take()
                outs = []
                for g in range(2):
                    qa = [big[64 * g:64 * g + 64, Q2 + r, tb * P:(tb + 1) * P] for r in range(4)]
                    b, bf = B.take()
                    for r in range(4):
                        t = pe.do([bf, tk[Q2], tk[Q2 + 1], tk[Q2 + 2], tk[Q2 + 3], cmpt], pe.e.matmul,
                                  b[:, 31 * r:31 * r + 31], qa[r], kct[64 * g:64 * g + 64, 0:31], start=True,
                                  stop=True, skip_group_check=True)
                    pc, pcf = T.take()
                    pv = pc[:, 2:126].rearrange("p (r n) -> p r n", r=4)
                    a = dve.do([t, biast, pcf], dve.e.tensor_tensor, pv,
                               b[:, 0:124].rearrange("p (r n) -> p r n", r=4), cb[:, tb, 4 * g:4 * g + 4, :],
                               ALU.add)
                    B.give(b, a)
                    a = dve.do([a], dve.e.tensor_reduce, cmx, pv, AX, ALU.max)
                    a = dve.do([a], dve.e.tensor_tensor, pv, pv, cmx.unsqueeze(2).to_broadcast([P, 4, 31]),
                               ALU.subtract)
                    a = act.do([a], act.e.activation, pc[:, 2:126], pc[:, 2:126], ACT.Exp)
                    a = dve.do([a], dve.e.tensor_reduce, csum, pv, AX, ALU.add)
                    a = dve.do([a], dve.e.reciprocal, cfac, csum)
                    a = dve.do([a, gt_], dve.e.tensor_tensor, cfac, cfac, gsig[:, tb, 12 * g:12 * g + 12:3],
                               ALU.mult)
                    pct = dve.do([a], dve.e.tensor_tensor, pv, pv, cfac.unsqueeze(2).to_broadcast([P, 4, 31]),
                                 ALU.mult)
                    ex = []
                    for r in range(4):
                        for w in range(2):
                            u = 2 * r + w
                            b, bf = B.take()
                            t = pe.do([bf, tk[KS], tk[KW]], pe.e.matmul, b[:, 0:L], qa[r],
                                      big[64 * g:64 * g + 64, (KS, KW)[w], 0:L], start=True, stop=True)
                            a = dve.do([t, biast, sb_free], dve.e.tensor_tensor_reduce, Sb[:, u, 0:L], b[:, 0:L],
                                       bias[:, 4 * g + r, S - L:S], 1.0, -3e38, ALU.add, ALU.max, mx[:, u:u + 1])
                            B.give(b, a)
                            a = dve.do([a], dve.e.tensor_scalar, nmx[:, u:u + 1], mx[:, u:u + 1], -1.0, None,
                                       ALU.mult)
                            x = act.do([a], act.e.activation, Sb[:, u, 0:L], Sb[:, u, 0:L], ACT.Exp,
                                       bias=nmx[:, u:u + 1], accum_out=sums[:, u:u + 1])
                    a = dve.do([x], dve.e.reciprocal, fac, sums)
                    gv = gsig[:, tb, 12 * g:12 * g + 12].rearrange("p (r c) -> p r c", c=3)[:, :, 1:3]
                    a = dve.do([a, gt_], dve.e.tensor_tensor, fac.rearrange("p (r c) -> p r c", c=2),
                               fac.rearrange("p (r c) -> p r c", c=2), gv, ALU.mult)
                    sc = []
                    for u in range(8):
                        eng = dve
                        sc.append(eng.do([a], eng.e.tensor_scalar, Sb[:, u, 0:L], Sb[:, u, 0:L], fac[:, u:u + 1],
                                         None, ALU.mult))
                    b, bf = B.take()
                    for r in range(4):
                        t = pe.do([bf, pct], pe.e.transpose, b[0:31, r * P:(r + 1) * P],
                                  pc[:, 2 + 31 * r:2 + 31 * r + 31], ident[:, :])
                    T.give(pc, t)
                    ct, ctf = T.take()
                    ctt = act.do([t, ctf], act.e.activation, ct[0:31, 0:512], b[0:31, :], ACT.Copy)
                    B.give(b, ctt)
                    sbt = []
                    for r in range(4):
                        oc = ob[64 * g:64 * g + 64, r * P:(r + 1) * P]
                        t = pe.do([obf, ctt, cmpt], pe.e.matmul, oc, vct[0:31, g, :], ct[0:31, r * P:(r + 1) * P],
                                  start=True, stop=False, skip_group_check=True)
                        for w in range(2):
                            u = 2 * r + w
                            b, bf = B.take()
                            for kb in range(tb + 1):
                                t = pe.do([bf, sc[u]], pe.e.transpose, b[:, kb * P:(kb + 1) * P],
                                          Sb[:, u, kb * P:(kb + 1) * P], ident[:, :])
                            sbt.append(t)
                            p_, pf = T.take()
                            if w == 0:
                                c = act.do([t, pf], act.e.activation, p_[:, 0:L], b[:, 0:L], ACT.Copy)
                            else:
                                c = dve.do([t, pf], dve.e.tensor_copy, p_[:, 0:L], b[:, 0:L])
                            B.give(b, c)
                            for kb in range(tb + 1):
                                t = pe.do([c, vst, vwt], pe.e.matmul, oc, vtok[:, w, kb, 64 * g:64 * g + 64],
                                          p_[:, kb * P:(kb + 1) * P], start=False, stop=w == 1 and kb == tb,
                                          skip_group_check=True)
                            T.give(p_, t)
                    T.give(ct, t)
                    sb_free = sbt
                    outs.append(t)
                src = ob[:, :].rearrange("p (r t) -> p r t", r=4)
                x = act.do([outs, hr], act.e.activation, Hh[:, 4:8, tb * P:(tb + 1) * P], src, ACT.Copy)
                l = dve.do([outs, x, hr], dve.e.tensor_tensor, Hl[:, 4:8, tb * P:(tb + 1) * P], src,
                           Hh[:, 4:8, tb * P:(tb + 1) * P].bitcast(F32), ALU.subtract)
                B.give(ob, l, x)
                for c in range(4, 8):
                    ht[c] += [x, l]
            T_pads()
            rhs = [(Hh[:, c, :], Hl[:, c, :], ht[c]) for c in range(KD)]
            nx = []
            for g in range(2):
                for i, (b, t) in enumerate(gemm([P] * 4, rhs)):
                    c = 4 * g + i
                    x = dve.do([t, sq[c], toks[c]], dve.e.tensor_tensor, X[:, c, :], b[:, :], X[:, c, :], ALU.add)
                    B.give(b, x)
                    nx.append(x)
            state["xt"] = nx
            state["h_readers"] = (pe, pe.count)
            state["m_readers"] = sb_free
            state["arena_readers"] = [(pe, pe.count), (dve, dve.count), (act, act.count), (pool, pool.count)]

        def T_pads():
            new = []
            for t, free in T.free:
                a = pool.do([free], pool.e.memset, t[:, 0:2], 0.0)
                new.append((t, [a]))
            T.free = new

        def ple_and_norm():
            af = state["arena_readers"]
            pr = sub("p_raw", [P, 2, S], 0)
            ph = sub("p_hi", [P, 2, S], 4096, F32R)
            pl = sub("p_lo", [P, 2, S], 8192, F32R)
            Y = sub("Y", [P, KD, S], 16384)
            lp = lot("s_p")
            d = act.dma([af], lp, act.e.dma_start, pr[:, :, :], A["pT"].rearrange("(c p) t -> p c t", p=P))
            xt = state["xt"]
            toks = [parts(c, "ple_g", xt[c]) for c in range(KD)]
            sq = squares(xt)
            a = act.do([d, af], act.e.activation, ph[:, :, :], pr[:, :, :], ACT.Copy)
            b = dve.do([a, af], dve.e.tensor_tensor, pl[:, :, :], pr[:, :, :], ph[:, :, :].bitcast(F32),
                       ALU.subtract)
            prhs = [(ph[:, k, :], pl[:, k, :], [a, b]) for k in range(2)]
            nx, held = [], []
            fin = None
            for g in range(2):
                res = gemm([P] * 4, hrhs(toks))
                if g == 0:
                    s = Stat()
                    for c in range(KD):
                        last = s.add(M[:, c, :], sq[c])
                    state["m_readers"] = [last]
                    rb = s.finish(state["rb_readers"])
                us = []
                for i, (b_, t) in enumerate(res):
                    u, uf = T.take()
                    x = dve.do([t, rb, uf], dve.e.tensor_tensor, u[:, 2:TW], b_[:, :], RB[:, :], ALU.mult)
                    B.give(b_, x)
                    x2 = act.do([x], act.e.activation, u[:, 2:TW], u[:, 2:TW], ACT.Sigmoid)
                    us.append((u, x2))
                state["rb_readers"] = [x]
                res = gemm([P] * 4, prhs)
                for i, (b_, t) in enumerate(res):
                    c = 4 * g + i
                    u, ut = us[i]
                    x = dve.do([t, ut], dve.e.tensor_tensor, u[:, 2:TW], b_[:, :], u[:, 2:TW], ALU.mult)
                    B.give(b_, x)
                    x = pool.do([x, sq[c], toks[c]], pool.e.tensor_tensor, X[:, c, :], X[:, c, :], u[:, 2:TW],
                                ALU.add)
                    T.give(u, x)
                    nx.append(x)
                    q, qf = T.take()
                    s_ = square_into(q[:, 2:TW], X[:, c, :], x, qf)
                    held.append((q, s_))
                if g == 0:
                    fin = Stat()
                count_squares(fin, held)
                held = []
            r = fin.finish(state["rb_readers"])
            lo = [lot("s_out0"), lot("s_out1")]
            ends = []
            o3 = out.rearrange("(c p) t -> p c t", p=P)
            for c in range(KD):
                g = col("final_g", c)
                a = dve.do([r, nx[c], af], dve.e.scalar_tensor_tensor, Y[:, c, :], X[:, c, :], g, RB[:, :], ALU.mult,
                           ALU.mult)
                ends.append(a)
                if c % 2 == 1:
                    l = Lot(ctx.enter_context(nc.semaphore(f"s_o{c}")))
                    dd = sp.dma([a], l, sp.e.dma_start, o3[:, c - 1:c + 1, :], Y[:, c - 1:c + 1, :])
                    state.setdefault("outs", []).append(dd)

        steps = [
            lambda: pool_mixer(),
            lambda: ffn(0, 11, "ffn_pre0", None, True, ACT.Gelu_apprx_tanh, FT, "ffn_post0"),
            lambda: window_mixer(),
            lambda: ffn(1, 11, "ffn_pre1", None, True, ACT.Gelu_apprx_tanh, FT, "ffn_post1"),
            lambda: second_mixer(),
            lambda: ffn(2, 8, "ln2", None, False, ACT.Silu, FT2, None),
            lambda: ple_and_norm(),
        ]
        n = len(steps) if stop is None else stop
        for s in steps[:n]:
            s()
        if stop is not None:
            o3 = out.rearrange("(c p) t -> p c t", p=P)
            l = lot("s_dbg")
            state["outs"] = [sp.dma([state["xt"]], l, sp.e.dma_start, o3, X[:, :, :])]
        sp.wait(state["outs"])

        with nc.Block() as block:
            @block.sync
            def _(e):
                sp.run()

            @block.tensor
            def _(e):
                pe.run()

            @block.vector
            def _(e):
                dve.run()

            @block.scalar
            def _(e):
                act.run()

            @block.gpsimd
            def _(e):
                pool.run()


def constants():
    c = np.zeros((P, NCONST), np.float32)
    p = np.arange(P)[:, None]
    c[:, 0:P] = np.eye(P)
    o = CONST["dist"][0]
    j = np.arange(S)[None, :]
    d = j - 384 - p
    c[:, o:o + S] = np.where(d <= 0, d, NEG)
    o = CONST["swa"][0]
    j = np.arange(256)[None, :]
    rel = 128 + p - j
    c[:, o:o + 256] = np.where((rel >= 0) & (rel < 128), 0.0, NEG)
    o = CONST["cmp"][0]
    for tb in range(4):
        d = (16 * np.arange(31)[None, :] + 31) - (tb * P + p)
        c[:, o + 31 * tb:o + 31 * tb + 31] = np.where(d <= 0, d, NEG)
    o = CONST["sel"][0]
    for h in range(4):
        c[h, o + h * P:o + (h + 1) * P] = 1.0
    o = CONST["invc"][0]
    for gi in range(4):
        w = 2 << gi
        c[:, o + 16 * gi:o + 16 * gi + 16] = 1.0 / np.minimum(np.arange(1, 17), w).astype(np.float32)
    return c


def tiles_of(v):
    return np.ascontiguousarray(v.reshape(-1, P).T)


def layout(i):
    f = np.float32
    i = {k: np.asarray(v) for k, v in i.items()}
    A = {}
    A["xT"] = np.ascontiguousarray(i["x"][0].T)
    A["pT"] = np.ascontiguousarray(i["p_2"][0, 0].T)
    A["pos"] = np.ascontiguousarray(np.broadcast_to(i["positions"][0][None, :], (P, S)))
    cols = np.zeros((P, NCOLS), f)

    def put(name, v):
        o, w = COLS[name]
        assert v.shape[1] == w, (name, v.shape)
        cols[:v.shape[0], o:o + w] = v

    for l in range(2):
        put(f"mix_pre{l}", tiles_of(i["mix_pre_g"][l]))
        put(f"mix_post{l}", tiles_of(i["mix_post_g"][l]))
        put(f"ffn_pre{l}", tiles_of(i["ffn_pre_g"][l]))
        put(f"ffn_post{l}", tiles_of(i["ffn_post_g"][l]))
        put(f"cw{l}", np.concatenate([tiles_of(i["ffn_conv_w"][l, k]) for k in range(3)], axis=1))
        put(f"cb{l}", tiles_of(i["ffn_conv_b"][l]))
    put("pool_scale", tiles_of(i["pool_scale"][0]))
    put("kv_g", tiles_of(i["kv_norm_g"]))
    put("ln1", tiles_of(i["ln1_g_2"][0]))
    put("ln2", tiles_of(i["ln2_g_2"][0]))
    put("ple_g", tiles_of(i["ple_norm_g_2"][0]))
    put("final_g", tiles_of(i["final_g_2"]))
    put("m_g", tiles_of(i["mlstm_norm_g_2"][0]))
    put("cw2", np.concatenate([tiles_of(i["conv_w_2"][0, k]) for k in range(3)], axis=1))
    put("cb2", tiles_of(i["conv_b_2"][0]))
    order = [4 * j + p for p in range(4) for j in range(4)]
    put("sinks", np.broadcast_to(i["sinks"][0][order][None, :], (P, 16)))
    put("gbias", np.ascontiguousarray(i["mlstm_gate_bias_2"][0].reshape(2, 4).T))
    fr = (1.0 / (10000.0 ** (np.arange(0, 64, 2, dtype=f) / 64))).astype(f)
    put("invf", np.tile(fr, 4)[:, None])
    put("rv", (np.arange(P) >= 31).astype(f)[:, None])
    A["cols"] = cols
    A["const"] = constants()
    A["pool_w"] = np.ascontiguousarray(i["pool_w"][0])
    d32 = np.arange(32)
    kcols = [np.concatenate([j * 64 + half * 32 + d32 for j in range(4)]) for half in range(2)]
    A["w_kv"] = np.ascontiguousarray(i["w_kv"][:, np.concatenate(kcols + [np.arange(256, 512)])])
    qcols = [np.concatenate([(4 * j + p) * 64 + half * 32 + d32 for j in range(4)])
             for p in range(4) for half in range(2)]
    A["w_q"] = np.ascontiguousarray(i["w_q"][0][:, np.concatenate(qcols)])
    orow = [np.concatenate([(4 * j + p) * 64 + np.arange(64) for j in (2 * jj, 2 * jj + 1)])
            for p in range(4) for jj in range(2)]
    A["w_o"] = np.ascontiguousarray(i["w_o"][0][np.concatenate(orow)])
    t = np.arange(P)
    for l in range(2):
        cc = [np.concatenate([(2 * g) * P + t, (2 * g + 1) * P + t, (FT + 2 * g) * P + t, (FT + 2 * g + 1) * P + t])
              for g in range(11)]
        A[f"w_in{l}"] = np.ascontiguousarray(i["ffn_w_in"][l][:, np.concatenate(cc)])
        A[f"w_out{l}"] = np.ascontiguousarray(i["ffn_w_out"][l])
    w = i["w_in_2"][0]
    sizes = [512] * 4 + [4, 4, 512] + [128] * 6 + [24]
    offs = np.concatenate([[0], np.cumsum(sizes)])
    sec = [w[:, offs[k]:offs[k + 1]] for k in range(len(sizes))]
    mq, mk, mv, mo, mi, mf, aq, akc, avc, aks, avs, akw, avw, ag = sec
    q2 = [np.concatenate([aq[:, r * 64:(r + 1) * 64], aq[:, (4 + r) * 64:(5 + r) * 64]], axis=1) for r in range(4)]
    z = np.zeros((D, 28), f)
    A["w_in_2"] = np.ascontiguousarray(np.concatenate(
        [akc, avc, aks, avs, akw, avw] + q2 + [mi, z, mf, z, ag, mq, mk, mv, mo], axis=1))
    wo = i["w_out_2"][0]
    rows = [np.arange(512)] + [np.concatenate([512 + r * 64 + np.arange(64), 512 + (4 + r) * 64 + np.arange(64)])
                               for r in range(4)]
    A["w_out_2"] = np.ascontiguousarray(wo[np.concatenate(rows)])
    cc = [np.concatenate([(2 * g) * P + t, (2 * g + 1) * P + t, (FT2 + 2 * g) * P + t, (FT2 + 2 * g + 1) * P + t])
          for g in range(8)]
    A["w_up_2"] = np.ascontiguousarray(i["w_up_2"][0][:, np.concatenate(cc)])
    A["w_down_2"] = np.ascontiguousarray(i["w_down_2"][0])
    A["w_pg"] = np.ascontiguousarray(i["w_ple_gate_2"][0])
    A["w_pp"] = np.ascontiguousarray(i["w_ple_proj_2"][0])
    A["cmp_w1"] = np.ascontiguousarray(np.stack([i["cmp_k_w1_2"][0], i["cmp_v_w1_2"][0]]))
    A["cmp_w2"] = np.ascontiguousarray(np.stack([i["cmp_k_w2_2"][0], i["cmp_v_w2_2"][0]], axis=1))
    pes = []
    for n in ("cmp_pos_k_2", "cmp_pos_v_2"):
        v = i[n][0].reshape(16, 2, 64).transpose(2, 1, 0)
        pes.append(np.concatenate([v, v], axis=0))
    A["cmp_pe"] = np.ascontiguousarray(np.stack(pes, axis=1))
    return A


def kernel(**inputs):
    import concourse.bacc as bacc
    from concourse.bass_utils import run_bass_kernel_spmd

    arrays = layout(inputs)
    nc = bacc.Bacc("TRN2", target_bir_lowering=False, num_devices=1)
    aps = {}
    feed = {}
    for name, a in arrays.items():
        feed[f"in_{name}"] = a
        aps[name] = nc.dram_tensor(f"in_{name}", a.shape, mybir.dt.from_np(a.dtype), kind="ExternalInput").ap()
    out = nc.dram_tensor("out_0", (D, S), F32, kind="ExternalOutput").ap()
    build(nc, aps, out)
    r = run_bass_kernel_spmd(nc, [feed], core_ids=[0])
    return np.ascontiguousarray(r.results[0]["out_0"].T)[None]
```

```python
import math
from contextlib import ExitStack

import numpy as np

import concourse.bass as bass
from concourse import mybir

ALU = mybir.AluOpType
ACT = mybir.ActivationFunctionType
F32 = mybir.dt.float32
F32R = mybir.dt.float32r
I32 = mybir.dt.int32
AX = mybir.AxisListType.X

P = 128
S = 512
D = 1024
KD = 8
FT = 22
FT2 = 16
NEG = -1e30
EPS = 1e-6
SLOPES = [2.0 ** (-(h + 1)) for h in range(8)]
NPIECE = 512
TW = S + 2
MAGIC = 12582912.0
PI_HI, PI_MID, PI_LO = 6.28125, 0.0019350051879882812, 3.0197183517896e-07

COLS = {}
_at = 0
for _n, _w in (("mix_pre0", 8), ("mix_pre1", 8), ("mix_post0", 8), ("mix_post1", 8), ("pool_scale", 8),
               ("kv_g", 8), ("ffn_pre0", 8), ("ffn_pre1", 8), ("ffn_post0", 8), ("ffn_post1", 8),
               ("ln1", 8), ("ln2", 8), ("ple_g", 8), ("final_g", 8), ("m_g", 4),
               ("cw0", 132), ("cb0", 44), ("cw1", 132), ("cb1", 44), ("cw2", 48), ("cb2", 16),
               ("sinks", 16), ("gbias", 2), ("invf", 1), ("rv", 1)):
    COLS[_n] = (_at, _w)
    _at += _w
NCOLS = _at

CONST = {}
_at = 0
for _n, _w in (("ident", 128), ("dist", 512), ("swa", 256), ("cmp", 124), ("sel", 512), ("invc", 64)):
    CONST[_n] = (_at, _w)
    _at += _w
NCONST = _at


class Engine:

    def __init__(self, e, sem):
        self.e, self.sem, self.count, self.queue, self.seen = e, sem, 0, [], {}

    def wait(self, *tokens):
        for t in flat(tokens):
            who, value = t
            if self.seen.get(who, 0) < value:
                self.seen[who] = value
                self.queue.append((self.e.wait_ge, (who.sem, value), {}, None, 0))

    def do(self, tokens, op, *args, **named):
        self.wait(tokens)
        self.count += 1
        self.queue.append((op, args, named, self.sem, 1))
        return (self, self.count)

    def quiet(self, tokens, op, *args, **named):
        self.wait(tokens)
        self.queue.append((op, args, named, None, 0))

    def dma(self, tokens, lot, op, *args, **named):
        self.wait(tokens)
        lot.count += 16
        self.queue.append((op, args, named, lot.sem, 16))
        return (lot, lot.count)

    def run(self):
        for op, args, named, sem, by in self.queue:
            done = op(*args, **named)
            if sem is not None:
                done.then_inc(sem, by)


class Lot:

    def __init__(self, sem):
        self.sem, self.count = sem, 0


def flat(tokens):
    for t in tokens:
        if isinstance(t, list):
            yield from flat(t)
        elif t is not None:
            yield t


class Slots:

    def __init__(self, places):
        self.free = [(p, []) for p in places]

    def take(self):
        return self.free.pop(0)

    def give(self, place, *tokens):
        self.free.append((place, list(flat(tokens))))


def build(nc, A, out, stop=None):
    ctx = ExitStack()
    with ctx:
        base = [(nc.sbuf_base + 63) // 64 * 64]
        limit = nc.sbuf_base + 212000

        def place(nbytes):
            at = base[0]
            base[0] += (nbytes + 63) // 64 * 64
            assert base[0] <= limit, (base[0], limit)
            return at

        def at(name, shape, off, dt=F32):
            return nc.alloc_sbuf_tensor_at(name, shape, dt, offset=off)

        def sb(name, shape, dt=F32):
            n = 4
            for x in shape[1:]:
                n *= x
            return at(name, shape, place(n), dt)

        pe, act, dve, pool, sp = (
            Engine(e, ctx.enter_context(nc.semaphore(n)))
            for e, n in ((nc.tensor, "s_pe"), (nc.scalar, "s_act"), (nc.vector, "s_dve"), (nc.gpsimd, "s_pool"),
                         (nc.sync, "s_sp")))

        def lot(name):
            return Lot(ctx.enter_context(nc.semaphore(name)))

        X = sb("X", [P, KD, S])
        m_at = place(KD * S * 4)
        M = at("M", [P, KD, S], m_at)
        Hh = sb("Hh", [P, KD, S], F32R)
        Hl = sb("Hl", [P, KD, S], F32R)
        arena = place(2 * FT * S * 4)
        NRAW, NSPL, NT = 5, 4, 8
        raws = [sb(f"raw{i}", [P, NPIECE]) for i in range(NRAW)]
        raw_lots = [lot(f"s_raw{i}") for i in range(NRAW)]
        spls = [(sb(f"wh{i}", [P, NPIECE], F32R), sb(f"wl{i}", [P, NPIECE], F32R)) for i in range(NSPL)]
        ts = [sb(f"t{i}", [P, TW]) for i in range(NT)]
        RB = sb("RB", [P, S])
        DG = sb("DG", [P, 4, P])
        cols = sb("cols", [P, NCOLS])
        ident = sb("ident", [P, P])
        ones = sb("ones", [P, P])
        st = sb("st", [P, 160])
        rows = sb("rows", [4, 2, S])
        banks = [ctx.enter_context(nc.psum_tensor(f"ps{i}", [P, S], F32)) for i in range(8)]

        raw_slots = Slots(list(range(NRAW)))
        spl_slots = Slots(list(range(NSPL)))
        T = Slots(ts)
        B = Slots(banks)

        def col(name, i):
            o = COLS[name][0] + i
            return cols[:, o:o + 1]

        l_c, l_k = lot("s_cols"), lot("s_ident")
        x_loaded = []
        for c in range(KD):
            x_loaded.append(sp.dma([], lot(f"s_x{c}"), sp.e.dma_start, X[:, c, :], A["xT"][c * P:(c + 1) * P, :]))
        d_c = act.dma([], l_c, act.e.dma_start, cols[:, :], A["cols"])
        d_k = act.dma([], l_k, act.e.dma_start, ident[:, :], A["const"][:, 0:P])
        ones_t = pool.do([], pool.e.memset, ones[:, :], 1.0)
        pw_t = pool.do([], pool.e.memset, st[:, 128:144], -0.5)
        pads = [pool.do([], pool.e.memset, t[:, 0:2], 0.0) for t in ts]
        pads_t = pads[-1]
        for e in (act, dve, pool, pe):
            e.wait(d_c)
        for e in (dve, pe):
            e.wait(d_k, ones_t, pads_t)
        act.wait(pads_t)

        plan = []

        def pieces_of(w, k, groups):
            at_ = 0
            for g in groups:
                for r in range(k):
                    plan.append((w[r * P:(r + 1) * P, at_:at_ + g], g))
                at_ += g

        for gi in range(4):
            plan.append((A["pool_w"][gi].rearrange("(k p) c -> p k c", p=P), 512))
        for layer in range(2):
            if layer == 1:
                pieces_of(A["w_kv"], 8, [512])
                pieces_of(A["w_q"], 8, [512, 512])
                pieces_of(A["w_o"], 8, [512, 512])
            pieces_of(A[f"w_in{layer}"], 8, [512] * 11)
            pieces_of(A[f"w_out{layer}"], FT, [512, 512])
        pieces_of(A["w_in_2"], 8, [512, 512, 344] + [512] * 4)
        pieces_of(A["w_out_2"], 8, [512, 512])
        pieces_of(A["w_up_2"], 8, [512] * 8)
        pieces_of(A["w_down_2"], FT2, [512, 512])
        for g in range(2):
            for k in range(8):
                plan.append((A["w_pg"][k * P:(k + 1) * P, g * 512:g * 512 + 512], 512))
            for k in range(2):
                plan.append((A["w_pp"][k * P:(k + 1) * P, g * 512:g * 512 + 512], 512))

        class W:
            loaded = 0
            split = 0
            used = 0
            raw = {}
            ready = {}

        def load_piece():
            n = W.loaded
            if n >= len(plan):
                return
            r, free = raw_slots.take()
            src, width = plan[n]
            dst = raws[r][:, 0:width]
            if len(src.shape) == 3:
                dst = dst.rearrange("p (k c) -> p k c", k=src.shape[1])
            t = sp.dma([free], raw_lots[r], sp.e.dma_start, dst, src)
            W.raw[n] = (r, t)
            W.loaded += 1

        def split_piece():
            n = W.split
            if n >= len(plan) or n - W.used >= NSPL:
                return
            while W.loaded <= n:
                load_piece()
            r, landed = W.raw.pop(n)
            width = plan[n][1]
            s, free = spl_slots.take()
            wh, wl = spls[s]
            raw = raws[r][:, 0:width]
            th = act.do([landed, free], act.e.activation, wh[:, 0:width], raw, ACT.Copy)
            tl = dve.do([landed, free, th], dve.e.tensor_tensor, wl[:, 0:width], raw, wh[:, 0:width].bitcast(F32),
                        ALU.subtract)
            raw_slots.give(r, th, tl)
            W.ready[n] = (s, th, tl)
            W.split += 1
            load_piece()

        def next_piece():
            while W.split <= W.used + (NSPL - 1) and W.split < len(plan) and W.split - W.used < NSPL:
                split_piece()
            n = W.used
            s, th, tl = W.ready.pop(n)
            return s, [th, tl]

        def done_piece(s, t):
            spl_slots.give(s, t)
            W.used += 1

        for _ in range(NRAW):
            load_piece()

        def mm3(bank_ap, wh, wl, xh, xl, first, last):
            pe.quiet([], pe.e.matmul, bank_ap, wh, xh, start=first, stop=False)
            pe.quiet([], pe.e.matmul, bank_ap, wh, xl, start=False, stop=False)
            return pe.do([], pe.e.matmul, bank_ap, wl, xh, start=False, stop=last)

        class Background:

            def __init__(self):
                self.tasks = []

            def add(self, task):
                self.tasks.append(task)
                self.advance(task)

            def advance(self, task):
                if next(task, "over") == "over":
                    self.tasks.remove(task)

            def step(self):
                for task in list(self.tasks):
                    self.advance(task)

            def until(self, ready):
                for _ in range(4000):
                    if ready():
                        return
                    self.step()
                assert ready()

            def finish(self):
                self.until(lambda: not self.tasks)

        bg = Background()

        def gemm(widths, rhs, nk=KD, mid=None, midk=3, pace=1):
            bg.until(lambda: len(B.free) >= len(widths))
            res = []
            for w in widths:
                b, free = B.take()
                res.append([b, free, None])
            for k in range(nk):
                xh, xl, t = rhs(k)
                s, ready = next_piece()
                wh, wl = spls[s]
                pe.wait(ready, t)
                o = 0
                for i, w in enumerate(widths):
                    b, free, _ = res[i]
                    if k == 0:
                        pe.wait(free)
                    last = mm3(b[0:w, :], wh[:, o:o + w], wl[:, o:o + w], xh, xl, k == 0, k == nk - 1)
                    res[i][2] = last
                    o += w
                done_piece(s, last)
                if mid is not None and k == midk:
                    mid()
                for _ in range(pace):
                    bg.step()
            return [(b, t) for b, _, t in res]

        class Stat:

            def __init__(self):
                bg.until(lambda: len(B.free) >= 2)
                self.bank, self.free = B.take()
                self.n = 0
                self.last = None

            def add(self, sq, tok):
                for b in range(4):
                    first = self.n == 0 and b == 0
                    self.last = pe.do([tok, self.free if first else None], pe.e.matmul, self.bank[:, b:b + 1],
                                      sq[:, b * P:(b + 1) * P], ones[:, 0:1], start=first, stop=True,
                                      skip_group_check=True)
                self.n += 1
                return self.last

            def finish(self):
                v, r = st[:, 0:4], st[:, 4:8]
                a = dve.do([self.last, state["st_readers"]], dve.e.tensor_scalar, v, self.bank[:, 0:4], 1.0 / D, EPS,
                           ALU.mult, ALU.add)
                B.give(self.bank, a)
                a = rsqrt(r, v, st[:, 128:132], a)
                b, t = spread(r, [a])
                state["st_readers"] = [t]
                return b, t

        def rsqrt(dst, src, power, tok):
            return pool.do([tok], pool.e.tensor_tensor, dst, src, power, ALU.pow)

        def spread(v, toks, place=None):
            a = dve.do([toks, state["dg_readers"]], dve.e.tensor_tensor, DG[:, :, :],
                       ident[:, :].unsqueeze(1).to_broadcast([P, 4, P]), v.unsqueeze(2).to_broadcast([P, 4, P]),
                       ALU.mult)
            b, bf = B.take() if place is None else place
            a = pe.do([a, bf], pe.e.matmul, b[:, :], ones[:, :], DG[:, :, :].rearrange("p a b -> p (a b)"),
                      start=True, stop=True)
            state["dg_readers"] = [a]
            return b, a

        state = {"rb_readers": [], "h_readers": None, "m_readers": [], "st_readers": [], "dg_readers": []}

        def to_rb(bank, t):
            a = act.do([t, state["rb_readers"]], act.e.activation, RB[:, :], bank[:, :], ACT.Copy)
            B.give(bank, a)
            return a

        def square_into(dst, src, *toks):
            return act.do([*toks], act.e.activation, dst, src, ACT.Square)

        def parts(c, gname, xt):
            g = col(gname, c)
            th = act.do([xt, state["h_readers"]], act.e.activation, Hh[:, c, :], X[:, c, :], ACT.Copy, scale=g)
            tl = dve.do([xt, th, state["h_readers"]], dve.e.scalar_tensor_tensor, Hl[:, c, :], X[:, c, :], g,
                        Hh[:, c, :].bitcast(F32), ALU.mult, ALU.subtract)
            return [th, tl]

        class Input:

            def __init__(self, gname, squares=True):
                self.parts, self.sq, self.x = [], [], []
                make = state["x"]
                for c in range(KD + 1):
                    if c < KD:
                        self.x.append(make(c))
                    if c > 0:
                        self.parts.append(parts(c - 1, gname, self.x[c - 1]))
                        if squares:
                            self.sq.append(square_into(M[:, c - 1, :], X[:, c - 1, :], self.x[c - 1],
                                                       state["m_readers"]))
                state["x"] = lambda c: self.x[c]

            def rhs(self, k):
                return Hh[:, k, :], Hl[:, k, :], self.parts[k]

            def rms(self):
                s = Stat()
                for c in range(KD):
                    last = s.add(M[:, c, :], self.sq[c])
                state["m_readers"] = [last]
                self.counted = last
                self.rb = to_rb(*s.finish())
                return self.rb

        def residual(mt, stat, gname):
            bank, r = stat.finish()

            def make(c):
                g = col(gname, c)
                a = dve.do([r, mt[c]], dve.e.scalar_tensor_tensor, M[:, c, :], M[:, c, :], g, bank[:, :], ALU.mult,
                           ALU.mult)
                if c == KD - 1:
                    B.give(bank, a)
                x = pool.do([a, state["x_readers"]], pool.e.tensor_tensor, X[:, c, :], X[:, c, :], M[:, c, :],
                            ALU.add)
                state["m_readers"] = [x]
                return x

            state["x"] = make

        state["x"] = lambda c: x_loaded[c]
        state["x_readers"] = []

        def evac_m(group, c0, scale=None):
            toks, held = [], []
            for i, (b, t) in enumerate(group):
                c = c0 + i
                g = 1.0 if scale is None else col(scale, c)
                if i % 2 == 0:
                    a = dve.do([t, state["m_readers"]], dve.e.tensor_scalar, M[:, c, :], b[:, :], g, None, ALU.mult)
                else:
                    a = act.do([t, state["m_readers"]], act.e.activation, M[:, c, :], b[:, :], ACT.Copy, scale=g)
                B.give(b, a)
                toks.append(a)
            for i, (b, t) in enumerate(group):
                c = c0 + i
                q, qf = T.take()
                if i % 2 == 0:
                    s = square_into(q[:, 2:TW], M[:, c, :], toks[i], qf)
                else:
                    s = dve.do([toks[i], qf], dve.e.tensor_tensor, q[:, 2:TW], M[:, c, :], M[:, c, :], ALU.mult)
                held.append((q, s))
            return toks, held

        def count_squares(stat, held):
            for q, s in held:
                T.give(q, stat.add(q[:, 2:TW], s))

        def closing_gemm(rhs, nk, gname, pace=1):
            mt, held, box = [], [], {}

            def mid():
                bg.until(lambda: len(B.free) >= 2)
                box["s"] = Stat()
                count_squares(box["s"], held)

            for g in range(2):
                res = gemm([P] * 4, rhs, nk, mid if g == 1 else None, pace=pace)
                bg.until(lambda: len(T.free) >= 4)
                m, held = evac_m(res, 4 * g)
                mt += m
            count_squares(box["s"], held)
            residual(mt, box["s"], gname)

        def ffn(n, groups, gname, both, func, ntile, post):
            AHn = at(f"AH{n}", [P, ntile, S], arena, F32R)
            ALn = at(f"AL{n}", [P, ntile, S], arena + ntile * S * 4, F32R)
            inp = Input(gname)
            cw, cb = (COLS[x][0] for x in (f"cw{n}", f"cb{n}"))
            nct = {0: 44, 1: 44, 2: 16}[n]
            at_toks = {}
            arena_free = state["arena_readers"]

            def after(g, res):
                us, tu = [], []
                for i in range(4):
                    b, t = res[i]
                    u, uf = T.take()
                    a = dve.do([t, inp.rb, uf], dve.e.tensor_tensor, u[:, 2:TW], b[:, :], RB[:, :], ALU.mult)
                    B.give(b, a)
                    us.append(u)
                    tu.append(a)
                state["rb_readers"] = [a]
                yield
                todo = range(4) if both else range(2)
                idx = [2 * g, 2 * g + 1, ntile + 2 * g, ntile + 2 * g + 1]
                cs = {}
                for i in todo:
                    c, cf = T.take()
                    o = cw + 2 * nct + idx[i]
                    a = act.do([tu[i], cf], act.e.activation, c[:, 2:TW], us[i][:, 2:TW], ACT.Identity,
                               bias=cols[:, cb + idx[i]:cb + idx[i] + 1], scale=cols[:, o:o + 1])
                    cs[i] = (c, a)
                yield
                for k in (1, 0):
                    for i in todo:
                        c, a = cs[i]
                        o = cw + k * nct + idx[i]
                        a = dve.do([a], dve.e.scalar_tensor_tensor, c[:, 2:TW], us[i][:, k:TW - 2 + k],
                                   cols[:, o:o + 1], c[:, 2:TW], ALU.mult, ALU.add)
                        cs[i] = (c, a)
                        if k == 0:
                            T.give(us[i], a)
                            us[i], tu[i] = c, a
                    yield
                for i in range(2):
                    tu[i] = act.do([tu[i]], act.e.activation, us[i][:, 2:TW], us[i][:, 2:TW], func)
                yield
                for i in range(2):
                    u, v = us[i], us[2 + i]
                    tu[i] = pool.do([tu[i], tu[2 + i]], pool.e.tensor_tensor, u[:, 2:TW], u[:, 2:TW], v[:, 2:TW],
                                    ALU.mult)
                    T.give(v, tu[i])
                yield
                for i in range(2):
                    f, u = 2 * g + i, us[i]
                    h = act.do([tu[i], arena_free], act.e.activation, AHn[:, f, :], u[:, 2:TW], ACT.Copy)
                    l = dve.do([tu[i], h, arena_free], dve.e.tensor_tensor, ALn[:, f, :], u[:, 2:TW],
                               AHn[:, f, :].bitcast(F32), ALU.subtract)
                    T.give(u, l, h)
                    at_toks[f] = [h, l]

            for g in range(groups):
                res = gemm([P] * 4, inp.rhs)
                if g == 0:
                    inp.rms()
                bg.until(lambda: len(T.free) >= 8)
                bg.add(after(g, res))
            state["h_readers"] = (pe, pe.count)

            def rhs(f):
                bg.until(lambda: f in at_toks)
                return AHn[:, f, :], ALn[:, f, :], at_toks[f]

            if post is None:
                added_gemm(rhs, ntile, inp)
            else:
                closing_gemm(rhs, ntile, post)
            state["arena_readers"] = [(pe, pe.count)]

        def added_gemm(rhs, nk, inp, pace=1):
            xt = []
            for g in range(2):
                for i, (b, t) in enumerate(gemm([P] * 4, rhs, nk, pace=pace)):
                    c = 4 * g + i
                    x = dve.do([t, inp.sq[c], inp.parts[c]], dve.e.tensor_tensor, X[:, c, :], b[:, :], X[:, c, :],
                               ALU.add)
                    B.give(b, x)
                    xt.append(x)
            state["x"] = lambda c: xt[c]

        state["arena_readers"] = []

        def sub(name, shape, off, dt=F32):
            return at(name, shape, arena + off, dt)

        def pool_mixer():
            invc = sub("invc", [P, 64], 0)
            dk = act.dma([], lot("s_invc"), act.e.dma_start, invc[:, :],
                         A["const"][:, CONST["invc"][0]:CONST["invc"][0] + 64])
            s = Stat()
            for c in range(KD):
                if c % 2 == 0:
                    t = act.do([x_loaded[c]], act.e.activation, M[:, c, :], X[:, c, :], ACT.Square)
                else:
                    t = dve.do([x_loaded[c]], dve.e.tensor_tensor, M[:, c, :], X[:, c, :], X[:, c, :], ALU.mult)
                last = s.add(M[:, c, :], t)
            rb = to_rb(*s.finish())
            toks = {}

            def pooled(c):
                eng = (dve, pool)[c % 2]
                gi = c // 2
                h = M[:, c, :]
                ht = dve.do([rb, last, x_loaded[c]], dve.e.scalar_tensor_tensor, h, X[:, c, :], col("mix_pre0", c),
                            RB[:, :], ALU.mult, ALU.mult)
                state["rb_readers"] = [ht]
                yield
                cur, ct = h, [ht]
                held = None
                for step in range(gi + 1):
                    w = 1 << step
                    n_, nf = T.take()
                    n = n_[:, 2:TW]
                    a = eng.do([ct, nf], eng.e.tensor_tensor, n[:, w:S], cur[:, w:S], cur[:, 0:S - w], ALU.add)
                    b = act.do([ct, nf], act.e.activation, n[:, 0:w], cur[:, 0:w], ACT.Copy)
                    if held is not None:
                        T.give(held, a, b)
                    cur, ct, held = n, [a, b], n_
                    yield
                w = 2 << gi
                a = dve.do([ct, ht], dve.e.scalar_tensor_tensor, h[:, w:S], cur[:, w:S], 1.0 / w, h[:, w:S],
                           ALU.mult, ALU.subtract)
                b = pool.do([ct, dk], pool.e.tensor_tensor, cur[:, 0:w], cur[:, 0:w], invc[:, 16 * gi:16 * gi + w],
                            ALU.mult)
                b = pool.do([b, ht], pool.e.tensor_tensor, h[:, 0:w], cur[:, 0:w], h[:, 0:w], ALU.subtract)
                T.give(held, a, b)
                yield
                th = act.do([a, b], act.e.activation, Hh[:, c, :], h, ACT.Copy)
                tl = dve.do([a, b, th], dve.e.tensor_tensor, Hl[:, c, :], h, Hh[:, c, :].bitcast(F32), ALU.subtract)
                toks[c] = [th, tl]

            for half in range(2):
                for c in range(4 * half, 4 * half + 4):
                    bg.add(pooled(c))
                bg.finish()
                for gi in (2 * half, 2 * half + 1):
                    if gi == 0:
                        mt, stat = [], Stat()
                    sl, ready = next_piece()
                    wh, wl = spls[sl]
                    res = []
                    for m in range(2):
                        b, bf = B.take()
                        pe.wait(bf, ready)
                        for k in range(2):
                            c = 2 * gi + k
                            pe.wait(toks[c])
                            o = k * 256 + m * P
                            t = mm3(b[:, :], wh[:, o:o + P], wl[:, o:o + P], Hh[:, c, :], Hl[:, c, :], k == 0, k == 1)
                        res.append((b, t))
                    done_piece(sl, t)
                    state["m_readers"] = toks[2 * gi] + toks[2 * gi + 1]
                    m_, held = evac_m(res, 2 * gi, "pool_scale")
                    mt += m_
                    count_squares(stat, held)
            state["h_readers"] = (pe, pe.count)
            residual(mt, stat, "mix_post0")

        def window_mixer():
            q = sub("wq", [P, 8, S], 0)
            k_ = sub("wk", [P, 2, S], 16384)
            v_ = sub("wv", [P, 2, S], 20480)
            vt_ = sub("wvt", [P, 4, 256], 24576)
            cs = sub("wcs", [P, S], 28672)
            sn = sub("wsn", [P, S], 30720)
            ang = sub("wang", [P, S], 32768)
            y0 = sub("wy0", [P, S], 34816)
            y1 = sub("wy1", [P, S], 36864)
            posi = sub("wpos", [P, S], 38912, I32)
            mask = sub("wmask", [P, 256], 40960)
            Sb = [sub(f"wSb{i}", [P, 4, 256], 43008 + 4096 * i) for i in range(2)]
            PT = [sub(f"wPT{i}", [P, 8, P], 51200 + 4096 * i) for i in range(2)]
            sm = [sub(f"wsm{i}", [P, 32], 59392 + 128 * i) for i in range(2)]
            af = state["arena_readers"]
            lp, lm = lot("s_pos"), lot("s_mask")
            dp = act.dma([af], lp, act.e.dma_start, posi[:, :], A["pos"])
            o = CONST["swa"][0]
            dm = act.dma([af], lm, act.e.dma_start, mask[:, :], A["const"][:, o:o + 256])
            inp = Input("kv_g")
            a = dve.do([dp, af], dve.e.tensor_copy, y0[:, :], posi[:, :])
            a = dve.do([a, af], dve.e.tensor_scalar, ang[:, :], y0[:, :], col("invf", 0), None, ALU.mult)
            r = None
            for turn, dst in ((0.0, sn), (0.25, cs)):
                b = dve.do([a, r], dve.e.tensor_scalar, y0[:, :], ang[:, :], 1.0 / (2 * math.pi), turn, ALU.mult,
                           ALU.add)
                b = dve.do([b], dve.e.tensor_scalar, y0[:, :], y0[:, :], MAGIC, None, ALU.add)
                b = dve.do([b], dve.e.tensor_scalar, y0[:, :], y0[:, :], MAGIC, None, ALU.subtract)
                src = ang
                for part in (PI_HI, PI_MID, PI_LO):
                    b = dve.do([b, r], dve.e.scalar_tensor_tensor, y1[:, :], y0[:, :], -part, src[:, :], ALU.mult,
                               ALU.add)
                    src = y1
                b = dve.do([b], dve.e.tensor_scalar, y1[:, :], y1[:, :], turn * 2 * math.pi, 3.1415925, ALU.add,
                           ALU.min)
                b = dve.do([b], dve.e.tensor_scalar, y1[:, :], y1[:, :], -3.1415925, None, ALU.max)
                r = act.do([b, af], act.e.activation, dst[:, :], y1[:, :], ACT.Sin)
            trig = r
            res = gemm([P] * 4, inp.rhs)
            rb = inp.rms()
            t1 = dve.do([trig, rb], dve.e.tensor_tensor, cs[:, :], cs[:, :], RB[:, :], ALU.mult)
            t2 = dve.do([trig, rb], dve.e.tensor_tensor, sn[:, :], sn[:, :], RB[:, :], ALU.mult)

            def rotate(ra, rbk, da, db, scale):
                (a, at_), (b, bt) = ra, rbk
                out_ = []
                tmp = []
                for src, st_, tab, tt in ((a, at_, cs, t1), (b, bt, sn, t2), (b, bt, cs, t1), (a, at_, sn, t2)):
                    x, xf = T.take()
                    if scale == 1.0:
                        y = dve.do([st_, tt, xf], dve.e.tensor_tensor, x[:, 2:TW], src[:, :], tab[:, :], ALU.mult)
                    else:
                        y = dve.do([st_, tt, xf], dve.e.scalar_tensor_tensor, x[:, 2:TW], src[:, :], scale,
                                   tab[:, :], ALU.mult, ALU.mult)
                    tmp.append((x, y))
                B.give(a, tmp[3][1])
                B.give(b, tmp[2][1])
                for i, dst, op in ((0, da, ALU.subtract), (2, db, ALU.add)):
                    (x, xt_), (y, yt_) = tmp[i], tmp[i + 1]
                    z = pool.do([xt_, yt_, af], pool.e.tensor_tensor, dst, x[:, 2:TW], y[:, 2:TW], op)
                    T.give(x, z)
                    T.give(y, z)
                    out_.append(z)
                return out_

            kt = rotate(res[0], res[1], k_[:, 0, :], k_[:, 1, :], 0.125)
            vts = []
            for i in range(2):
                b, t = res[2 + i]
                a = dve.do([t, rb, af], dve.e.tensor_tensor, v_[:, i, :], b[:, :], RB[:, :], ALU.mult)
                B.give(b, a)
                vts.append(a)
            state["rb_readers"] = [a]
            state["h_readers"] = (pe, pe.count)
            inp = Input("mix_pre1", squares=False)
            qt = []
            for g in range(2):
                res = gemm([P] * 4, inp.rhs)
                for i in range(2):
                    p = 2 * g + i
                    qt.append(rotate(res[2 * i], res[2 * i + 1], q[:, 2 * p, :], q[:, 2 * p + 1, :], 1.0))
                if g == 0:
                    for i in range(2):
                        b, bf = B.take()
                        for n in range(4):
                            t = pe.do([bf, vts[i]], pe.e.transpose, b[:, n * P:(n + 1) * P],
                                      v_[:, i, n * P:(n + 1) * P], ident[:, :])
                        vtok = act.do([t], act.e.activation, vt_[:, :, i * P:(i + 1) * P],
                                      b[:, :].rearrange("p (n c) -> p n c", n=4), ACT.Copy)
                        B.give(b, vtok)
            state["h_readers"] = (pe, pe.count)
            hr = state["h_readers"]
            ht = {}
            SB = Slots(list(range(2)))
            so = COLS["sinks"][0]
            done = {p: [] for p in range(4)}

            def attend(p, n):
                k0 = 128 * max(n - 1, 0)
                nk = 128 * (n + 1) - k0
                mo = 256 - nk
                nb = nk // P
                while len(B.free) < 4 or not SB.free:
                    yield
                z, zf = SB.take()
                sx, sc, pt = Sb[z], sm[z], PT[z]
                sbk = [B.take() for j in range(4)]
                for half in range(2):
                    for j in range(4):
                        b, bf = sbk[j]
                        t = pe.do([bf, qt[p], kt], pe.e.matmul, b[:, 0:nk],
                                  q[32 * j:32 * j + 32, 2 * p + half, n * P:(n + 1) * P],
                                  k_[32 * j:32 * j + 32, half, k0:k0 + nk], start=half == 0, stop=half == 1)
                        if half == 1:
                            sbk[j] = (b, t)
                qread = t
                yield
                for j in range(4):
                    b, t = sbk[j]
                    a = dve.do([t, dm, zf], dve.e.tensor_tensor_reduce, sx[:, j, 0:nk], b[:, 0:nk], mask[:, mo:256],
                               1.0, -3e38, ALU.add, ALU.max, sc[:, j:j + 1])
                    B.give(b, a)
                sk = cols[:, so + 4 * p:so + 4 * p + 4]
                a = dve.do([a], dve.e.tensor_tensor, sc[:, 4:8], sc[:, 0:4], sk, ALU.max)
                a = dve.do([a], dve.e.tensor_scalar, sc[:, 8:12], sc[:, 4:8], -1.0, None, ALU.mult)
                b2 = dve.do([a], dve.e.tensor_tensor, sc[:, 12:16], sc[:, 8:12], sk, ALU.add)
                yield
                for j in range(4):
                    x = act.do([a], act.e.activation, sx[:, j, 0:nk], sx[:, j, 0:nk], ACT.Exp, bias=sc[:, 8 + j:9 + j],
                               accum_out=sc[:, 16 + j:17 + j])
                x = act.do([b2], act.e.activation, sc[:, 20:24], sc[:, 12:16], ACT.Exp)
                yield
                a = dve.do([x], dve.e.tensor_tensor, sc[:, 24:28], sc[:, 16:20], sc[:, 20:24], ALU.add)
                a = dve.do([a], dve.e.reciprocal, sc[:, 28:32], sc[:, 24:28])
                for j in range(4):
                    a = dve.do([a], dve.e.tensor_scalar, sx[:, j, 0:nk], sx[:, j, 0:nk], sc[:, 28 + j:29 + j], None,
                               ALU.mult)
                yield
                while len(B.free) < nb + 1:
                    yield
                ob, obf = B.take()
                tb_ = []
                for kb in range(nb):
                    b, bf = B.take()
                    for j in range(4):
                        t = pe.do([bf, a], pe.e.transpose, b[:, j * P:(j + 1) * P], sx[:, j, kb * P:(kb + 1) * P],
                                  ident[:, :])
                    tb_.append((b, t))
                yield
                pts = []
                for kb in range(nb):
                    b, t = tb_[kb]
                    src = b[:, :].rearrange("p (j c) -> p j c", j=4)
                    if kb == 0:
                        c = act.do([t, zf], act.e.activation, pt[:, 0:4, :], src, ACT.Copy)
                    else:
                        c = dve.do([t, zf], dve.e.tensor_copy, pt[:, 4:8, :], src)
                    B.give(b, c)
                    pts.append(c)
                yield
                for j in range(4):
                    o = (j // 2) * P
                    r0 = 64 * (j % 2)
                    for kb in range(nb):
                        blk = k0 // P + kb
                        t = pe.do([pts, vtok, obf], pe.e.matmul, ob[r0:r0 + 64, o:o + P],
                                  vt_[:, blk, j * 64:(j + 1) * 64], pt[:, 4 * kb + j, :], start=kb == 0,
                                  stop=kb == nb - 1, skip_group_check=True)
                SB.give(z, t)
                yield
                o = act.do([t, qread], act.e.activation, q[:, 2 * p:2 * p + 2, n * P:(n + 1) * P],
                           ob[:, 0:256].rearrange("p (c t) -> p c t", c=2), ACT.Copy)
                B.give(ob, o)
                done[p].append(o)

            def pairs(which):
                for i in range(which, 16, 2):
                    yield from attend(i // 4, i % 4)

            bg.add(pairs(0))
            bg.add(pairs(1))

            def rhs(c):
                p = c // 2
                if c not in ht:
                    bg.until(lambda: len(done[p]) == 4)
                    h = act.do([done[p], hr], act.e.activation, Hh[:, c, :], q[:, c, :], ACT.Copy)
                    l = dve.do([h, done[p], hr], dve.e.tensor_tensor, Hl[:, c, :], q[:, c, :],
                               Hh[:, c, :].bitcast(F32), ALU.subtract)
                    ht[c] = [h, l]
                return Hh[:, c, :], Hl[:, c, :], ht[c]

            closing_gemm(rhs, KD, "mix_post1")
            state["h_readers"] = (pe, pe.count)
            state["arena_readers"] = [(pe, pe.count), (dve, dve.count), (act, act.count), (pool, pool.count)]

        def second_mixer():
            af = state["arena_readers"]
            big = sub("b_big", [P, 26, S], 0)
            KCR, VCR, KS, VS, KW, VW, Q2, MQ, MK, MV, MO = 0, 1, 2, 3, 4, 5, 6, 10, 14, 18, 22
            o = 26 * 2048
            bias = sub("b_bias", [P, 8, S], o)
            o += 16384
            vtok = sub("b_vtok", [P, 2, 4, P], o)
            o += 4096
            mvt = sub("b_mvt", [P, 4, 4, P], o)
            blk = [at(f"b_blk{i}", [P, 16, 62], arena + o + 4096 * i) for i in range(2)]
            o += 8192
            pe2 = sub("b_pe", [P, 2, 2, 16], o)
            w2 = sub("b_w2", [P, 2, 64], o + 256)
            hid = sub("b_hid", [P, 2, 64], o + 768)
            kct = sub("b_kct", [P, 32], o + 1280)
            vct = sub("b_vct", [32, 2, 64], o + 1408)
            cb = sub("b_cb", [P, 4, 8, 31], o + 1920)
            gsig = sub("b_gsig", [P, 4, 24], o + 5888)
            assert o + 6272 <= 2 * FT * 2048, o
            w1 = [at(f"b_w1{i}", [P, 16, P], m_at + 8192 * i) for i in range(2)]
            Sb = [at(f"b_Sb{i}", [P, 4, S], m_at + 8192 * i) for i in range(2)]
            inp = Input("ln1")
            lots = [lot(f"s_b{i}") for i in range(6)]
            dist = at("b_dist", [P, S], arena + MO * 2048)
            cmpc = at("b_cmp", [P, 124], arena + (MO + 1) * 2048)
            def const(name):
                c, w = CONST[name]
                return A["const"][:, c:c + w]
            d_dist = act.dma([af], lots[0], act.e.dma_start, dist[:, :], const("dist"))
            d_cmp = act.dma([af], lots[1], act.e.dma_start, cmpc[:, :], const("cmp"))
            d_sel = act.dma([], lot("s_sel"), act.e.dma_start, rows[:, 0, :],
                            A["const"][0:4, CONST["sel"][0]:CONST["sel"][0] + 512])
            d_pe = act.dma([af], lots[2], act.e.dma_start, pe2[:, :, :, :], A["cmp_pe"])
            d_w2 = act.dma([af], lots[3], act.e.dma_start, w2[:, :, :], A["cmp_w2"])
            bt = []
            for h in range(8):
                bt.append(pool.do([d_dist, af], pool.e.tensor_scalar, bias[:, h, :], dist[:, :], SLOPES[h], None,
                                  ALU.mult))
                bt.append(pool.do([d_cmp, af], pool.e.tensor_scalar, cb[:, :, h, :],
                                  cmpc[:, :].rearrange("p (b n) -> p b n", b=4), SLOPES[h], None, ALU.mult))
            biast = bt[-1]
            box = {}
            tk = {}

            def scaled(i, b, t, scale, eng=None, extra=None):
                if scale == 1.0:
                    a = dve.do([t, box["rb"], af, extra], dve.e.tensor_tensor, big[:, i, :], b[:, :], RB[:, :],
                               ALU.mult)
                else:
                    a = dve.do([t, box["rb"], af, extra], dve.e.scalar_tensor_tensor, big[:, i, :], b[:, :], scale,
                               RB[:, :], ALU.mult, ALU.mult)
                B.give(b, a)
                tk[i] = a
                return a

            def to_tokens(src, dst, t, eng):
                b, bf = B.take()
                for n in range(4):
                    a = pe.do([bf, t], pe.e.transpose, b[:, n * P:(n + 1) * P], big[:, src, n * P:(n + 1) * P],
                              ident[:, :])
                a = act.do([a, af], act.e.activation, dst, b[:, :].rearrange("p (n c) -> p n c", n=4), ACT.Copy)
                B.give(b, a)
                return a

            res = gemm([P] * 4, inp.rhs)
            box["rb"] = inp.rms()
            box["sq"] = inp.counted
            dw1 = [act.dma([box["sq"]], lots[4 + i], act.e.dma_start, w1[i][:, :, :],
                           A["cmp_w1"][i].rearrange("(c p) m -> p c m", p=P)) for i in range(2)]
            for i, (b, t) in enumerate(res):
                scaled((KCR, VCR, KS, VS)[i], b, t, 1.0)
            bl = []
            for i in range(2):
                for g in range(2):
                    for par in range(2):
                        src = big[64 * g:64 * g + 64, i, :]
                        a0 = src.rearrange("p (n c r) -> p n c r", c=8, r=2)[:, :, :, par]
                        for hf in range(2):
                            a = dve.do([tk[i], d_pe, af], dve.e.tensor_tensor,
                                       blk[i][64 * par:64 * par + 64, 8 * hf:8 * hf + 8, 31 * g:31 * g + 31],
                                       a0[:, hf:hf + 31, :].rearrange("p n c -> p c n"),
                                       pe2[64 * g:64 * g + 64, i, par, 8 * hf:8 * hf + 8].unsqueeze(2).to_broadcast( [64, 8, 31]),
                                       ALU.add)
                            bl.append(a)
            res = gemm([P] * 4, inp.rhs, pace=2)
            for i, (b, t) in enumerate(res):
                scaled((KW, VW, Q2, Q2 + 1)[i], b, t, 1.0 if i < 2 else 0.125)
            hb, hbf = B.take()
            for i in range(2):
                for c in range(16):
                    t = pe.do([hbf, dw1[i], bl], pe.e.matmul, hb[:, 64 * i:64 * i + 62], w1[i][:, c, :],
                              blk[i][:, c, :], start=c == 0, stop=c == 15, skip_group_check=True)
            hidt = t
            a = act.do([t, af], act.e.activation, hid[:, :, 0:62],
                       hb[:, 0:128].rearrange("p (i n) -> p i n", i=2)[:, :, 0:62], ACT.Gelu_apprx_tanh)
            B.give(hb, a)
            cbk, cbf = B.take()
            t = pe.do([cbf, a, d_w2], pe.e.matmul, cbk[0:64, 0:62], w2[:, 0, :], hid[:, 0, 0:62], start=True,
                      stop=True)
            k0 = dve.do([t, af], dve.e.tensor_copy, kct[0:64, 0:31], cbk[0:64, 0:31])
            k1 = dve.do([t, af], dve.e.tensor_copy, kct[64:128, 0:31], cbk[0:64, 31:62])
            B.give(cbk, k0, k1)
            cbk, cbf = B.take()
            for g in range(2):
                t = pe.do([cbf, a, d_w2], pe.e.matmul, cbk[0:31, 64 * g:64 * g + 64], hid[:, 1, 31 * g:31 * g + 31],
                          w2[:, 1, :], start=True, stop=True, skip_group_check=True)
            vc = dve.do([t, af], dve.e.tensor_copy, vct[0:31, :, :],
                        cbk[0:31, 0:128].rearrange("p (g d) -> p g d", g=2))
            B.give(cbk, vc)
            cmpt = [k0, k1, vc]
            vst = to_tokens(VS, vtok[:, 0, :, :], tk[VS], act)
            vwt = to_tokens(VW, vtok[:, 1, :, :], tk[VW], act)
            res = gemm([P, P, 88], inp.rhs)
            scaled(Q2 + 2, res[0][0], res[0][1], 0.125)
            scaled(Q2 + 3, res[1][0], res[1][1], 0.125)
            gb, gt = res[2]
            zi, zif = T.take()
            zf, zff = T.take()
            za, zaf = T.take()
            a0 = dve.do([gt, box["rb"], zif], dve.e.tensor_tensor, zi[0:4, 2:TW], gb[0:4, :], RB[0:4, :], ALU.mult)
            a1 = dve.do([gt, zff], dve.e.tensor_tensor, zf[0:4, 2:TW], gb[32:36, :], RB[32:36, :], ALU.mult)
            a2 = dve.do([gt, zaf], dve.e.tensor_tensor, za[0:24, 2:TW], gb[64:88, :], RB[64:88, :], ALU.mult)
            B.give(gb, a2)
            b, bf = B.take()
            for n in range(4):
                t = pe.do([bf, a2], pe.e.transpose, b[:, 24 * n:24 * n + 24], za[0:24, 2 + n * P:2 + (n + 1) * P],
                          ident[0:24, 0:24])
            a = act.do([t, af], act.e.activation, gsig[:, :, :], b[:, 0:96].rearrange("p (n c) -> p n c", n=4),
                       ACT.Sigmoid)
            gc = dve.do([a], dve.e.tensor_scalar, gsig[:, 0, 0:24:3], gsig[:, 0, 0:24:3], col("rv", 0), None,
                        ALU.mult)
            gt_ = [a, gc]
            B.give(b, a)
            T.give(za, t)
            gbo = COLS["gbias"][0]
            lf, lff = T.take()
            l1, l1f = T.take()
            on, onf = T.take()
            R = lambda x: x[0:4, 2:TW]
            i1 = dve.do([a0], dve.e.tensor_scalar, R(zi), R(zi), cols[0:4, gbo:gbo + 1], None, ALU.add)
            f1 = dve.do([a1], dve.e.tensor_scalar, R(zf), R(zf), cols[0:4, gbo + 1:gbo + 2], None, ALU.add)
            a = act.do([f1, l1f], act.e.activation, R(l1), R(zf), ACT.Abs)
            a = act.do([a], act.e.activation, R(l1), R(l1), ACT.Exp, scale=-1.0)
            a = act.do([a], act.e.activation, R(l1), R(l1), ACT.Ln, bias=1.0)
            a = dve.do([a, lff], dve.e.scalar_tensor_tensor, R(lf), R(zf), 0.0, R(l1), ALU.min, ALU.subtract)
            c = dve.do([onf], dve.e.memset, R(on), 1.0)
            a = dve.do([a, c], dve.e.tensor_tensor_scan, R(zf), R(on), R(lf), 0.0, ALU.mult, ALU.add)
            T.give(on, a)
            g_ = dve.do([a, i1], dve.e.tensor_tensor, R(zi), R(zi), R(zf), ALU.subtract)
            m_ = dve.do([g_], dve.e.tensor_tensor_scan, R(lf), R(zi), R(zi), 0.0, ALU.max, ALU.max)
            nm = dve.do([m_], dve.e.scalar_tensor_tensor, R(l1), R(zf), -1.0, R(lf), ALU.mult, ALU.subtract)
            nM = dve.do([m_, nm], dve.e.tensor_scalar, rows[:, 1, :], R(lf), -1.0, None, ALU.mult)
            T.give(lf, nM)
            T.give(zf, nm)
            b, bf = B.take()
            for n in range(4):
                t = pe.do([bf, g_], pe.e.transpose, b[:, 4 * n:4 * n + 4], zi[0:4, 2 + n * P:2 + (n + 1) * P],
                          ident[0:4, 0:4])
            for n in range(4):
                t = pe.do([nm], pe.e.transpose, b[:, 16 + 4 * n:20 + 4 * n], l1[0:4, 2 + n * P:2 + (n + 1) * P],
                          ident[0:4, 0:4])
            gcol = st[:, 32:48]
            emc = st[:, 48:64]
            gct = act.do([t], act.e.activation, gcol, b[:, 0:16], ACT.Copy)
            emt = act.do([t], act.e.activation, emc, b[:, 16:32], ACT.Exp)
            B.give(b, emt)
            T.give(zi, t)
            T.give(l1, t)
            U = Slots([0, 1])
            CP = Slots([(KCR, VCR), (VS, VW)])
            CP.free = [(CP.free[0][0], [(dve, dve.count)]), (CP.free[1][0], [vst, vwt])]
            comp = {}
            qt = [tk[Q2 + r] for r in range(4)]
            ot = {r: [] for r in range(4)}
            left = {tb: 4 for tb in range(4)}
            crd = {tb: [] for tb in range(4)}

            def compressed(tb):
                while not CP.free:
                    yield
                pl, plf = CP.take()
                ready = []
                for g in range(2):
                    cmx, csum, cfac = (st[:, 80 + 4 * k:84 + 4 * k] for k in range(3))
                    while len(B.free) < 1 or len(T.free) < 1:
                        yield
                    b, bf = B.take()
                    pc, pcf = T.take()
                    for r in range(4):
                        t = pe.do([bf, qt, cmpt], pe.e.matmul, b[:, 31 * r:31 * r + 31],
                                  big[64 * g:64 * g + 64, Q2 + r, tb * P:(tb + 1) * P], kct[64 * g:64 * g + 64, 0:31],
                                  start=True, stop=True, skip_group_check=True)
                    yield
                    pv = pc[:, 2:126].rearrange("p (r n) -> p r n", r=4)
                    a = dve.do([t, biast, pcf], dve.e.tensor_tensor, pv,
                               b[:, 0:124].rearrange("p (r n) -> p r n", r=4), cb[:, tb, 4 * g:4 * g + 4, :], ALU.add)
                    B.give(b, a)
                    a = dve.do([a], dve.e.tensor_reduce, cmx, pv, AX, ALU.max)
                    a = dve.do([a], dve.e.tensor_tensor, pv, pv, cmx.unsqueeze(2).to_broadcast([P, 4, 31]),
                               ALU.subtract)
                    yield
                    a = act.do([a], act.e.activation, pc[:, 2:126], pc[:, 2:126], ACT.Exp)
                    yield
                    a = dve.do([a], dve.e.tensor_reduce, csum, pv, AX, ALU.add)
                    a = dve.do([a], dve.e.reciprocal, cfac, csum)
                    a = dve.do([a, gt_], dve.e.tensor_tensor, cfac, cfac, gsig[:, tb, 12 * g:12 * g + 12:3], ALU.mult)
                    a = dve.do([a], dve.e.tensor_tensor, pv, pv, cfac.unsqueeze(2).to_broadcast([P, 4, 31]),
                               ALU.mult)
                    yield
                    while len(B.free) < 1:
                        yield
                    b, bf = B.take()
                    for r in range(4):
                        t = pe.do([bf, a], pe.e.transpose, b[0:31, r * P:(r + 1) * P], pc[:, 2 + 31 * r:33 + 31 * r],
                                  ident[:, :])
                    T.give(pc, t)
                    yield
                    c = act.do([t, plf], act.e.activation, big[0:31, pl[g], :], b[0:31, :], ACT.Copy)
                    B.give(b, c)
                    ready.append(c)
                comp[tb] = (pl, ready)

            def attend(tb, r):
                L = (tb + 1) * P
                while tb not in comp or len(B.free) < 4 or not U.free:
                    yield
                z, zf = U.take()
                sx = Sb[z]
                sc = st[:, 96 + 16 * z:112 + 16 * z]
                sbk = [B.take() for i in range(4)]
                for w in range(2):
                    for g in range(2):
                        b, bf = sbk[2 * g + w]
                        t = pe.do([bf, qt, tk[KS], tk[KW]], pe.e.matmul, b[:, 0:L],
                                  big[64 * g:64 * g + 64, Q2 + r, tb * P:(tb + 1) * P],
                                  big[64 * g:64 * g + 64, (KS, KW)[w], 0:L], start=True, stop=True)
                        sbk[2 * g + w] = (b, t)
                qread = t
                yield
                for u in range(4):
                    b, t = sbk[u]
                    a = dve.do([t, biast, zf], dve.e.tensor_tensor_reduce, sx[:, u, 0:L], b[:, 0:L],
                               bias[:, 4 * (u // 2) + r, S - L:S], 1.0, -3e38, ALU.add, ALU.max, sc[:, u:u + 1])
                    B.give(b, a)
                a = dve.do([a], dve.e.tensor_scalar, sc[:, 4:8], sc[:, 0:4], -1.0, None, ALU.mult)
                yield
                for u in range(4):
                    x = act.do([a], act.e.activation, sx[:, u, 0:L], sx[:, u, 0:L], ACT.Exp, bias=sc[:, 4 + u:5 + u],
                               accum_out=sc[:, 8 + u:9 + u])
                yield
                a = dve.do([x], dve.e.reciprocal, sc[:, 12:16], sc[:, 8:12])
                gv = gsig[:, tb, :].rearrange("p (g r c) -> p g r c", g=2, r=4)[:, :, r, 1:3]
                fv = sc[:, 12:16].rearrange("p (g w) -> p g w", g=2)
                a = dve.do([a, gt_], dve.e.tensor_tensor, fv, fv, gv, ALU.mult)
                for u in range(4):
                    a = dve.do([a], dve.e.tensor_scalar, sx[:, u, 0:L], sx[:, u, 0:L], sc[:, 12 + u:13 + u], None,
                               ALU.mult)
                yield
                while len(B.free) < 3 or len(T.free) < 2:
                    yield
                ob, obf = B.take()
                pl, cready = comp[tb]
                for g in range(2):
                    t = pe.do([obf, cready, cmpt], pe.e.matmul, ob[64 * g:64 * g + 64, 0:P], vct[0:31, g, :],
                              big[0:31, pl[g], r * P:(r + 1) * P], start=True, stop=False, skip_group_check=True)
                crd[tb].append(t)
                for w in range(2):
                    while len(B.free) < 2 or len(T.free) < 2:
                        yield
                    got = []
                    for g in range(2):
                        b, bf = B.take()
                        for kb in range(tb + 1):
                            t = pe.do([bf, a], pe.e.transpose, b[:, kb * P:(kb + 1) * P],
                                      sx[:, 2 * g + w, kb * P:(kb + 1) * P], ident[:, :])
                        got.append((b, t, T.take()))
                    yield
                    pts = []
                    for g in range(2):
                        b, t, (p_, pf) = got[g]
                        if g == 0:
                            c = act.do([t, pf], act.e.activation, p_[:, 2:2 + L], b[:, 0:L], ACT.Copy)
                        else:
                            c = dve.do([t, pf], dve.e.tensor_copy, p_[:, 2:2 + L], b[:, 0:L])
                        B.give(b, c)
                        pts.append(c)
                    yield
                    for g in range(2):
                        p_ = got[g][2][0]
                        for kb in range(tb + 1):
                            t = pe.do([pts, vst, vwt], pe.e.matmul, ob[64 * g:64 * g + 64, 0:P],
                                      vtok[:, w, kb, 64 * g:64 * g + 64], p_[:, 2 + kb * P:2 + (kb + 1) * P],
                                      start=False, stop=w == 1 and kb == tb, skip_group_check=True)
                        T.give(p_, t)
                U.give(z, t)
                yield
                o = act.do([t, qread], act.e.activation, big[:, Q2 + r, tb * P:(tb + 1) * P], ob[:, 0:P], ACT.Copy)
                B.give(ob, o)
                ot[r].append(o)
                left[tb] -= 1
                if left[tb] == 0:
                    CP.give(pl, crd[tb])

            def lane(tasks):
                for task in tasks:
                    yield from task

            bg.add(lane([compressed(tb) for tb in range(4)]))
            units = [(tb, r) for tb in range(4) for r in range(4)]
            bg.add(lane([attend(*u) for u in units[0::2]]))
            bg.add(lane([attend(*u) for u in units[1::2]]))

            for i, (b, t) in enumerate(gemm([P] * 4, inp.rhs, pace=2)):
                scaled(MQ + i, b, t, 128 ** -0.5)
            for i, (b, t) in enumerate(gemm([P] * 4, inp.rhs, pace=2)):
                scaled(MK + i, b, t, 1.0)
            for i, (b, t) in enumerate(gemm([P] * 4, inp.rhs, pace=2)):
                scaled(MV + i, b, t, 1.0)
            mvtt = []
            for h in range(4):
                bg.until(lambda: len(B.free) >= 1)
                mvtt.append(to_tokens(MV + h, mvt[:, h, :, :], [tk[MV + h], hidt], act))

            mt = {}

            def mlstm(h, lane_):
                while len(B.free) < 3 or len(T.free) < 3:
                    yield
                b, bf = B.take()
                num, numf = B.take()
                den, denf = B.take()
                nb_, nbf = T.take()
                t = pe.do([bf, nM, d_sel], pe.e.matmul, b[:, :], rows[:, 0, h * P:(h + 1) * P], rows[:, 1, :],
                          start=True, stop=True)
                yield
                nbt = act.do([t, nbf], act.e.activation, nb_[:, 2:TW], b[:, :], ACT.Copy)
                s_, sf = b, nbt
                yield
                for sbk in range(4):
                    n0 = sbk * P
                    w = S - n0
                    while len(T.free) < 1:
                        yield
                    e_, ef = T.take()
                    ts_ = pe.do([sf, tk[MK + h], tk[MQ + h]], pe.e.matmul, s_[:, 0:w], big[:, MK + h, n0:n0 + P],
                                big[:, MQ + h, n0:S], start=True, stop=True)
                    qread = ts_
                    a = dve.do([nbt, gct, ef], dve.e.tensor_scalar, e_[:, 2 + n0:TW], nb_[:, 2 + n0:TW],
                               gcol[:, 4 * sbk + h:4 * sbk + h + 1], 0.0, ALU.add, ALU.min)
                    nbr = a
                    yield
                    a = act.do([a], act.e.activation, e_[:, 2 + n0:TW], e_[:, 2 + n0:TW], ACT.Exp)
                    yield
                    a = dve.do([a, ts_], dve.e.tensor_tensor, e_[:, 2 + n0:TW], s_[:, 0:w], e_[:, 2 + n0:TW],
                               ALU.mult)
                    sf = a
                    yield
                    a = pool.do([a], pool.e.affine_select, out=e_[:, 2 + n0:2 + n0 + P],
                                in_=e_[:, 2 + n0:2 + n0 + P], compare_op=ALU.is_ge, fill=0.0, base=0,
                                pattern=[[1, P]], channel_multiplier=-1)
                    yield
                    t = pe.do([numf, a, mvtt[h]], pe.e.matmul, num[:, n0:S], mvt[:, h, sbk, :], e_[:, 2 + n0:TW],
                              start=sbk == 0, stop=sbk == 3, skip_group_check=True)
                    for tb in range(sbk, 4):
                        t = pe.do([denf], pe.e.matmul, den[:, tb:tb + 1], e_[:, 2 + tb * P:2 + (tb + 1) * P],
                                  ones[:, 0:1], start=sbk == 0 and tb == 0, stop=True, skip_group_check=True)
                    T.give(e_, t)
                T.give(nb_, nbr)
                yield
                res = big[:, MQ + h, :]
                a = dve.do([t, qread], dve.e.tensor_copy, res, num[:, :])
                B.give(num, a)
                while len(T.free) < 1:
                    yield
                q_, qf = T.take()
                s2 = act.do([a, qf], act.e.activation, q_[:, 2:TW], res, ACT.Square)
                yield
                for tb in range(4):
                    t = pe.do([s2], pe.e.matmul, den[:, 8 + tb:9 + tb], q_[:, 2 + tb * P:2 + (tb + 1) * P],
                              ones[:, 0:1], start=False, stop=True, skip_group_check=True)
                T.give(q_, t)
                yield
                c0, c1 = (st[:, 64 + 8 * lane_ + 4 * k:68 + 8 * lane_ + 4 * k] for k in range(2))
                em = emc.rearrange("p (n h) -> p n h", h=4)[:, :, h]
                z = act.do([t, mt.get(("c", lane_))], act.e.activation, c0, den[:, 0:4], ACT.Abs)
                z = dve.do([z, emt], dve.e.tensor_tensor, c0, c0, em, ALU.max)
                z = dve.do([z], dve.e.reciprocal, c1, c0)
                z = dve.do([z], dve.e.tensor_tensor, c0, c1, c1, ALU.mult)
                z = dve.do([z], dve.e.tensor_tensor, c0, den[:, 8:12], c0, ALU.mult)
                B.give(den, z)
                z = dve.do([z], dve.e.tensor_scalar, c0, c0, 1.0 / 128, EPS, ALU.mult, ALU.add)
                yield
                z = rsqrt(c0, c0, st[:, 128:132], z)
                yield
                z = dve.do([z], dve.e.tensor_tensor, c1, c1, c0, ALU.mult)
                rbk, r = spread(c1, [z], (s_, sf))
                mt[("c", lane_)] = r
                yield
                a = dve.do([r, s2], dve.e.scalar_tensor_tensor, res, res, col("m_g", h), rbk[:, :], ALU.mult,
                           ALU.mult)
                B.give(rbk, a)
                while MO + h not in tk:
                    yield
                mt[h] = pool.do([a, tk[MO + h]], pool.e.tensor_tensor, res, res, big[:, MO + h, :], ALU.mult)

            bg.add(lane([mlstm(0, 0), mlstm(2, 0)]))
            bg.add(lane([mlstm(1, 1), mlstm(3, 1)]))
            for i, (b, t) in enumerate(gemm([P] * 4, inp.rhs, pace=2)):
                a = scaled(MO + i, b, t, 1.0, extra=[biast])
                tk[MO + i] = act.do([a], act.e.activation, big[:, MO + i, :], big[:, MO + i, :], ACT.Sigmoid)
            state["rb_readers"] = [a]
            hr = (pe, pe.count)
            ht = {}

            def rhs(c):
                if c not in ht:
                    if c < 4:
                        bg.until(lambda: len(ot[c]) == 4)
                        src, tok = big[:, Q2 + c, :], ot[c]
                    else:
                        bg.until(lambda: c - 4 in mt)
                        src, tok = big[:, MQ + c - 4, :], mt[c - 4]
                    h = act.do([tok, hr], act.e.activation, Hh[:, c, :], src, ACT.Copy)
                    l = dve.do([h, tok, hr], dve.e.tensor_tensor, Hl[:, c, :], src, Hh[:, c, :].bitcast(F32),
                               ALU.subtract)
                    ht[c] = [h, l]
                return Hh[:, c, :], Hl[:, c, :], ht[c]

            added_gemm(rhs, KD, inp)
            bg.finish()
            state["h_readers"] = (pe, pe.count)
            state["m_readers"] = [(pe, pe.count)]
            state["arena_readers"] = [(pe, pe.count), (dve, dve.count), (act, act.count), (pool, pool.count)]

        def ple_and_norm():
            af = state["arena_readers"]
            pr = sub("p_raw", [P, 2, S], 0)
            ph = sub("p_hi", [P, 2, S], 4096, F32R)
            pl = sub("p_lo", [P, 2, S], 8192, F32R)
            Y = sub("Y", [P, KD, S], 16384)
            lp = lot("s_p")
            d = act.dma([af], lp, act.e.dma_start, pr[:, :, :], A["pT"].rearrange("(c p) t -> p c t", p=P))
            inp = Input("ple_g")
            a = act.do([d, af], act.e.activation, ph[:, :, :], pr[:, :, :], ACT.Copy)
            b = dve.do([a, af], dve.e.tensor_tensor, pl[:, :, :], pr[:, :, :], ph[:, :, :].bitcast(F32),
                       ALU.subtract)
            pt = [a, b]

            def prhs(k):
                return ph[:, k, :], pl[:, k, :], pt

            nx, held = [], []
            fin = None
            for g in range(2):
                res = gemm([P] * 4, inp.rhs)
                if g == 0:
                    rb = inp.rms()
                us = []
                for i, (b_, t) in enumerate(res):
                    u, uf = T.take()
                    x = dve.do([t, rb, uf], dve.e.tensor_tensor, u[:, 2:TW], b_[:, :], RB[:, :], ALU.mult)
                    B.give(b_, x)
                    x2 = act.do([x], act.e.activation, u[:, 2:TW], u[:, 2:TW], ACT.Sigmoid)
                    us.append((u, x2))
                state["rb_readers"] = [x]
                res = gemm([P] * 4, prhs, 2)
                for i, (b_, t) in enumerate(res):
                    c = 4 * g + i
                    u, ut = us[i]
                    x = dve.do([t, ut], dve.e.tensor_tensor, u[:, 2:TW], b_[:, :], u[:, 2:TW], ALU.mult)
                    B.give(b_, x)
                    x = pool.do([x, inp.sq[c], inp.parts[c]], pool.e.tensor_tensor, X[:, c, :], X[:, c, :], u[:, 2:TW],
                                ALU.add)
                    T.give(u, x)
                    nx.append(x)
                    q, qf = T.take()
                    s_ = square_into(q[:, 2:TW], X[:, c, :], x, qf)
                    held.append((q, s_))
                if g == 0:
                    fin = Stat()
                count_squares(fin, held)
                held = []
            fbank, r = fin.finish()
            lo = [lot("s_out0"), lot("s_out1")]
            ends = []
            o3 = out.rearrange("(c p) t -> p c t", p=P)
            for c in range(KD):
                g = col("final_g", c)
                a = dve.do([r, nx[c], af], dve.e.scalar_tensor_tensor, Y[:, c, :], X[:, c, :], g, fbank[:, :], ALU.mult,
                           ALU.mult)
                ends.append(a)
                if c % 2 == 1:
                    l = Lot(ctx.enter_context(nc.semaphore(f"s_o{c}")))
                    dd = sp.dma([a], l, sp.e.dma_start, o3[:, c - 1:c + 1, :], Y[:, c - 1:c + 1, :])
                    state.setdefault("outs", []).append(dd)

        steps = [
            lambda: pool_mixer(),
            lambda: ffn(0, 11, "ffn_pre0", True, ACT.Gelu_apprx_tanh, FT, "ffn_post0"),
            lambda: window_mixer(),
            lambda: ffn(1, 11, "ffn_pre1", True, ACT.Gelu_apprx_tanh, FT, "ffn_post1"),
            lambda: second_mixer(),
            lambda: ffn(2, 8, "ln2", False, ACT.Silu, FT2, None),
            lambda: ple_and_norm(),
        ]
        n = len(steps) if stop is None else stop
        for s in steps[:n]:
            s()
        if stop is not None:
            o3 = out.rearrange("(c p) t -> p c t", p=P)
            l = lot("s_dbg")
            state["outs"] = [sp.dma([[state["x"](c) for c in range(KD)]], l, sp.e.dma_start, o3, X[:, :, :])]
        sp.wait(state["outs"])

        with nc.Block() as block:
            @block.sync
            def _(e):
                sp.run()

            @block.tensor
            def _(e):
                pe.run()

            @block.vector
            def _(e):
                dve.run()

            @block.scalar
            def _(e):
                act.run()

            @block.gpsimd
            def _(e):
                pool.run()


def constants():
    c = np.zeros((P, NCONST), np.float32)
    p = np.arange(P)[:, None]
    c[:, 0:P] = np.eye(P)
    o = CONST["dist"][0]
    j = np.arange(S)[None, :]
    d = j - 384 - p
    c[:, o:o + S] = np.where(d <= 0, d, NEG)
    o = CONST["swa"][0]
    j = np.arange(256)[None, :]
    rel = 128 + p - j
    c[:, o:o + 256] = np.where((rel >= 0) & (rel < 128), 0.0, NEG)
    o = CONST["cmp"][0]
    for tb in range(4):
        d = (16 * np.arange(31)[None, :] + 31) - (tb * P + p)
        c[:, o + 31 * tb:o + 31 * tb + 31] = np.where(d <= 0, d, NEG)
    o = CONST["sel"][0]
    for h in range(4):
        c[h, o + h * P:o + (h + 1) * P] = 1.0
    o = CONST["invc"][0]
    for gi in range(4):
        w = 2 << gi
        c[:, o + 16 * gi:o + 16 * gi + 16] = 1.0 / np.minimum(np.arange(1, 17), w).astype(np.float32)
    return c


def tiles_of(v):
    return np.ascontiguousarray(v.reshape(-1, P).T)


def layout(i):
    f = np.float32
    i = {k: np.asarray(v) for k, v in i.items()}
    A = {}
    A["xT"] = np.ascontiguousarray(i["x"][0].T)
    A["pT"] = np.ascontiguousarray(i["p_2"][0, 0].T)
    A["pos"] = np.ascontiguousarray(np.broadcast_to(i["positions"][0][None, :], (P, S)))
    cols = np.zeros((P, NCOLS), f)

    def put(name, v):
        o, w = COLS[name]
        assert v.shape[1] == w, (name, v.shape)
        cols[:v.shape[0], o:o + w] = v

    for l in range(2):
        put(f"mix_pre{l}", tiles_of(i["mix_pre_g"][l]))
        put(f"mix_post{l}", tiles_of(i["mix_post_g"][l]))
        put(f"ffn_pre{l}", tiles_of(i["ffn_pre_g"][l]))
        put(f"ffn_post{l}", tiles_of(i["ffn_post_g"][l]))
        put(f"cw{l}", np.concatenate([tiles_of(i["ffn_conv_w"][l, k]) for k in range(3)], axis=1))
        put(f"cb{l}", tiles_of(i["ffn_conv_b"][l]))
    put("pool_scale", tiles_of(i["pool_scale"][0]))
    put("kv_g", tiles_of(i["kv_norm_g"]))
    put("ln1", tiles_of(i["ln1_g_2"][0]))
    put("ln2", tiles_of(i["ln2_g_2"][0]))
    put("ple_g", tiles_of(i["ple_norm_g_2"][0]))
    put("final_g", tiles_of(i["final_g_2"]))
    put("m_g", tiles_of(i["mlstm_norm_g_2"][0]))
    put("cw2", np.concatenate([tiles_of(i["conv_w_2"][0, k]) for k in range(3)], axis=1))
    put("cb2", tiles_of(i["conv_b_2"][0]))
    order = [4 * j + p for p in range(4) for j in range(4)]
    put("sinks", np.broadcast_to(i["sinks"][0][order][None, :], (P, 16)))
    put("gbias", np.ascontiguousarray(i["mlstm_gate_bias_2"][0].reshape(2, 4).T))
    fr = (1.0 / (10000.0 ** (np.arange(0, 64, 2, dtype=f) / 64))).astype(f)
    put("invf", np.tile(fr, 4)[:, None])
    put("rv", (np.arange(P) >= 31).astype(f)[:, None])
    A["cols"] = cols
    A["const"] = constants()
    A["pool_w"] = np.ascontiguousarray(i["pool_w"][0])
    d32 = np.arange(32)
    kcols = [np.concatenate([j * 64 + half * 32 + d32 for j in range(4)]) for half in range(2)]
    A["w_kv"] = np.ascontiguousarray(i["w_kv"][:, np.concatenate(kcols + [np.arange(256, 512)])])
    qcols = [np.concatenate([(4 * j + p) * 64 + half * 32 + d32 for j in range(4)])
             for p in range(4) for half in range(2)]
    A["w_q"] = np.ascontiguousarray(i["w_q"][0][:, np.concatenate(qcols)])
    orow = [np.concatenate([(4 * j + p) * 64 + np.arange(64) for j in (2 * jj, 2 * jj + 1)])
            for p in range(4) for jj in range(2)]
    A["w_o"] = np.ascontiguousarray(i["w_o"][0][np.concatenate(orow)])
    t = np.arange(P)
    for l in range(2):
        cc = [np.concatenate([(2 * g) * P + t, (2 * g + 1) * P + t, (FT + 2 * g) * P + t, (FT + 2 * g + 1) * P + t])
              for g in range(11)]
        A[f"w_in{l}"] = np.ascontiguousarray(i["ffn_w_in"][l][:, np.concatenate(cc)])
        A[f"w_out{l}"] = np.ascontiguousarray(i["ffn_w_out"][l])
    w = i["w_in_2"][0]
    sizes = [512] * 4 + [4, 4, 512] + [128] * 6 + [24]
    offs = np.concatenate([[0], np.cumsum(sizes)])
    sec = [w[:, offs[k]:offs[k + 1]] for k in range(len(sizes))]
    mq, mk, mv, mo, mi, mf, aq, akc, avc, aks, avs, akw, avw, ag = sec
    q2 = [np.concatenate([aq[:, r * 64:(r + 1) * 64], aq[:, (4 + r) * 64:(5 + r) * 64]], axis=1) for r in range(4)]
    z = np.zeros((D, 28), f)
    A["w_in_2"] = np.ascontiguousarray(np.concatenate(
        [akc, avc, aks, avs, akw, avw] + q2 + [mi, z, mf, z, ag, mq, mk, mv, mo], axis=1))
    wo = i["w_out_2"][0]
    rows = [np.concatenate([512 + r * 64 + np.arange(64), 512 + (4 + r) * 64 + np.arange(64)])
            for r in range(4)] + [np.arange(512)]
    A["w_out_2"] = np.ascontiguousarray(wo[np.concatenate(rows)])
    cc = [np.concatenate([(2 * g) * P + t, (2 * g + 1) * P + t, (FT2 + 2 * g) * P + t, (FT2 + 2 * g + 1) * P + t])
          for g in range(8)]
    A["w_up_2"] = np.ascontiguousarray(i["w_up_2"][0][:, np.concatenate(cc)])
    A["w_down_2"] = np.ascontiguousarray(i["w_down_2"][0])
    A["w_pg"] = np.ascontiguousarray(i["w_ple_gate_2"][0])
    A["w_pp"] = np.ascontiguousarray(i["w_ple_proj_2"][0])
    A["cmp_w1"] = np.ascontiguousarray(np.stack([i["cmp_k_w1_2"][0], i["cmp_v_w1_2"][0]]))
    A["cmp_w2"] = np.ascontiguousarray(np.stack([i["cmp_k_w2_2"][0], i["cmp_v_w2_2"][0]], axis=1))
    pes = []
    for n in ("cmp_pos_k_2", "cmp_pos_v_2"):
        v = i[n][0].reshape(16, 2, 64).transpose(2, 1, 0)
        pes.append(np.concatenate([v, v], axis=0))
    A["cmp_pe"] = np.ascontiguousarray(np.stack(pes, axis=1))
    return A


def kernel(**inputs):
    import concourse.bacc as bacc
    from concourse.bass_utils import run_bass_kernel_spmd

    arrays = layout(inputs)
    nc = bacc.Bacc("TRN2", target_bir_lowering=False, num_devices=1)
    aps = {}
    feed = {}
    for name, a in arrays.items():
        feed[f"in_{name}"] = a
        aps[name] = nc.dram_tensor(f"in_{name}", a.shape, mybir.dt.from_np(a.dtype), kind="ExternalInput").ap()
    out = nc.dram_tensor("out_0", (D, S), F32, kind="ExternalOutput").ap()
    build(nc, aps, out)
    r = run_bass_kernel_spmd(nc, [feed], core_ids=[0])
    return np.ascontiguousarray(r.results[0]["out_0"].T)[None]
```

```python
import math
from contextlib import ExitStack

import numpy as np

import concourse.bass as bass
from concourse import mybir

ALU = mybir.AluOpType
ACT = mybir.ActivationFunctionType
F32 = mybir.dt.float32
F32R = mybir.dt.float32r
I32 = mybir.dt.int32
AX = mybir.AxisListType.X

P = 128
S = 512
D = 1024
KD = 8
FT = 22
FT2 = 16
NEG = -1e30
EPS = 1e-6
SLOPES = [2.0 ** (-(h + 1)) for h in range(8)]
NPIECE = 512
TW = S + 2
MAGIC = 12582912.0
PI_HI, PI_MID, PI_LO = 6.28125, 0.0019350051879882812, 3.0197183517896e-07

COLS = {}
_at = 0
for _n, _w in (("mix_pre0", 8), ("mix_pre1", 8), ("mix_post0", 8), ("mix_post1", 8), ("pool_scale", 8),
               ("kv_g", 8), ("ffn_pre0", 8), ("ffn_pre1", 8), ("ffn_post0", 8), ("ffn_post1", 8),
               ("ln1", 8), ("ln2", 8), ("ple_g", 8), ("final_g", 8), ("m_g", 4),
               ("cw0", 132), ("cb0", 44), ("cw1", 132), ("cb1", 44), ("cw2", 48), ("cb2", 16),
               ("sinks", 16), ("gbias", 2), ("invf", 1), ("rv", 1)):
    COLS[_n] = (_at, _w)
    _at += _w
NCOLS = _at

CONST = {}
_at = 0
for _n, _w in (("ident", 128), ("dist", 512), ("swa", 256), ("cmp", 124), ("sel", 512), ("band", 1088)):
    CONST[_n] = (_at, _w)
    _at += _w
NCONST = _at


class Engine:

    def __init__(self, e, sem):
        self.e, self.sem, self.count, self.queue, self.seen = e, sem, 0, [], {}

    def wait(self, *tokens):
        for t in flat(tokens):
            who, value = t
            if self.seen.get(who, 0) < value:
                self.seen[who] = value
                self.queue.append((self.e.wait_ge, (who.sem, value), {}, None, 0))

    def do(self, tokens, op, *args, **named):
        self.wait(tokens)
        self.count += 1
        self.queue.append((op, args, named, self.sem, 1))
        return (self, self.count)

    def quiet(self, tokens, op, *args, **named):
        self.wait(tokens)
        self.queue.append((op, args, named, None, 0))

    def dma(self, tokens, lot, op, *args, **named):
        self.wait(tokens)
        lot.count += 16
        self.queue.append((op, args, named, lot.sem, 16))
        return (lot, lot.count)

    def run(self):
        for op, args, named, sem, by in self.queue:
            done = op(*args, **named)
            if sem is not None:
                done.then_inc(sem, by)


class Lot:

    def __init__(self, sem):
        self.sem, self.count = sem, 0


def flat(tokens):
    for t in tokens:
        if isinstance(t, list):
            yield from flat(t)
        elif t is not None:
            yield t


class Slots:

    def __init__(self, places):
        self.free = [(p, []) for p in places]

    def take(self):
        return self.free.pop(0)

    def give(self, place, *tokens):
        self.free.append((place, list(flat(tokens))))


def build(nc, A, out, stop=None):
    ctx = ExitStack()
    with ctx:
        base = [(nc.sbuf_base + 63) // 64 * 64]
        limit = nc.sbuf_base + 212000

        def place(nbytes):
            at = base[0]
            base[0] += (nbytes + 63) // 64 * 64
            assert base[0] <= limit, (base[0], limit)
            return at

        def at(name, shape, off, dt=F32):
            return nc.alloc_sbuf_tensor_at(name, shape, dt, offset=off)

        def sb(name, shape, dt=F32):
            n = 4
            for x in shape[1:]:
                n *= x
            return at(name, shape, place(n), dt)

        pe, act, dve, pool, sp = (
            Engine(e, ctx.enter_context(nc.semaphore(n)))
            for e, n in ((nc.tensor, "s_pe"), (nc.scalar, "s_act"), (nc.vector, "s_dve"), (nc.gpsimd, "s_pool"),
                         (nc.sync, "s_sp")))

        def lot(name):
            return Lot(ctx.enter_context(nc.semaphore(name)))

        X = sb("X", [P, KD, S])
        m_at = place(KD * S * 4)
        M = at("M", [P, KD, S], m_at)
        Hh = sb("Hh", [P, KD, S], F32R)
        Hl = sb("Hl", [P, KD, S], F32R)
        arena = place(2 * FT * S * 4)
        NRAW, NSPL, NT = 5, 4, 8
        raws = [sb(f"raw{i}", [P, NPIECE]) for i in range(NRAW)]
        raw_lots = [lot(f"s_raw{i}") for i in range(NRAW)]
        spls = [(sb(f"wh{i}", [P, NPIECE], F32R), sb(f"wl{i}", [P, NPIECE], F32R)) for i in range(NSPL)]
        ts = [sb(f"t{i}", [P, TW]) for i in range(NT)]
        RB = sb("RB", [P, S])
        DG = sb("DG", [P, 4, P])
        cols = sb("cols", [P, NCOLS])
        ident = sb("ident", [P, P])
        ones = sb("ones", [P, P])
        mean = sb("mean", [P, 1])
        st = sb("st", [P, 160])
        rows = sb("rows", [4, 2, S])
        banks = [ctx.enter_context(nc.psum_tensor(f"ps{i}", [P, S], F32)) for i in range(8)]

        raw_slots = Slots(list(range(NRAW)))
        spl_slots = Slots(list(range(NSPL)))
        T = Slots(ts)
        B = Slots(banks)

        def col(name, i):
            o = COLS[name][0] + i
            return cols[:, o:o + 1]

        l_c, l_k = lot("s_cols"), lot("s_ident")
        x_loaded = []
        for c in range(KD):
            x_loaded.append(sp.dma([], lot(f"s_x{c}"), sp.e.dma_start, X[:, c, :], A["xT"][c * P:(c + 1) * P, :]))
        d_c = act.dma([], l_c, act.e.dma_start, cols[:, :], A["cols"])
        d_k = act.dma([], l_k, act.e.dma_start, ident[:, :], A["const"][:, 0:P])
        ones_t = pool.do([], pool.e.memset, ones[:, :], 1.0)
        pool.do([], pool.e.memset, mean[:, :], 1.0 / D)
        pool.do([], pool.e.memset, st[:, 128:132], -0.5)
        pads = [pool.do([], pool.e.memset, t[:, 0:2], 0.0) for t in ts]
        pads_t = pads[-1]
        for e in (act, dve, pool, pe):
            e.wait(d_c)
        for e in (dve, pe):
            e.wait(d_k, ones_t, pads_t)
        act.wait(pads_t)

        plan = []

        on_pool = set()

        def pieces_of(w, k, groups, gain=None, spare=False):
            at_ = 0
            for g in groups:
                for r in range(k):
                    if spare:
                        on_pool.add(len(plan))
                    plan.append((w[r * P:(r + 1) * P, at_:at_ + g], g, None if gain is None else col(gain, r)))
                at_ += g

        for gi in range(4):
            plan.append((A["pool_w"][gi].rearrange("(k p) c -> p k c", p=P), 512, None))
        for layer in range(2):
            if layer == 1:
                pieces_of(A["w_kv"], 8, [512], "kv_g")
                pieces_of(A["w_q"], 8, [512, 512], "mix_pre1")
                pieces_of(A["w_o"], 8, [256, 256, 256, 256])
            pieces_of(A[f"w_in{layer}"], 8, [512] * 11)
            pieces_of(A[f"w_out{layer}"], FT, [512, 512])
        pieces_of(A["w_in_2"], 8, [512, 512, 344] + [256] * 8)
        pieces_of(A["w_out_2"], 8, [256] * 4)
        pieces_of(A["w_up_2"], 8, [512] * 8)
        pieces_of(A["w_down_2"], FT2, [512, 512])
        for g in range(2):
            for k in range(8):
                plan.append((A["w_pg"][k * P:(k + 1) * P, g * 512:g * 512 + 512], 512, None))
            for k in range(2):
                plan.append((A["w_pp"][k * P:(k + 1) * P, g * 512:g * 512 + 512], 512, None))

        class W:
            loaded = 0
            split = 0
            used = 0
            raw = {}
            ready = {}

        def load_piece():
            n = W.loaded
            if n >= len(plan):
                return
            r, free = raw_slots.take()
            src, width, _ = plan[n]
            dst = raws[r][:, 0:width]
            if len(src.shape) == 3:
                dst = dst.rearrange("p (k c) -> p k c", k=src.shape[1])
            t = sp.dma([free], raw_lots[r], sp.e.dma_start, dst, src)
            W.raw[n] = (r, t)
            W.loaded += 1

        def split_piece():
            n = W.split
            if n >= len(plan) or n - W.used >= NSPL:
                return
            while W.loaded <= n:
                load_piece()
            r, landed = W.raw.pop(n)
            width = plan[n][1]
            s, free = spl_slots.take()
            wh, wl = spls[s]
            raw = raws[r][:, 0:width]
            gain = plan[n][2]
            if gain is None:
                th = act.do([landed, free], act.e.activation, wh[:, 0:width], raw, ACT.Copy)
                eng = pool if n in on_pool else dve
                tl = eng.do([landed, free, th], eng.e.tensor_tensor, wl[:, 0:width], raw, wh[:, 0:width].bitcast(F32),
                            ALU.subtract)
            else:
                th = act.do([landed, free], act.e.activation, wh[:, 0:width], raw, ACT.Copy, scale=gain)
                tl = dve.do([landed, free, th], dve.e.scalar_tensor_tensor, wl[:, 0:width], raw, gain,
                            wh[:, 0:width].bitcast(F32), ALU.mult, ALU.subtract)
            raw_slots.give(r, th, tl)
            W.ready[n] = (s, th, tl)
            W.split += 1
            load_piece()

        def next_piece():
            while W.split <= W.used + (NSPL - 1) and W.split < len(plan) and W.split - W.used < NSPL:
                split_piece()
            n = W.used
            s, th, tl = W.ready.pop(n)
            return s, [th, tl]

        def done_piece(s, t):
            spl_slots.give(s, t)
            W.used += 1

        for _ in range(NRAW):
            load_piece()

        def mm3(bank_ap, wh, wl, xh, xl, first, last):
            pe.quiet([], pe.e.matmul, bank_ap, wh, xh, start=first, stop=False)
            pe.quiet([], pe.e.matmul, bank_ap, wh, xl, start=False, stop=False)
            return pe.do([], pe.e.matmul, bank_ap, wl, xh, start=False, stop=last)

        class Background:

            def __init__(self):
                self.tasks = []

            def add(self, task):
                self.tasks.append(task)
                self.advance(task)

            def advance(self, task):
                if next(task, "over") == "over":
                    self.tasks.remove(task)

            def step(self):
                for task in list(self.tasks):
                    self.advance(task)

            def until(self, ready):
                for _ in range(4000):
                    if ready():
                        return
                    self.step()
                assert ready()

            def finish(self):
                self.until(lambda: not self.tasks)

        bg = Background()

        def lane(tasks):
            for task in tasks:
                yield from task

        def gemm(widths, rhs, nk=KD, mid=None, pace=1):
            bg.until(lambda: len(B.free) >= len(widths))
            res = []
            for w in widths:
                b, free = B.take()
                res.append([b, free, None])
            for k in range(nk):
                xh, xl, t = rhs(k)
                s, ready = next_piece()
                wh, wl = spls[s]
                pe.wait(ready, t)
                o = 0
                for i, w in enumerate(widths):
                    b, free, _ = res[i]
                    if k == 0:
                        pe.wait(free)
                    last = mm3(b[0:w, :], wh[:, o:o + w], wl[:, o:o + w], xh, xl, k == 0, k == nk - 1)
                    res[i][2] = last
                    o += w
                done_piece(s, last)
                if mid is not None:
                    mid(k)
                for _ in range(pace):
                    bg.step()
            return [(b, t) for b, _, t in res]

        class Stat:

            def __init__(self):
                bg.until(lambda: len(B.free) >= 1)
                self.bank, self.free = B.take()
                self.last = None

            def add(self, sq, tok):
                for b in range(4):
                    first = self.last is None
                    self.last = pe.do([tok, self.free if first else None], pe.e.matmul, self.bank[:, b:b + 1],
                                      sq[:, b * P:(b + 1) * P], mean[:, 0:1], start=first, stop=True,
                                      skip_group_check=True)
                return self.last

            def root(self):
                a = dve.do([self.last, state["st_readers"]], dve.e.tensor_scalar, st[:, 0:4], self.bank[:, 0:4], EPS,
                           None, ALU.add)
                return a, rsqrt(st[:, 4:8], st[:, 0:4], st[:, 128:132], a)

            def column(self):
                a, r = self.root()
                B.give(self.bank, a)
                return r

            def half(self):
                self.diag = diagonal(st[:, 4:8], [self.root()[1]])
                state["st_readers"] = [self.diag]

            def spread(self):
                return broadcast(self.diag, (self.bank, []))

        def rsqrt(dst, src, power, tok):
            return pool.do([tok], pool.e.tensor_tensor, dst, src, power, ALU.pow)

        def diagonal(v, toks):
            return dve.do([toks, state["dg_readers"]], dve.e.tensor_tensor, DG[:, :, :],
                          ident[:, :].unsqueeze(1).to_broadcast([P, 4, P]), v.unsqueeze(2).to_broadcast([P, 4, P]),
                          ALU.mult)

        def broadcast(a, place=None):
            b, bf = B.take() if place is None else place
            a = pe.do([a, bf], pe.e.matmul, b[:, :], ones[:, :], DG[:, :, :].rearrange("p a b -> p (a b)"),
                      start=True, stop=True)
            state["dg_readers"] = [a]
            return b, a

        state = {"rb_readers": [], "h_readers": None, "m_readers": [], "st_readers": [], "dg_readers": []}

        def to_rb(bank, t):
            a = act.do([t, state["rb_readers"]], act.e.activation, RB[:, :], bank[:, :], ACT.Copy)
            B.give(bank, a)
            return a

        def square_into(dst, src, *toks):
            return act.do([*toks], act.e.activation, dst, src, ACT.Square)

        def parts(c, gname, xt):
            g = 1.0 if gname is None else col(gname, c)
            th = act.do([xt, state["h_readers"]], act.e.activation, Hh[:, c, :], X[:, c, :], ACT.Copy, scale=g)
            tl = dve.do([xt, th, state["h_readers"]], dve.e.scalar_tensor_tensor, Hl[:, c, :], X[:, c, :], g,
                        Hh[:, c, :].bitcast(F32), ALU.mult, ALU.subtract)
            return [th, tl]

        class Input:

            def __init__(self, gname):
                self.parts, self.sq, self.x, self.sums = [], [], [], []
                self.make, self.gname = state["x"], gname
                self.ahead(1)
                state["x"] = lambda c: self.x[c]

            def ahead(self, n):
                while len(self.parts) < min(n, KD):
                    c = len(self.parts)
                    while len(self.x) < min(c + 3, KD):
                        self.x.append(self.make(len(self.x)))
                    self.parts.append(parts(c, self.gname, self.x[c]))

            def squares(self, n):
                while len(self.sq) < min(n, KD):
                    c = len(self.sq)
                    a = square_into(M[:, c, :], X[:, c, :], self.x[c], state["m_readers"])
                    self.sq.append(a)
                    if c % 4:
                        a = pool.do([a, self.sums[-1]], pool.e.tensor_tensor, M[:, c - c % 4, :],
                                    M[:, c - c % 4, :], M[:, c, :], ALU.add)
                        self.sums[-1] = a
                    else:
                        self.sums.append(a)

            def rhs(self, k):
                self.ahead(k + 4)
                self.squares(k + 2)
                return Hh[:, k, :], Hl[:, k, :], self.parts[k]

            def rms(self, k):
                if k == 6:
                    s = Stat()
                    for i in range(2):
                        last = s.add(M[:, 4 * i, :], self.sums[i])
                    state["m_readers"] = [last]
                    self.counted = last
                    s.half()
                    self.stat = s
                elif k == 7:
                    self.rb = to_rb(*self.stat.spread())

        def residual(mt, stat, gname):
            stat.half()
            bank, r = stat.spread()

            def make(c):
                g = col(gname, c)
                a = dve.do([r, mt[c]], dve.e.scalar_tensor_tensor, M[:, c, :], M[:, c, :], g, bank[:, :], ALU.mult,
                           ALU.mult)
                if c == KD - 1:
                    B.give(bank, a)
                eng = dve if c in (0,1,5) else pool
                x = eng.do([a, state["x_readers"]], eng.e.tensor_tensor, X[:, c, :], X[:, c, :], M[:, c, :],
                           ALU.add)
                state["m_readers"] = [state["m_readers"], x]
                return x

            state["m_readers"] = []
            state["x"] = make

        state["x"] = lambda c: x_loaded[c]
        state["x_readers"] = []

        def evac_m(group, c0, scale=None):
            toks, held, sq = [], [], []
            for i, (b, t) in enumerate(group):
                g = 1.0 if scale is None else col(scale, c0 + i)
                q, qf = T.take()
                sq.append((q, act.do([t, qf], act.e.activation, q[:, 2:TW], b[:, :], ACT.Square, scale=g)))
            for i, (b, t) in enumerate(group):
                c = c0 + i
                g = 1.0 if scale is None else col(scale, c)
                a = dve.do([sq[i][1], state["m_readers"]], dve.e.tensor_scalar, M[:, c, :], b[:, :], g, None, ALU.mult)
                B.give(b, a)
                toks.append(a)
                if i % 2:
                    (p, pt_), (q, qt_) = sq[i - 1], sq[i]
                    a = dve.do([pt_, qt_], dve.e.tensor_tensor, p[:, 2:TW], p[:, 2:TW], q[:, 2:TW], ALU.add)
                    T.give(q, a)
                    held.append((p, a))
            return toks, held

        def count_squares(stat, held):
            for q, s in held:
                T.give(q, stat.add(q[:, 2:TW], s))

        def merged(held):
            (p, pt_), (q, qt_) = held
            a = pool.do([pt_, qt_], pool.e.tensor_tensor, p[:, 2:TW], p[:, 2:TW], q[:, 2:TW], ALU.add)
            T.give(q, a)
            return [(p, a)]

        def closing_gemm(rhs, nk, gname, groups, pace=1):
            mt, held, box = [], [], {}

            def mid(k):
                if k == 4:
                    box["s"] = Stat()
                    count_squares(box["s"], held)

            for i, n in enumerate(groups):
                res = gemm([P] * n, rhs, nk, mid if i == len(groups) - 1 else None, pace=pace)
                bg.until(lambda: len(T.free) >= n)
                m, new = evac_m(res, len(mt))
                mt += m
                if i == len(groups) - 1:
                    count_squares(box["s"], new)
                else:
                    held += new
                    while len(held) > 1:
                        held = merged(held[0:2]) + held[2:]
            residual(mt, box["s"], gname)

        def ffn(n, groups, gname, both, func, ntile, post):
            AHn = at(f"AH{n}", [P, ntile, S], arena, F32R)
            ALn = at(f"AL{n}", [P, ntile, S], arena + ntile * S * 4, F32R)
            inp = Input(gname)
            cw, cb = (COLS[x][0] for x in (f"cw{n}", f"cb{n}"))
            nct = {0: 44, 1: 44, 2: 16}[n]
            at_toks = {}
            arena_free = state["arena_readers"]

            def after(g, res):
                us, tu = [], []
                for i in range(4):
                    b, t = res[i]
                    u, uf = T.take()
                    a = dve.do([t, inp.rb, uf], dve.e.tensor_tensor, u[:, 2:TW], b[:, :], RB[:, :], ALU.mult)
                    B.give(b, a)
                    us.append(u)
                    tu.append(a)
                state["rb_readers"] = [a]
                yield
                todo = range(4) if both else range(2)
                idx = [2 * g, 2 * g + 1, ntile + 2 * g, ntile + 2 * g + 1]
                cs = {}
                for i in todo:
                    c, cf = T.take()
                    o = cw + 2 * nct + idx[i]
                    a = act.do([tu[i], cf], act.e.activation, c[:, 2:TW], us[i][:, 2:TW], ACT.Identity,
                               bias=cols[:, cb + idx[i]:cb + idx[i] + 1], scale=cols[:, o:o + 1])
                    cs[i] = (c, a)
                yield
                for k in (1, 0):
                    for i in todo:
                        c, a = cs[i]
                        o = cw + k * nct + idx[i]
                        a = dve.do([a], dve.e.scalar_tensor_tensor, c[:, 2:TW], us[i][:, k:TW - 2 + k],
                                   cols[:, o:o + 1], c[:, 2:TW], ALU.mult, ALU.add)
                        cs[i] = (c, a)
                        if k == 0:
                            T.give(us[i], a)
                            us[i], tu[i] = c, a
                    yield
                for i in range(2):
                    tu[i] = act.do([tu[i]], act.e.activation, us[i][:, 2:TW], us[i][:, 2:TW], func)
                yield
                for i in range(2):
                    u, v = us[i], us[2 + i]
                    tu[i] = pool.do([tu[i], tu[2 + i]], pool.e.tensor_tensor, u[:, 2:TW], u[:, 2:TW], v[:, 2:TW],
                                    ALU.mult)
                    T.give(v, tu[i])
                yield
                for i in range(2):
                    f, u = 2 * g + i, us[i]
                    h = act.do([tu[i], arena_free], act.e.activation, AHn[:, f, :], u[:, 2:TW], ACT.Copy)
                    l = dve.do([tu[i], h, arena_free], dve.e.tensor_tensor, ALn[:, f, :], u[:, 2:TW],
                               AHn[:, f, :].bitcast(F32), ALU.subtract)
                    T.give(u, l, h)
                    at_toks[f] = [h, l]

            for g in range(groups):
                res = gemm([P] * 4, inp.rhs, mid=inp.rms if g == 0 else None)
                bg.until(lambda: len(T.free) >= 8)
                bg.add(after(g, res))
            state["h_readers"] = (pe, pe.count)

            if n == 0:
                bg.add(rotation())

            def rhs(f):
                bg.until(lambda: f in at_toks)
                return AHn[:, f, :], ALn[:, f, :], at_toks[f]

            if post is None:
                added_gemm(rhs, ntile, inp)
            else:
                closing_gemm(rhs, ntile, post, [4, 4])
            state["arena_readers"] = [(pe, pe.count)]

        def added_gemm(rhs, nk, inp, pace=1, n=4):
            xt = []
            for g in range(8 // n):
                for i, (b, t) in enumerate(gemm([P] * n, rhs, nk, pace=pace)):
                    c = n * g + i
                    x = dve.do([t, inp.sq[c], inp.parts[c]], dve.e.tensor_tensor, X[:, c, :], b[:, :], X[:, c, :],
                               ALU.add)
                    B.give(b, x)
                    xt.append(x)
            state["x"] = lambda c: xt[c]

        state["arena_readers"] = []

        def sub(name, shape, off, dt=F32):
            return at(name, shape, arena + off, dt)

        def pool_mixer():
            band = sub("band", [P, 4, 272], 0)
            Z = sub("Z", [P, 4, D], 4608)
            o = CONST["band"][0]
            dk = act.dma([], lot("s_band"), act.e.dma_start, band[:, :, :].rearrange("p g n -> p (g n)"),
                         A["const"][:, o:o + 1088])
            toks, sums = [], []
            for c in range(KD):
                toks.append(parts(c, "mix_pre0", x_loaded[c]))
                if c in (1, 3):
                    split_piece()
            for c in range(KD):
                if c % 2 == 0:
                    was = act.do([x_loaded[c]], act.e.activation, M[:, c, :], X[:, c, :], ACT.Square)
                else:
                    t = dve.do([x_loaded[c]], dve.e.tensor_tensor, M[:, c, :], X[:, c, :], X[:, c, :], ALU.mult)
                    sums.append(pool.do([t, was], pool.e.tensor_tensor, M[:, c - 1, :], M[:, c - 1, :], M[:, c, :],
                                        ALU.add))
            stat = Stat()
            r, zt = None, []
            for pair in range(2):
                got = []
                for g in (2 * pair, 2 * pair + 1):
                    sl, ready = next_piece()
                    wh, wl = spls[sl]
                    pe.wait(ready, toks[2 * g], toks[2 * g + 1])
                    for n in range(4):
                        if g % 2 == 0:
                            got.append(B.take())
                            pe.wait(got[n][1])
                        for k in range(2):
                            c = 2 * g + k
                            o = 256 * (g % 2)
                            t = mm3(got[n][0][:, o:o + 256], Hh[:, c, n * P:(n + 1) * P], Hl[:, c, n * P:(n + 1) * P],
                                    wh[:, k * 256:k * 256 + 256], wl[:, k * 256:k * 256 + 256], k == 0, k == 1)
                    done_piece(sl, t)
                if pair == 0:
                    for i in range(4):
                        last = stat.add(M[:, 2 * i, :], sums[i])
                    r = stat.column()
                for n in range(4):
                    b = got[n][0]
                    z, f = Z[:, n, pair * 512:pair * 512 + 512], st[:, 4 + n:5 + n]
                    if n % 2 == 0:
                        a = act.do([t, r], act.e.activation, z, b[:, :], ACT.Copy, scale=f)
                    else:
                        a = dve.do([t, r], dve.e.tensor_scalar, z, b[:, :], f, None, ALU.mult)
                    B.give(b, a)
                    zt.append(a)
            state["st_readers"] = zt
            state["m_readers"] = [last]
            mt, stat = [], Stat()
            for g in range(4):
                res = []
                for m in range(2):
                    b, bf = B.take()
                    o = g * 256 + m * P
                    pe.wait(bf, dk, zt[0:4] if g < 2 else zt)
                    for n in range(4):
                        f = 0 if n == 0 else P
                        t = pe.do([], pe.e.matmul, b[:, n * P:(n + 1) * P], Z[:, n, o:o + P], band[:, g, f:f + P],
                                  start=True, stop=n == 0, skip_group_check=True)
                        if n > 0:
                            t = pe.do([], pe.e.matmul, b[:, n * P:n * P + 16], Z[:, n - 1, o:o + P],
                                      band[:, g, 256:272], start=False, stop=True, skip_group_check=True)
                    res.append((b, t))
                if g > 0:
                    count_squares(stat, held)
                m_, held = evac_m(res, 2 * g, "pool_scale")
                mt += m_
            count_squares(stat, held)
            state["h_readers"] = (pe, pe.count)
            state["arena_readers"] = [(pe, pe.count)]
            residual(mt, stat, "mix_post0")

        def rotation():
            while len(T.free) < 7:
                yield
            got = [T.take() for _ in range(5)]
            p_, a_, y_, c_, s_ = (g[0][:, 2:TW] for g in got)
            posi = p_.bitcast(I32)
            a = act.dma([g[1] for g in got], lot("s_pos"), act.e.dma_start, posi, A["pos"])
            yield
            a = dve.do([a], dve.e.tensor_copy, y_, posi)
            a = dve.do([a], dve.e.tensor_scalar, a_, y_, col("invf", 0), None, ALU.mult)
            yield
            r = None
            for turn, dst in ((0.0, s_), (0.25, c_)):
                b = dve.do([a, r], dve.e.tensor_scalar, y_, a_, 1.0 / (2 * math.pi), turn, ALU.mult, ALU.add)
                b = dve.do([b], dve.e.tensor_scalar, y_, y_, MAGIC, None, ALU.add)
                yield
                b = dve.do([b], dve.e.tensor_scalar, y_, y_, MAGIC, None, ALU.subtract)
                src = a_
                for part in (PI_HI, PI_MID, PI_LO):
                    b = dve.do([b, r], dve.e.scalar_tensor_tensor, p_, y_, -part, src, ALU.mult, ALU.add)
                    src = p_
                    yield
                b = dve.do([b], dve.e.tensor_scalar, p_, p_, turn * 2 * math.pi, 3.1415925, ALU.add, ALU.min)
                b = dve.do([b], dve.e.tensor_scalar, p_, p_, -3.1415925, None, ALU.max)
                yield
                r = act.do([b], act.e.activation, dst, p_, ACT.Sin)
            for g in got[0:3]:
                T.give(g[0], r)
            state["trig"] = (got[3][0], got[4][0], r)

        def window_mixer():
            q = sub("wq", [P, 8, S], 0)
            k_ = sub("wk", [P, 2, S], 16384)
            v_ = sub("wv", [P, 2, S], 20480)
            vt_ = sub("wvt", [P, 4, 256], 24576)
            mask = sub("wmask", [P, 256], 40960)
            Sb = [sub(f"wSb{i}", [P, 4, 256], 43008 + 4096 * i) for i in range(5)]
            PT = [sub(f"wPT{i}", [P, 8, P], 63488 + 4096 * i) for i in range(5)]
            sm = [sub(f"wsm{i}", [P, 32], 83968 + 128 * i) for i in range(5)]
            af = state["arena_readers"]
            lm = lot("s_mask")
            o = CONST["swa"][0]
            dm = act.dma([af], lm, act.e.dma_start, mask[:, :], A["const"][:, o:o + 256])
            inp = Input(None)
            cst, snt, trig = state["trig"]
            cs, sn = cst[:, 2:TW], snt[:, 2:TW]
            res = gemm([P] * 4, inp.rhs, mid=inp.rms)
            rb = inp.rb
            t1 = dve.do([trig, rb], dve.e.tensor_tensor, cs, cs, RB[:, :], ALU.mult)
            t2 = dve.do([trig, rb], dve.e.tensor_tensor, sn, sn, RB[:, :], ALU.mult)

            def rotate(ra, rbk, dst, scale):
                (a, at_), (b, bt) = ra, rbk
                out_ = []
                tmp = []
                for src, st_, tab, tt in ((a, at_, cs, t1), (b, bt, sn, t2), (b, bt, cs, t1), (a, at_, sn, t2)):
                    x, xf = T.take()
                    if scale == 1.0:
                        y = dve.do([st_, tt, xf], dve.e.tensor_tensor, x[:, 2:TW], src[:, :], tab, ALU.mult)
                    else:
                        y = dve.do([st_, tt, xf], dve.e.scalar_tensor_tensor, x[:, 2:TW], src[:, :], scale,
                                   tab, ALU.mult, ALU.mult)
                    tmp.append((x, y))
                B.give(a, tmp[3][1])
                B.give(b, tmp[2][1])
                for i, half, op in ((0, 0, ALU.subtract), (2, 1, ALU.add)):
                    (x, xt_), (y, yt_) = tmp[i], tmp[i + 1]
                    ends = []
                    for j in range(4):
                        r0 = 64 * (j % 2) + 32 * half
                        eng = (dve, pool)[j % 2]
                        ends.append(eng.do([xt_, yt_, af], eng.e.tensor_tensor, dst[r0:r0 + 32, j // 2, :],
                                           x[32 * j:32 * j + 32, 2:TW], y[32 * j:32 * j + 32, 2:TW], op))
                    T.give(x, ends)
                    T.give(y, ends)
                    out_.append(ends)
                return out_

            kt = rotate(res[0], res[1], k_, 0.125)
            vts = []
            for i in range(2):
                b, t = res[2 + i]
                a = dve.do([t, rb, af], dve.e.tensor_tensor, v_[:, i, :], b[:, :], RB[:, :], ALU.mult)
                B.give(b, a)
                vts.append(a)
            state["rb_readers"] = [a]
            qt, vtok_t = [], []
            SB = Slots(list(range(5)))
            so = COLS["sinks"][0]
            done = {p: [] for p in range(4)}

            def attend(p, n):
                k0 = 128 * max(n - 1, 0)
                nk = 128 * (n + 1) - k0
                mo = 256 - nk
                nb = nk // P
                while len(B.free) < 2 or not SB.free or len(qt) <= p or not vtok_t:
                    yield
                z, zf = SB.take()
                sx, sc, pt = Sb[z], sm[z], PT[z]
                sbk = [B.take() for j in range(2)]
                sts = []
                for j in range(4):
                    b, bf = sbk[j % 2]
                    r0 = 64 * (j % 2)
                    o = 256 * (j // 2)
                    sts.append(pe.do([bf, qt[p], kt], pe.e.matmul, b[:, o:o + nk],
                                     q[r0:r0 + 64, 2 * p + j // 2, n * P:(n + 1) * P],
                                     k_[r0:r0 + 64, j // 2, k0:k0 + nk], start=True, stop=True,
                                     skip_group_check=True))
                qread = sts[-1]
                yield
                for j in range(4):
                    b, o = sbk[j % 2][0], 256 * (j // 2)
                    a = dve.do([sts[2 + j % 2], dm, zf], dve.e.tensor_tensor_reduce, sx[:, j, 0:nk],
                               b[:, o:o + nk], mask[:, mo:256], 1.0, -3e38, ALU.add, ALU.max, sc[:, j:j + 1])
                    if j > 1:
                        B.give(b, a)
                sk = cols[:, so + 4 * p:so + 4 * p + 4]
                a = dve.do([a], dve.e.tensor_tensor, sc[:, 4:8], sc[:, 0:4], sk, ALU.max)
                a = dve.do([a], dve.e.tensor_scalar, sc[:, 8:12], sc[:, 4:8], -1.0, None, ALU.mult)
                b2 = dve.do([a], dve.e.tensor_tensor, sc[:, 12:16], sc[:, 8:12], sk, ALU.add)
                yield
                for j in range(4):
                    x = act.do([a], act.e.activation, sx[:, j, 0:nk], sx[:, j, 0:nk], ACT.Exp, bias=sc[:, 8 + j:9 + j],
                               accum_out=sc[:, 16 + j:17 + j])
                x = act.do([b2], act.e.activation, sc[:, 20:24], sc[:, 12:16], ACT.Exp)
                yield
                a = dve.do([x], dve.e.tensor_tensor, sc[:, 24:28], sc[:, 16:20], sc[:, 20:24], ALU.add)
                a = dve.do([a], dve.e.reciprocal, sc[:, 28:32], sc[:, 24:28])
                for j in range(4):
                    a = dve.do([a], dve.e.tensor_scalar, sx[:, j, 0:nk], sx[:, j, 0:nk], sc[:, 28 + j:29 + j], None,
                               ALU.mult)
                yield
                while len(B.free) < nb + 1:
                    yield
                ob, obf = B.take()
                tb_ = []
                for kb in range(nb):
                    b, bf = B.take()
                    for j in range(4):
                        t = pe.do([bf, a], pe.e.transpose, b[:, j * P:(j + 1) * P], sx[:, j, kb * P:(kb + 1) * P],
                                  ident[:, :])
                    tb_.append((b, t))
                yield
                pts = []
                for kb in range(nb):
                    b, t = tb_[kb]
                    src = b[:, :].rearrange("p (j c) -> p j c", j=4)
                    if kb == 0:
                        c = act.do([t, zf], act.e.activation, pt[:, 0:4, :], src, ACT.Copy)
                    else:
                        c = act.do([t, zf], act.e.activation, pt[:, 4:8, :], src, ACT.Copy)
                    B.give(b, c)
                    pts.append(c)
                yield
                for j in range(4):
                    o = (j // 2) * P
                    r0 = 64 * (j % 2)
                    for kb in range(nb):
                        blk = k0 // P + kb
                        t = pe.do([pts, vtok_t, obf], pe.e.matmul, ob[r0:r0 + 64, o:o + P],
                                  vt_[:, blk, j * 64:(j + 1) * 64], pt[:, 4 * kb + j, :], start=kb == 0,
                                  stop=kb == nb - 1, skip_group_check=True)
                SB.give(z, t)
                yield
                o = act.do([t, qread], act.e.activation, q[:, 2 * p:2 * p + 2, n * P:(n + 1) * P],
                           ob[:, 0:256].rearrange("p (c t) -> p c t", c=2), ACT.Copy)
                B.give(ob, o)
                done[p].append(o)

            def pairs(which):
                for i in range(which, 16, 5):
                    yield from attend(i // 4, i % 4)

            for i in range(5):
                bg.add(pairs(i))
            for g in range(2):
                res = gemm([P] * 4, inp.rhs, pace=1 if g else 1)
                for i in range(2):
                    p = 2 * g + i
                    qt.append(rotate(res[2 * i], res[2 * i + 1], q[:, 2 * p:2 * p + 2, :], 1.0))
                if g == 0:
                    last = []
                    for i in range(2):
                        b, bf = B.take()
                        for n in range(4):
                            t = pe.do([bf, vts[i]], pe.e.transpose, b[:, n * P:(n + 1) * P],
                                      v_[:, i, n * P:(n + 1) * P], ident[:, :])
                        vtok = act.do([t], act.e.activation, vt_[:, :, i * P:(i + 1) * P],
                                      b[:, :].rearrange("p (n c) -> p n c", n=4), ACT.Copy)
                        B.give(b, vtok)
                        last.append(vtok)
                    vtok_t.append(last)
            T.give(cst, (dve, dve.count))
            T.give(snt, (dve, dve.count))
            state["h_readers"] = (pe, pe.count)
            hr = state["h_readers"]
            ht = {}

            def rhs(c):
                p = c // 2
                if c not in ht:
                    bg.until(lambda: len(done[p]) == 4)
                    h = act.do([done[p], hr], act.e.activation, Hh[:, c, :], q[:, c, :], ACT.Copy)
                    l = dve.do([h, done[p], hr], dve.e.tensor_tensor, Hl[:, c, :], q[:, c, :],
                               Hh[:, c, :].bitcast(F32), ALU.subtract)
                    ht[c] = [h, l]
                return Hh[:, c, :], Hl[:, c, :], ht[c]

            closing_gemm(rhs, KD, "mix_post1", [2, 2, 2, 2], pace=1)
            state["h_readers"] = (pe, pe.count)
            state["arena_readers"] = [(pe, pe.count), (dve, dve.count), (act, act.count), (pool, pool.count)]

        def second_mixer():
            af = state["arena_readers"]
            big = sub("b_big", [P, 26, S], 0)
            KCR, VCR, KS, VS, KW, VW, Q2, MQ, MK, MV, MO = 0, 1, 2, 3, 4, 5, 6, 10, 14, 18, 22
            o = 26 * 2048
            bias = sub("b_bias", [P, 8, S], o)
            o += 16384
            vtok = sub("b_vtok", [P, 2, 4, P], o)
            o += 4096
            mvt = sub("b_mvt", [P, 4, 4, P], o)
            blk = [at(f"b_blk{i}", [P, 16, 62], arena + o + 4096 * i) for i in range(2)]
            o += 8192
            pe2 = sub("b_pe", [P, 2, 2, 16], o)
            w2 = sub("b_w2", [P, 2, 64], o + 256)
            hid = sub("b_hid", [P, 2, 64], o + 768)
            kct = sub("b_kct", [P, 32], o + 1280)
            vct = sub("b_vct", [32, 2, 64], o + 1408)
            cb = sub("b_cb", [P, 4, 8, 31], o + 1920)
            gsig = sub("b_gsig", [P, 4, 24], o + 5888)
            assert o + 6272 <= 2 * FT * 2048, o
            w1 = [at(f"b_w1{i}", [P, 16, P], m_at + 8192 * i) for i in range(2)]
            Sb = [at(f"b_Sb{i}", [P, 4, S], m_at + 8192 * i) for i in range(2)]
            inp = Input("ln1")
            lots = [lot(f"s_b{i}") for i in range(6)]
            dist = at("b_dist", [P, S], arena + MO * 2048)
            cmpc = at("b_cmp", [P, 124], arena + (MO + 1) * 2048)
            def const(name):
                c, w = CONST[name]
                return A["const"][:, c:c + w]
            d_dist = act.dma([af], lots[0], act.e.dma_start, dist[:, :], const("dist"))
            d_cmp = act.dma([af], lots[1], act.e.dma_start, cmpc[:, :], const("cmp"))
            d_sel = act.dma([], lot("s_sel"), act.e.dma_start, rows[:, 0, :],
                            A["const"][0:4, CONST["sel"][0]:CONST["sel"][0] + 512])
            d_pe = act.dma([af], lots[2], act.e.dma_start, pe2[:, :, :, :], A["cmp_pe"])
            d_w2 = act.dma([af], lots[3], act.e.dma_start, w2[:, :, :], A["cmp_w2"])
            box = {}
            tk = {}

            def scaled(i, b, t, scale, eng=None, extra=None):
                if scale == 1.0:
                    a = dve.do([t, box["rb"], af, extra], dve.e.tensor_tensor, big[:, i, :], b[:, :], RB[:, :],
                               ALU.mult)
                else:
                    a = dve.do([t, box["rb"], af, extra], dve.e.scalar_tensor_tensor, big[:, i, :], b[:, :], scale,
                               RB[:, :], ALU.mult, ALU.mult)
                B.give(b, a)
                tk[i] = a
                return a

            def to_tokens(src, dst, t, eng):
                b, bf = B.take()
                for n in range(4):
                    a = pe.do([bf, t], pe.e.transpose, b[:, n * P:(n + 1) * P], big[:, src, n * P:(n + 1) * P],
                              ident[:, :])
                a = act.do([a, af], act.e.activation, dst, b[:, :].rearrange("p (n c) -> p n c", n=4), ACT.Copy)
                B.give(b, a)
                return a

            res = gemm([P] * 4, inp.rhs, mid=inp.rms)
            box["rb"] = inp.rb
            box["sq"] = inp.counted
            dw1 = [act.dma([box["sq"]], lots[4 + i], act.e.dma_start, w1[i][:, :, :],
                           A["cmp_w1"][i].rearrange("(c p) m -> p c m", p=P)) for i in range(2)]
            for i, (b, t) in enumerate(res):
                scaled((KCR, VCR, KS, VS)[i], b, t, 1.0)
            bt = []

            def slopes():
                for h in range(8):
                    pool.do([d_dist, af], pool.e.tensor_scalar, bias[:, h, :], dist[:, :], SLOPES[h], None, ALU.mult)
                    a = pool.do([d_cmp, af], pool.e.tensor_scalar, cb[:, :, h, :],
                                cmpc[:, :].rearrange("p (b n) -> p b n", b=4), SLOPES[h], None, ALU.mult)
                    yield
                bt.append(a)

            bg.add(slopes())
            bl = []
            for i in range(2):
                for g in range(2):
                    for par in range(2):
                        src = big[64 * g:64 * g + 64, i, :]
                        a0 = src.rearrange("p (n c r) -> p n c r", c=8, r=2)[:, :, :, par]
                        for hf in range(2):
                            a = dve.do([tk[i], d_pe, af], dve.e.tensor_tensor,
                                       blk[i][64 * par:64 * par + 64, 8 * hf:8 * hf + 8, 31 * g:31 * g + 31],
                                       a0[:, hf:hf + 31, :].rearrange("p n c -> p c n"),
                                       pe2[64 * g:64 * g + 64, i, par, 8 * hf:8 * hf + 8].unsqueeze(2).to_broadcast( [64, 8, 31]),
                                       ALU.add)
                            bl.append(a)
            res = gemm([P] * 4, inp.rhs, pace=2)
            for i, (b, t) in enumerate(res):
                scaled((KW, VW, Q2, Q2 + 1)[i], b, t, 1.0 if i < 2 else 0.125)
            box["kv"] = None

            def compression():
                while len(B.free) < 1:
                    yield
                hb, hbf = B.take()
                for i in range(2):
                    for c in range(16):
                        t = pe.do([hbf, dw1[i], bl], pe.e.matmul, hb[:, 64 * i:64 * i + 62], w1[i][:, c, :],
                                  blk[i][:, c, :], start=c == 0, stop=c == 15, skip_group_check=True)
                        if c % 4 == 3:
                            yield
                hidt = t
                a = act.do([t, af], act.e.activation, hid[:, :, 0:62],
                           hb[:, 0:128].rearrange("p (i n) -> p i n", i=2)[:, :, 0:62], ACT.Gelu_apprx_tanh)
                yield
                t = pe.do([a, d_w2], pe.e.matmul, hb[0:64, 0:62], w2[:, 0, :], hid[:, 0, 0:62], start=True,
                          stop=True, skip_group_check=True)
                for g in range(2):
                    t = pe.do([a, d_w2], pe.e.matmul, hb[0:31, 128 + 64 * g:192 + 64 * g],
                              hid[:, 1, 31 * g:31 * g + 31], w2[:, 1, :], start=True, stop=True,
                              skip_group_check=True)
                yield
                k0 = dve.do([t, af], dve.e.tensor_copy, kct[0:64, 0:31], hb[0:64, 0:31])
                k1 = dve.do([t, af], dve.e.tensor_copy, kct[64:128, 0:31], hb[0:64, 31:62])
                vc = dve.do([t, af], dve.e.tensor_copy, vct[0:31, :, :],
                            hb[0:31, 128:256].rearrange("p (g d) -> p g d", g=2))
                B.give(hb, k0, k1, vc)
                vs = []
                for i in range(2):
                    while len(B.free) < 1:
                        yield
                    vs.append(to_tokens((VS, VW)[i], vtok[:, i, :, :], tk[(VS, VW)[i]], act))
                    yield
                box["kv"] = (hidt, [k0, k1, vc], vs)

            bg.add(compression())
            res = gemm([P, P, 88], inp.rhs, pace=3)
            bg.until(lambda: box["kv"] is not None and bt)
            biast = bt[-1]
            hidt, cmpt, (vst, vwt) = box["kv"]
            scaled(Q2 + 2, res[0][0], res[0][1], 0.125)
            scaled(Q2 + 3, res[1][0], res[1][1], 0.125)
            gb, gt = res[2]
            zi, zif = T.take()
            zf, zff = T.take()
            za, zaf = T.take()
            a0 = dve.do([gt, box["rb"], zif], dve.e.tensor_tensor, zi[0:4, 2:TW], gb[0:4, :], RB[0:4, :], ALU.mult)
            a1 = dve.do([gt, zff], dve.e.tensor_tensor, zf[0:4, 2:TW], gb[32:36, :], RB[32:36, :], ALU.mult)
            a2 = dve.do([gt, zaf], dve.e.tensor_tensor, za[0:24, 2:TW], gb[64:88, :], RB[64:88, :], ALU.mult)
            B.give(gb, a2)
            b, bf = B.take()
            for n in range(4):
                t = pe.do([bf, a2], pe.e.transpose, b[:, 24 * n:24 * n + 24], za[0:24, 2 + n * P:2 + (n + 1) * P],
                          ident[0:24, 0:24])
            a = act.do([t, af], act.e.activation, gsig[:, :, :], b[:, 0:96].rearrange("p (n c) -> p n c", n=4),
                       ACT.Sigmoid)
            gc = dve.do([a], dve.e.tensor_scalar, gsig[:, 0, 0:24:3], gsig[:, 0, 0:24:3], col("rv", 0), None,
                        ALU.mult)
            gt_ = [a, gc]
            B.give(b, a)
            T.give(za, t)
            gbo = COLS["gbias"][0]
            lf, lff = T.take()
            l1, l1f = T.take()
            on, onf = T.take()
            R = lambda x: x[0:4, 2:TW]
            gcol = st[:, 32:48]
            emc = st[:, 48:64]

            def gates():
                i1 = dve.do([a0], dve.e.tensor_scalar, R(zi), R(zi), cols[0:4, gbo:gbo + 1], None, ALU.add)
                f1 = dve.do([a1], dve.e.tensor_scalar, R(zf), R(zf), cols[0:4, gbo + 1:gbo + 2], None, ALU.add)
                yield
                a = act.do([f1, l1f], act.e.activation, R(l1), R(zf), ACT.Abs)
                a = act.do([a], act.e.activation, R(l1), R(l1), ACT.Exp, scale=-1.0)
                a = act.do([a], act.e.activation, R(l1), R(l1), ACT.Ln, bias=1.0)
                yield
                a = dve.do([a, lff], dve.e.scalar_tensor_tensor, R(lf), R(zf), 0.0, R(l1), ALU.min, ALU.subtract)
                c = dve.do([onf], dve.e.memset, R(on), 1.0)
                yield
                a = dve.do([a, c], dve.e.tensor_tensor_scan, R(zf), R(on), R(lf), 0.0, ALU.mult, ALU.add)
                T.give(on, a)
                yield
                g_ = dve.do([a, i1], dve.e.tensor_tensor, R(zi), R(zi), R(zf), ALU.subtract)
                m_ = dve.do([g_], dve.e.tensor_tensor_scan, R(lf), R(zi), R(zi), 0.0, ALU.max, ALU.max)
                nm = dve.do([m_], dve.e.scalar_tensor_tensor, R(l1), R(zf), -1.0, R(lf), ALU.mult, ALU.subtract)
                nM = dve.do([m_, nm], dve.e.tensor_scalar, rows[:, 1, :], R(lf), -1.0, None, ALU.mult)
                T.give(lf, nM)
                T.give(zf, nm)
                yield
                while len(B.free) < 1:
                    yield
                b, bf = B.take()
                for n in range(4):
                    t = pe.do([bf, g_], pe.e.transpose, b[:, 4 * n:4 * n + 4], zi[0:4, 2 + n * P:2 + (n + 1) * P],
                              ident[0:4, 0:4])
                for n in range(4):
                    t = pe.do([nm], pe.e.transpose, b[:, 16 + 4 * n:20 + 4 * n], l1[0:4, 2 + n * P:2 + (n + 1) * P],
                              ident[0:4, 0:4])
                gct = act.do([t], act.e.activation, gcol, b[:, 0:16], ACT.Copy)
                emt = act.do([t], act.e.activation, emc, b[:, 16:32], ACT.Exp)
                B.give(b, emt)
                T.give(zi, t)
                T.give(l1, t)
                box["gates"] = (nM, gct, emt)

            bg.add(gates())
            U = Slots([0, 1])
            CP = Slots([(KCR, VCR), (VS, VW)])
            CP.free = [(CP.free[0][0], [(dve, dve.count)]), (CP.free[1][0], [vst, vwt])]
            comp = {}
            qt = [tk[Q2 + r] for r in range(4)]
            ot = {r: [] for r in range(4)}
            left = {tb: 4 for tb in range(4)}
            crd = {tb: [] for tb in range(4)}

            def compressed(tb):
                while not CP.free:
                    yield
                pl, plf = CP.take()
                ready = []
                for g in range(2):
                    cmx, csum, cfac = (st[:, 80 + 4 * k:84 + 4 * k] for k in range(3))
                    while len(B.free) < 1 or len(T.free) < 1:
                        yield
                    b, bf = B.take()
                    pc, pcf = T.take()
                    for r in range(4):
                        t = pe.do([bf, qt, cmpt], pe.e.matmul, b[:, 31 * r:31 * r + 31],
                                  big[64 * g:64 * g + 64, Q2 + r, tb * P:(tb + 1) * P], kct[64 * g:64 * g + 64, 0:31],
                                  start=True, stop=True, skip_group_check=True)
                    yield
                    pv = pc[:, 2:126].rearrange("p (r n) -> p r n", r=4)
                    a = dve.do([t, biast, pcf], dve.e.tensor_tensor, pv,
                               b[:, 0:124].rearrange("p (r n) -> p r n", r=4), cb[:, tb, 4 * g:4 * g + 4, :], ALU.add)
                    B.give(b, a)
                    a = dve.do([a], dve.e.tensor_reduce, cmx, pv, AX, ALU.max)
                    a = dve.do([a], dve.e.tensor_tensor, pv, pv, cmx.unsqueeze(2).to_broadcast([P, 4, 31]),
                               ALU.subtract)
                    yield
                    a = act.do([a], act.e.activation, pc[:, 2:126], pc[:, 2:126], ACT.Exp)
                    yield
                    a = dve.do([a], dve.e.tensor_reduce, csum, pv, AX, ALU.add)
                    a = dve.do([a], dve.e.reciprocal, cfac, csum)
                    a = dve.do([a, gt_], dve.e.tensor_tensor, cfac, cfac, gsig[:, tb, 12 * g:12 * g + 12:3], ALU.mult)
                    a = dve.do([a], dve.e.tensor_tensor, pv, pv, cfac.unsqueeze(2).to_broadcast([P, 4, 31]),
                               ALU.mult)
                    yield
                    while len(B.free) < 1:
                        yield
                    b, bf = B.take()
                    for r in range(4):
                        t = pe.do([bf, a], pe.e.transpose, b[0:31, r * P:(r + 1) * P], pc[:, 2 + 31 * r:33 + 31 * r],
                                  ident[:, :])
                    T.give(pc, t)
                    yield
                    c = act.do([t, plf], act.e.activation, big[0:31, pl[g], :], b[0:31, :], ACT.Copy)
                    B.give(b, c)
                    ready.append(c)
                comp[tb] = (pl, ready)

            def attend(tb, r):
                L = (tb + 1) * P
                while tb not in comp or len(B.free) < 4 or not U.free:
                    yield
                z, zf = U.take()
                sx = Sb[z]
                sc = st[:, 96 + 16 * z:112 + 16 * z]
                sbk = [B.take() for i in range(4)]
                for w in range(2):
                    for g in range(2):
                        b, bf = sbk[2 * g + w]
                        t = pe.do([bf, qt, tk[KS], tk[KW]], pe.e.matmul, b[:, 0:L],
                                  big[64 * g:64 * g + 64, Q2 + r, tb * P:(tb + 1) * P],
                                  big[64 * g:64 * g + 64, (KS, KW)[w], 0:L], start=True, stop=True)
                        sbk[2 * g + w] = (b, t)
                qread = t
                yield
                for u in range(4):
                    b, t = sbk[u]
                    a = dve.do([t, biast, zf], dve.e.tensor_tensor_reduce, sx[:, u, 0:L], b[:, 0:L],
                               bias[:, 4 * (u // 2) + r, S - L:S], 1.0, -3e38, ALU.add, ALU.max, sc[:, u:u + 1])
                    B.give(b, a)
                a = dve.do([a], dve.e.tensor_scalar, sc[:, 4:8], sc[:, 0:4], -1.0, None, ALU.mult)
                yield
                for u in range(4):
                    x = act.do([a], act.e.activation, sx[:, u, 0:L], sx[:, u, 0:L], ACT.Exp, bias=sc[:, 4 + u:5 + u],
                               accum_out=sc[:, 8 + u:9 + u])
                yield
                a = dve.do([x], dve.e.reciprocal, sc[:, 12:16], sc[:, 8:12])
                gv = gsig[:, tb, :].rearrange("p (g r c) -> p g r c", g=2, r=4)[:, :, r, 1:3]
                fv = sc[:, 12:16].rearrange("p (g w) -> p g w", g=2)
                a = dve.do([a, gt_], dve.e.tensor_tensor, fv, fv, gv, ALU.mult)
                for u in range(4):
                    a = dve.do([a], dve.e.tensor_scalar, sx[:, u, 0:L], sx[:, u, 0:L], sc[:, 12 + u:13 + u], None,
                               ALU.mult)
                yield
                while len(B.free) < 3 or len(T.free) < 2:
                    yield
                ob, obf = B.take()
                pl, cready = comp[tb]
                for g in range(2):
                    t = pe.do([obf, cready, cmpt], pe.e.matmul, ob[64 * g:64 * g + 64, 0:P], vct[0:31, g, :],
                              big[0:31, pl[g], r * P:(r + 1) * P], start=True, stop=False, skip_group_check=True)
                crd[tb].append(t)
                for w in range(2):
                    while len(B.free) < 2 or len(T.free) < 2:
                        yield
                    got = []
                    for g in range(2):
                        b, bf = B.take()
                        for kb in range(tb + 1):
                            t = pe.do([bf, a], pe.e.transpose, b[:, kb * P:(kb + 1) * P],
                                      sx[:, 2 * g + w, kb * P:(kb + 1) * P], ident[:, :])
                        got.append((b, t, T.take()))
                    yield
                    pts = []
                    for g in range(2):
                        b, t, (p_, pf) = got[g]
                        if g == 0:
                            c = act.do([t, pf], act.e.activation, p_[:, 2:2 + L], b[:, 0:L], ACT.Copy)
                        else:
                            c = dve.do([t, pf], dve.e.tensor_copy, p_[:, 2:2 + L], b[:, 0:L])
                        B.give(b, c)
                        pts.append(c)
                    yield
                    for g in range(2):
                        p_ = got[g][2][0]
                        for kb in range(tb + 1):
                            t = pe.do([pts, vst, vwt], pe.e.matmul, ob[64 * g:64 * g + 64, 0:P],
                                      vtok[:, w, kb, 64 * g:64 * g + 64], p_[:, 2 + kb * P:2 + (kb + 1) * P],
                                      start=False, stop=w == 1 and kb == tb, skip_group_check=True)
                        T.give(p_, t)
                U.give(z, t)
                yield
                o = act.do([t, qread], act.e.activation, big[:, Q2 + r, tb * P:(tb + 1) * P], ob[:, 0:P], ACT.Copy)
                B.give(ob, o)
                ot[r].append(o)
                left[tb] -= 1
                if left[tb] == 0:
                    CP.give(pl, crd[tb])

            bg.add(lane([compressed(tb) for tb in range(4)]))
            units = [(tb, r) for tb in range(4) for r in range(4)]
            bg.add(lane([attend(*u) for u in units[0::2]]))
            bg.add(lane([attend(*u) for u in units[1::2]]))

            for at_, scale, pace in ((MQ, 128 ** -0.5, 1), (MK, 1.0, 1), (MV, 1.0, 1)):
                for half in range(2):
                    for i, (b, t) in enumerate(gemm([P] * 2, inp.rhs, pace=pace)):
                        scaled(at_ + 2 * half + i, b, t, scale)
            mvtt = []

            def value_tokens():
                for h in range(4):
                    yield
                    while not B.free:
                        yield
                    mvtt.append(to_tokens(MV + h, mvt[:, h, :, :], [tk[MV + h], hidt], act))

            bg.add(value_tokens())
            mt = {}

            def mlstm(h, lane_):
                while len(B.free) < 2 or len(T.free) < 3 or "gates" not in box:
                    yield
                nM, gct, emt = box["gates"]
                b, bf = B.take()
                num, numf = B.take()
                nb_, nbf = T.take()
                t = pe.do([bf, nM, d_sel], pe.e.matmul, b[:, :], rows[:, 0, h * P:(h + 1) * P], rows[:, 1, :],
                          start=True, stop=True)
                yield
                nbt = act.do([t, nbf], act.e.activation, nb_[:, 2:TW], b[:, :], ACT.Copy)
                s_, sf = b, nbt
                yield
                made = {}

                def decay(sbk):
                    n0 = sbk * P
                    e_, ef = T.take()
                    a = dve.do([nbt, gct, ef], dve.e.tensor_scalar, e_[:, 2 + n0:TW], nb_[:, 2 + n0:TW],
                               gcol[:, 4 * sbk + h:4 * sbk + h + 1], 0.0, ALU.add, ALU.min)
                    a = act.do([a], act.e.activation, e_[:, 2 + n0:TW], e_[:, 2 + n0:TW], ACT.Exp)
                    a = pool.do([a], pool.e.affine_select, out=e_[:, 2 + n0:2 + n0 + P],
                                in_=e_[:, 2 + n0:2 + n0 + P], compare_op=ALU.is_ge, fill=0.0, base=0,
                                pattern=[[1, P]], channel_multiplier=-1)
                    made[sbk] = (e_, a)

                while len(T.free) < 2:
                    yield
                decay(0)
                for sbk in range(4):
                    n0 = sbk * P
                    w = S - n0
                    ts_ = pe.do([sf, tk[MK + h], tk[MQ + h]], pe.e.matmul, s_[:, 0:w], big[:, MK + h, n0:n0 + P],
                                big[:, MQ + h, n0:S], start=True, stop=True)
                    qread = ts_
                    if sbk < 3:
                        while not T.free:
                            yield
                        decay(sbk + 1)
                    yield
                    e_, a = made[sbk]
                    a = dve.do([a, ts_], dve.e.tensor_tensor, e_[:, 2 + n0:TW], s_[:, 0:w], e_[:, 2 + n0:TW],
                               ALU.mult)
                    sf = a
                    yield
                    while len(mvtt) <= h:
                        yield
                    t = pe.do([numf, a, mvtt[h]], pe.e.matmul, num[:, n0:S], mvt[:, h, sbk, :], e_[:, 2 + n0:TW],
                              start=sbk == 0, stop=sbk == 3, skip_group_check=True)
                    if sbk == 0:
                        e0, et = e_, t
                    else:
                        eng = pool if sbk < 3 else dve
                        et = eng.do([a, et], eng.e.tensor_tensor, e0[:, 2 + n0:TW], e0[:, 2 + n0:TW],
                                    e_[:, 2 + n0:TW], ALU.add)
                        T.give(e_, t, et)
                T.give(nb_, a)
                yield
                den = s_
                for tb in range(4):
                    dt_ = pe.do([sf, et], pe.e.matmul, den[:, tb:tb + 1], e0[:, 2 + tb * P:2 + (tb + 1) * P],
                                ones[:, 0:1], start=tb == 0, stop=True, skip_group_check=True)
                T.give(e0, dt_)
                res = big[:, MQ + h, :]
                a = dve.do([t, qread], dve.e.tensor_copy, res, num[:, :])
                B.give(num, a)
                while len(T.free) < 1:
                    yield
                q_, qf = T.take()
                s2 = act.do([a, qf], act.e.activation, q_[:, 2:TW], res, ACT.Square)
                yield
                for tb in range(4):
                    t = pe.do([s2], pe.e.matmul, den[:, 8 + tb:9 + tb], q_[:, 2 + tb * P:2 + (tb + 1) * P],
                              ones[:, 0:1], start=False, stop=True, skip_group_check=True)
                T.give(q_, t)
                yield
                c0, c1 = (st[:, 64 + 8 * lane_ + 4 * k:68 + 8 * lane_ + 4 * k] for k in range(2))
                em = emc.rearrange("p (n h) -> p n h", h=4)[:, :, h]
                z = act.do([t, mt.get(("c", lane_))], act.e.activation, c0, den[:, 0:4], ACT.Abs)
                z = dve.do([z, emt], dve.e.tensor_tensor, c0, c0, em, ALU.max)
                z = dve.do([z], dve.e.reciprocal, c1, c0)
                z = dve.do([z], dve.e.tensor_tensor, c0, c1, c1, ALU.mult)
                z = dve.do([z], dve.e.tensor_tensor, c0, den[:, 8:12], c0, ALU.mult)
                sf = z
                z = dve.do([z], dve.e.tensor_scalar, c0, c0, 1.0 / 128, EPS, ALU.mult, ALU.add)
                yield
                z = rsqrt(c0, c0, st[:, 128:132], z)
                yield
                z = dve.do([z], dve.e.tensor_tensor, c1, c1, c0, ALU.mult)
                rbk, r = broadcast(diagonal(c1, [z]), (s_, sf))
                mt[("c", lane_)] = r
                yield
                a = dve.do([r, s2], dve.e.scalar_tensor_tensor, res, res, col("m_g", h), rbk[:, :], ALU.mult,
                           ALU.mult)
                B.give(rbk, a)
                while MO + h not in tk:
                    yield
                mt[h] = pool.do([a, tk[MO + h]], pool.e.tensor_tensor, res, res, big[:, MO + h, :], ALU.mult)

            bg.tasks.insert(0, lane([mlstm(0, 0), mlstm(2, 0)]))
            bg.add(lane([mlstm(1, 1), mlstm(3, 1)]))
            for half in range(2):
                for i, (b, t) in enumerate(gemm([P] * 2, inp.rhs, pace=3)):
                    i += MO + 2 * half
                    a = scaled(i, b, t, 1.0, extra=[biast])
                    tk[i] = act.do([a], act.e.activation, big[:, i, :], big[:, i, :], ACT.Sigmoid)
            state["rb_readers"] = [a]
            hr = (pe, pe.count)
            ht = {}

            def rhs(c):
                if c not in ht:
                    if c < 4:
                        bg.until(lambda: len(ot[c]) == 4)
                        src, tok = big[:, Q2 + c, :], ot[c]
                    else:
                        bg.until(lambda: c - 4 in mt)
                        src, tok = big[:, MQ + c - 4, :], mt[c - 4]
                    h = act.do([tok, hr], act.e.activation, Hh[:, c, :], src, ACT.Copy)
                    l = dve.do([h, tok, hr], dve.e.tensor_tensor, Hl[:, c, :], src, Hh[:, c, :].bitcast(F32),
                               ALU.subtract)
                    ht[c] = [h, l]
                return Hh[:, c, :], Hl[:, c, :], ht[c]

            added_gemm(rhs, KD, inp, pace=2, n=2)
            bg.finish()
            state["h_readers"] = (pe, pe.count)
            state["m_readers"] = [(pe, pe.count)]
            state["arena_readers"] = [(pe, pe.count), (dve, dve.count), (act, act.count), (pool, pool.count)]

        def ple_and_norm():
            af = state["arena_readers"]
            pr = sub("p_raw", [P, 2, S], 0)
            ph = sub("p_hi", [P, 2, S], 4096, F32R)
            pl = sub("p_lo", [P, 2, S], 8192, F32R)
            Y = sub("Y", [P, KD, S], 16384)
            lp = lot("s_p")
            d = act.dma([af], lp, act.e.dma_start, pr[:, :, :], A["pT"].rearrange("(c p) t -> p c t", p=P))
            inp = Input("ple_g")
            a = act.do([d, af], act.e.activation, ph[:, :, :], pr[:, :, :], ACT.Copy)
            b = dve.do([a, af], dve.e.tensor_tensor, pl[:, :, :], pr[:, :, :], ph[:, :, :].bitcast(F32),
                       ALU.subtract)
            pt = [a, b]

            def prhs(k):
                return ph[:, k, :], pl[:, k, :], pt

            nx, held, pair = [], [], []
            fin = None
            for g in range(2):
                res = gemm([P] * 4, inp.rhs, mid=inp.rms if g == 0 else None)
                rb = inp.rb
                us = []
                for i, (b_, t) in enumerate(res):
                    u, uf = T.take()
                    x = dve.do([t, rb, uf], dve.e.tensor_tensor, u[:, 2:TW], b_[:, :], RB[:, :], ALU.mult)
                    B.give(b_, x)
                    x2 = act.do([x], act.e.activation, u[:, 2:TW], u[:, 2:TW], ACT.Sigmoid)
                    us.append((u, x2))
                state["rb_readers"] = [x]
                res = gemm([P] * 4, prhs, 2)
                for i, (b_, t) in enumerate(res):
                    c = 4 * g + i
                    u, ut = us[i]
                    x = dve.do([t, ut], dve.e.tensor_tensor, u[:, 2:TW], b_[:, :], u[:, 2:TW], ALU.mult)
                    B.give(b_, x)
                    x = pool.do([x, inp.sq[c], inp.parts[c]], pool.e.tensor_tensor, X[:, c, :], X[:, c, :], u[:, 2:TW],
                                ALU.add)
                    T.give(u, x)
                    nx.append(x)
                    q, qf = T.take()
                    s_ = square_into(q[:, 2:TW], X[:, c, :], x, qf)
                    held.append((q, s_))
                for i in (0, 2):
                    (p_, pt_), (q_, qt_) = held[i:i + 2]
                    a = dve.do([pt_, qt_], dve.e.tensor_tensor, p_[:, 2:TW], p_[:, 2:TW], q_[:, 2:TW], ALU.add)
                    T.give(q_, a)
                    pair.append((p_, a))
                held = []
                if g == 0:
                    pair = merged(pair)
            fin = Stat()
            count_squares(fin, pair)
            fin.half()
            fbank, r = fin.spread()
            lo = [lot("s_out0"), lot("s_out1")]
            ends = []
            o3 = out.rearrange("(c p) t -> p c t", p=P)
            for c in range(KD):
                g = col("final_g", c)
                a = dve.do([r, nx[c], af], dve.e.scalar_tensor_tensor, Y[:, c, :], X[:, c, :], g, fbank[:, :], ALU.mult,
                           ALU.mult)
                ends.append(a)
                if c % 2 == 1:
                    l = Lot(ctx.enter_context(nc.semaphore(f"s_o{c}")))
                    dd = sp.dma([a], l, sp.e.dma_start, o3[:, c - 1:c + 1, :], Y[:, c - 1:c + 1, :])
                    state.setdefault("outs", []).append(dd)

        steps = [
            lambda: pool_mixer(),
            lambda: ffn(0, 11, "ffn_pre0", True, ACT.Gelu_apprx_tanh, FT, "ffn_post0"),
            lambda: window_mixer(),
            lambda: ffn(1, 11, "ffn_pre1", True, ACT.Gelu_apprx_tanh, FT, "ffn_post1"),
            lambda: second_mixer(),
            lambda: ffn(2, 8, "ln2", False, ACT.Silu, FT2, None),
            lambda: ple_and_norm(),
        ]
        n = len(steps) if stop is None else stop
        for s in steps[:n]:
            s()
        if stop is not None:
            o3 = out.rearrange("(c p) t -> p c t", p=P)
            l = lot("s_dbg")
            state["outs"] = [sp.dma([[state["x"](c) for c in range(KD)]], l, sp.e.dma_start, o3, X[:, :, :])]
        sp.wait(state["outs"])

        with nc.Block() as block:
            @block.sync
            def _(e):
                sp.run()

            @block.tensor
            def _(e):
                pe.run()

            @block.vector
            def _(e):
                dve.run()

            @block.scalar
            def _(e):
                act.run()

            @block.gpsimd
            def _(e):
                pool.run()


def constants():
    c = np.zeros((P, NCONST), np.float32)
    p = np.arange(P)[:, None]
    c[:, 0:P] = np.eye(P)
    o = CONST["dist"][0]
    j = np.arange(S)[None, :]
    d = j - 384 - p
    c[:, o:o + S] = np.where(d <= 0, d, NEG)
    o = CONST["swa"][0]
    j = np.arange(256)[None, :]
    rel = 128 + p - j
    c[:, o:o + 256] = np.where((rel >= 0) & (rel < 128), 0.0, NEG)
    o = CONST["cmp"][0]
    for tb in range(4):
        d = (16 * np.arange(31)[None, :] + 31) - (tb * P + p)
        c[:, o + 31 * tb:o + 31 * tb + 31] = np.where(d <= 0, d, NEG)
    o = CONST["sel"][0]
    for h in range(4):
        c[h, o + h * P:o + (h + 1) * P] = 1.0
    o = CONST["band"][0]
    q = np.arange(P)[None, :]
    for gi in range(4):
        w = 2 << gi
        inside = (q - p >= 0) & (q - p < w)
        b = o + 272 * gi
        c[:, b:b + P] = np.where(inside, 1.0 / np.minimum(q + 1, w), 0.0) - (q == p)
        c[:, b + P:b + 2 * P] = np.where(inside, 1.0 / w, 0.0) - (q == p)
        c[:, b + 2 * P:b + 272] = np.where(P + q[:, 0:16] - p < w, 1.0 / w, 0.0)
    return c


def tiles_of(v):
    return np.ascontiguousarray(v.reshape(-1, P).T)


def layout(i):
    f = np.float32
    i = {k: np.asarray(v) for k, v in i.items()}
    A = {}
    A["xT"] = np.ascontiguousarray(i["x"][0].T)
    A["pT"] = np.ascontiguousarray(i["p_2"][0, 0].T)
    A["pos"] = np.ascontiguousarray(np.broadcast_to(i["positions"][0][None, :], (P, S)))
    cols = np.zeros((P, NCOLS), f)

    def put(name, v):
        o, w = COLS[name]
        assert v.shape[1] == w, (name, v.shape)
        cols[:v.shape[0], o:o + w] = v

    for l in range(2):
        put(f"mix_pre{l}", tiles_of(i["mix_pre_g"][l]))
        put(f"mix_post{l}", tiles_of(i["mix_post_g"][l]))
        put(f"ffn_pre{l}", tiles_of(i["ffn_pre_g"][l]))
        put(f"ffn_post{l}", tiles_of(i["ffn_post_g"][l]))
        put(f"cw{l}", np.concatenate([tiles_of(i["ffn_conv_w"][l, k]) for k in range(3)], axis=1))
        put(f"cb{l}", tiles_of(i["ffn_conv_b"][l]))
    put("pool_scale", tiles_of(i["pool_scale"][0]))
    put("kv_g", tiles_of(i["kv_norm_g"]))
    put("ln1", tiles_of(i["ln1_g_2"][0]))
    put("ln2", tiles_of(i["ln2_g_2"][0]))
    put("ple_g", tiles_of(i["ple_norm_g_2"][0]))
    put("final_g", tiles_of(i["final_g_2"]))
    put("m_g", tiles_of(i["mlstm_norm_g_2"][0]))
    put("cw2", np.concatenate([tiles_of(i["conv_w_2"][0, k]) for k in range(3)], axis=1))
    put("cb2", tiles_of(i["conv_b_2"][0]))
    order = [4 * j + p for p in range(4) for j in range(4)]
    put("sinks", np.broadcast_to(i["sinks"][0][order][None, :], (P, 16)))
    put("gbias", np.ascontiguousarray(i["mlstm_gate_bias_2"][0].reshape(2, 4).T))
    fr = (1.0 / (10000.0 ** (np.arange(0, 64, 2, dtype=f) / 64))).astype(f)
    put("invf", np.tile(fr, 4)[:, None])
    put("rv", (np.arange(P) >= 31).astype(f)[:, None])
    A["cols"] = cols
    A["const"] = constants()
    A["pool_w"] = np.ascontiguousarray(i["pool_w"][0])
    d32 = np.arange(32)
    kcols = [np.concatenate([j * 64 + half * 32 + d32 for j in range(4)]) for half in range(2)]
    A["w_kv"] = np.ascontiguousarray(i["w_kv"][:, np.concatenate(kcols + [np.arange(256, 512)])])
    qcols = [np.concatenate([(4 * j + p) * 64 + half * 32 + d32 for j in range(4)])
             for p in range(4) for half in range(2)]
    A["w_q"] = np.ascontiguousarray(i["w_q"][0][:, np.concatenate(qcols)])
    orow = [np.concatenate([(4 * j + p) * 64 + np.arange(64) for j in (2 * jj, 2 * jj + 1)])
            for p in range(4) for jj in range(2)]
    A["w_o"] = np.ascontiguousarray(i["w_o"][0][np.concatenate(orow)])
    t = np.arange(P)
    for l in range(2):
        cc = [np.concatenate([(2 * g) * P + t, (2 * g + 1) * P + t, (FT + 2 * g) * P + t, (FT + 2 * g + 1) * P + t])
              for g in range(11)]
        A[f"w_in{l}"] = np.ascontiguousarray(i["ffn_w_in"][l][:, np.concatenate(cc)])
        A[f"w_out{l}"] = np.ascontiguousarray(i["ffn_w_out"][l])
    w = i["w_in_2"][0]
    sizes = [512] * 4 + [4, 4, 512] + [128] * 6 + [24]
    offs = np.concatenate([[0], np.cumsum(sizes)])
    sec = [w[:, offs[k]:offs[k + 1]] for k in range(len(sizes))]
    mq, mk, mv, mo, mi, mf, aq, akc, avc, aks, avs, akw, avw, ag = sec
    q2 = [np.concatenate([aq[:, r * 64:(r + 1) * 64], aq[:, (4 + r) * 64:(5 + r) * 64]], axis=1) for r in range(4)]
    z = np.zeros((D, 28), f)
    A["w_in_2"] = np.ascontiguousarray(np.concatenate(
        [akc, avc, aks, avs, akw, avw] + q2 + [mi, z, mf, z, ag, mq, mk, mv, mo], axis=1))
    wo = i["w_out_2"][0]
    rows = [np.concatenate([512 + r * 64 + np.arange(64), 512 + (4 + r) * 64 + np.arange(64)])
            for r in range(4)] + [np.arange(512)]
    A["w_out_2"] = np.ascontiguousarray(wo[np.concatenate(rows)])
    cc = [np.concatenate([(2 * g) * P + t, (2 * g + 1) * P + t, (FT2 + 2 * g) * P + t, (FT2 + 2 * g + 1) * P + t])
          for g in range(8)]
    A["w_up_2"] = np.ascontiguousarray(i["w_up_2"][0][:, np.concatenate(cc)])
    A["w_down_2"] = np.ascontiguousarray(i["w_down_2"][0])
    A["w_pg"] = np.ascontiguousarray(i["w_ple_gate_2"][0])
    A["w_pp"] = np.ascontiguousarray(i["w_ple_proj_2"][0])
    A["cmp_w1"] = np.ascontiguousarray(np.stack([i["cmp_k_w1_2"][0], i["cmp_v_w1_2"][0]]))
    A["cmp_w2"] = np.ascontiguousarray(np.stack([i["cmp_k_w2_2"][0], i["cmp_v_w2_2"][0]], axis=1))
    pes = []
    for n in ("cmp_pos_k_2", "cmp_pos_v_2"):
        v = i[n][0].reshape(16, 2, 64).transpose(2, 1, 0)
        pes.append(np.concatenate([v, v], axis=0))
    A["cmp_pe"] = np.ascontiguousarray(np.stack(pes, axis=1))
    return A


def kernel(**inputs):
    import concourse.bacc as bacc
    from concourse.bass_utils import run_bass_kernel_spmd

    arrays = layout(inputs)
    nc = bacc.Bacc("TRN2", target_bir_lowering=False, num_devices=1)
    aps = {}
    feed = {}
    for name, a in arrays.items():
        feed[f"in_{name}"] = a
        aps[name] = nc.dram_tensor(f"in_{name}", a.shape, mybir.dt.from_np(a.dtype), kind="ExternalInput").ap()
    out = nc.dram_tensor("out_0", (D, S), F32, kind="ExternalOutput").ap()
    build(nc, aps, out)
    r = run_bass_kernel_spmd(nc, [feed], core_ids=[0])
    return np.ascontiguousarray(r.results[0]["out_0"].T)[None]
```
